# Optimizing a Trainium2 kernel written in Bass

```python
import jax, jax.numpy as jnp
from jax import lax
import numpy as np
import math
import jax
import jax.numpy as jnp

D_MODEL = 1024
BATCH = 1
SEQ = 256
DEPTH = 2

HEAD_DIM = 64
ROPE_THETA = 500000.0
ROT_DIM = HEAD_DIM // 4
GRID_W = 64
EPS = 1e-6
NEG_INF = -1e30
QBLK = 128

A_HEADS = 3 * D_MODEL // (4 * HEAD_DIM)
A_WIDTH = A_HEADS * HEAD_DIM
A_PATTERNS = ((128, 1), (512, 4), (2048, 16))
B_GROUP_DIM = 64
B_GROUPS = D_MODEL // (4 * B_GROUP_DIM)
B_WIDTH = B_GROUPS * B_GROUP_DIM
B_CHUNK = 128
EVEN_IN = 3 * A_WIDTH + 2 * B_WIDTH
C_HEADS = D_MODEL // (2 * HEAD_DIM)
C_Q_RANK = D_MODEL // 4
C_KV_RANK = D_MODEL // 8
C_NOPE = HEAD_DIM
C_ROPE = HEAD_DIM // 2
C_V = HEAD_DIM
D_HEADS = D_MODEL // (2 * HEAD_DIM)
D_KV_HEADS = 2
D_GROUP = D_HEADS // D_KV_HEADS
D_THETA = 10000.0
ODD_IN = C_Q_RANK + C_KV_RANK + C_ROPE + (D_HEADS + 2 * D_KV_HEADS) * HEAD_DIM
N_EXPERTS = 16
EC_FACTOR = 2
EXPERT_FF = 512


def rmsnorm(x, g):
    xf = x.astype(jnp.float32)
    y = xf * lax.rsqrt(jnp.mean(xf * xf, axis=-1, keepdims=True) + EPS)
    return (y * g.astype(jnp.float32)).astype(x.dtype)

def rope(x, pos, theta):
    r = x.shape[-1]
    half = r // 2
    inv = jnp.power(jnp.float32(theta), -jnp.arange(half, dtype=jnp.float32) * (2.0 / r))
    ang = pos.astype(jnp.float32)[:, None] * inv[None, :]
    shape = (pos.shape[0],) + (1,) * (x.ndim - 3) + (half,)
    cos = jnp.cos(ang).reshape(shape)
    sin = jnp.sin(ang).reshape(shape)
    xf = x.astype(jnp.float32)
    x1, x2 = xf[..., :half], xf[..., half:]
    return jnp.concatenate([x1 * cos - x2 * sin, x1 * sin + x2 * cos], axis=-1).astype(x.dtype)

def partial_rope(x, pos):
    return jnp.concatenate([rope(x[..., :ROT_DIM], pos, ROPE_THETA), x[..., ROT_DIM:]], axis=-1)

def axial_rope(x, row, col):
    half = x.shape[-1] // 2
    return jnp.concatenate([rope(x[..., :half], row, D_THETA), rope(x[..., half:], col, D_THETA)], axis=-1)

def dilated_band_attention(q, k, v, window, dilation):
    b, s, h, dh = q.shape
    r = window // (2 * dilation)
    blk = r
    L = s // dilation
    nb = -(-L // blk)
    lp = nb * blk

    def residue(t):
        return t.reshape(b, L, dilation, h, dh).transpose(0, 2, 1, 3, 4)

    qr = jnp.pad(residue(q), ((0, 0), (0, 0), (0, lp - L), (0, 0), (0, 0)))
    qr = qr.reshape(b, dilation, nb, blk, h, dh)

    def band(t):
        tp = jnp.pad(residue(t), ((0, 0), (0, 0), (blk, lp - L + blk), (0, 0), (0, 0)))
        tp = tp.reshape(b, dilation, nb + 2, blk, h, dh)
        return jnp.concatenate([tp[:, :, 0:nb], tp[:, :, 1:nb + 1], tp[:, :, 2:nb + 2]], axis=3)

    kb, vb = band(k), band(v)
    scores = jnp.einsum('bdnqhc,bdnkhc->bdnhqk', qr, kb).astype(jnp.float32) * (dh ** -0.5)
    qi = jnp.arange(blk)[:, None]
    ki = jnp.arange(3 * blk)[None, :]
    in_band = jnp.abs(ki - blk - qi) <= r
    kpos = jnp.arange(nb)[:, None] * blk - blk + jnp.arange(3 * blk)[None, :]
    valid = in_band[None] & ((kpos >= 0) & (kpos < L))[:, None, :]
    scores = jnp.where(valid[None, None, :, None], scores, NEG_INF)
    lse = jax.nn.logsumexp(scores, axis=-1)
    p = jnp.exp(scores - lse[..., None])
    out = jnp.einsum('bdnhqk,bdnkhc->bdnqhc', p.astype(v.dtype), vb)
    out = out.reshape(b, dilation, lp, h, dh)[:, :, :L].transpose(0, 2, 1, 3, 4).reshape(b, s, h, dh)
    lse = lse.transpose(0, 1, 2, 4, 3).reshape(b, dilation, lp, h)[:, :, :L]
    lse = lse.transpose(0, 2, 1, 3).reshape(b, s, h)
    return out, lse

def dilated_mixture(q, k, v):
    results = [dilated_band_attention(q, k, v, w, d) for (w, d) in A_PATTERNS]
    outs = jnp.stack([o for (o, _) in results], axis=0)
    lses = jnp.stack([l for (_, l) in results], axis=0)
    wts = jax.nn.softmax(lses, axis=0)
    return jnp.einsum('pbsh,pbshc->bshc', wts.astype(q.dtype), outs)

def spatial_gating(z, v_norm, w_s, b_s):
    b, s, _ = z.shape
    z = jax.nn.gelu(z)
    u, vv = jnp.split(z, 2, axis=-1)
    u = u.reshape(b, s, B_GROUPS, B_GROUP_DIM)
    vv = rmsnorm(vv.reshape(b, s, B_GROUPS, B_GROUP_DIM), v_norm)
    vv = vv.reshape(b, s // B_CHUNK, B_CHUNK, B_GROUPS, B_GROUP_DIM)
    mixed = jnp.einsum('gpq,bnqgc->bnpgc', w_s, vv) + b_s.T[None, None, :, :, None]
    return (u * mixed.reshape(b, s, B_GROUPS, B_GROUP_DIM)).reshape(b, s, B_WIDTH)

def block_attention(q, k, v):
    b, s, kvh, g, dk = q.shape
    nq = s // QBLK
    scale = dk ** -0.5
    qb = q.reshape(b, nq, QBLK, kvh, g, dk).transpose(1, 0, 2, 3, 4, 5)

    def one(qblk):
        sc = jnp.einsum('bqkgc,bskc->bkgqs', qblk, k).astype(jnp.float32) * scale
        p = jax.nn.softmax(sc, axis=-1)
        return jnp.einsum('bkgqs,bskc->bqkgc', p.astype(v.dtype), v)

    out = lax.map(one, qb)
    return out.transpose(1, 0, 2, 3, 4, 5).reshape(b, s, kvh * g * v.shape[-1])

def mixer_even(h, pos, w_in, gmlp_norm, w_s, b_s, w_out):
    b, s, _ = h.shape
    proj = h @ w_in
    q, k, v, z = jnp.split(proj, [A_WIDTH, 2 * A_WIDTH, 3 * A_WIDTH], axis=-1)
    q = partial_rope(q.reshape(b, s, A_HEADS, HEAD_DIM), pos)
    k = partial_rope(k.reshape(b, s, A_HEADS, HEAD_DIM), pos)
    v = v.reshape(b, s, A_HEADS, HEAD_DIM)
    a_out = dilated_mixture(q, k, v).reshape(b, s, A_WIDTH)
    g_out = spatial_gating(z, gmlp_norm, w_s, b_s)
    return jnp.concatenate([a_out, g_out], axis=-1) @ w_out

def mixer_odd(h, pos, row, col, w_in, cq_norm, w_cq_up, ckv_norm, w_ckv_up, dq_norm, dk_norm, w_out):
    b, s, _ = h.shape
    proj = h @ w_in
    o1 = C_Q_RANK
    o2 = o1 + C_KV_RANK
    o3 = o2 + C_ROPE
    o4 = o3 + D_HEADS * HEAD_DIM
    o5 = o4 + D_KV_HEADS * HEAD_DIM
    cq, ckv, ck_rope, dq, dk, dv = jnp.split(proj, [o1, o2, o3, o4, o5], axis=-1)
    cq = (rmsnorm(cq, cq_norm) @ w_cq_up).reshape(b, s, C_HEADS, C_NOPE + C_ROPE)
    q_nope, q_rope = cq[..., :C_NOPE], rope(cq[..., C_NOPE:], pos, ROPE_THETA)
    kv = (rmsnorm(ckv, ckv_norm) @ w_ckv_up).reshape(b, s, C_HEADS, C_NOPE + C_V)
    k_nope, v_c = kv[..., :C_NOPE], kv[..., C_NOPE:]
    k_rope = rope(ck_rope, pos, ROPE_THETA)
    q_c = jnp.concatenate([q_nope, q_rope], axis=-1)[:, :, :, None]
    k_c = jnp.concatenate([k_nope, jnp.broadcast_to(k_rope[:, :, None], (b, s, C_HEADS, C_ROPE))], axis=-1)
    c_out = block_attention(q_c, k_c, v_c)
    dq = axial_rope(rmsnorm(dq.reshape(b, s, D_KV_HEADS, D_GROUP, HEAD_DIM), dq_norm), row, col)
    dk = axial_rope(rmsnorm(dk.reshape(b, s, D_KV_HEADS, HEAD_DIM), dk_norm), row, col)
    dv = dv.reshape(b, s, D_KV_HEADS, HEAD_DIM)
    d_out = block_attention(dq, dk, dv)
    return jnp.concatenate([c_out, d_out], axis=-1) @ w_out

def ec_moe(h, w_router, w_gate, w_up, w_down):
    b, s, d = h.shape
    cap = EC_FACTOR * s // N_EXPERTS
    logits = jnp.einsum('bsd,de->bse', h, w_router).astype(jnp.float32)
    aff = jax.nn.softmax(logits, axis=-1)
    gates, idx = lax.top_k(aff.transpose(0, 2, 1), cap)
    xs = jax.vmap(lambda hb, ib: hb[ib])(h, idx)
    g = jnp.einsum('becd,edf->becf', xs, w_gate)
    u = jnp.einsum('becd,edf->becf', xs, w_up)
    y = jnp.einsum('becf,efd->becd', jax.nn.silu(g) * u, w_down)
    y = y * gates[..., None].astype(y.dtype)
    return jax.vmap(lambda ib, yb: jnp.zeros((s, d), yb.dtype).at[ib.reshape(-1)].add(yb.reshape(-1, d)))(idx, y)

def first_inputs(seed: int = 0) -> dict:
    key = jax.random.key(seed)
    ks = jax.random.split(key, 21)
    n_even = (DEPTH + 1) // 2
    n_odd = DEPTH // 2

    def normal(k, shape, scale):
        return jax.random.normal(k, shape, jnp.float32) * scale

    def gain(k, shape):
        return 1.0 + 0.02 * jax.random.normal(k, shape, jnp.float32)

    return {
        "x": normal(ks[0], (BATCH, SEQ, D_MODEL), 1.0),
        "norm_mix": gain(ks[1], (DEPTH, D_MODEL)),
        "norm_ffn": gain(ks[2], (DEPTH, D_MODEL)),
        "even_w_in": normal(ks[3], (n_even, D_MODEL, EVEN_IN), D_MODEL ** -0.5),
        "even_gmlp_norm": gain(ks[4], (n_even, B_GROUPS, B_GROUP_DIM)),
        "even_w_spatial": normal(ks[5], (n_even, B_GROUPS, B_CHUNK, B_CHUNK), B_CHUNK ** -0.5),
        "even_b_spatial": normal(ks[6], (n_even, B_GROUPS, B_CHUNK), 0.02),
        "even_w_out": normal(ks[7], (n_even, A_WIDTH + B_WIDTH, D_MODEL), (A_WIDTH + B_WIDTH) ** -0.5),
        "odd_w_in": normal(ks[8], (n_odd, D_MODEL, ODD_IN), D_MODEL ** -0.5),
        "odd_cq_norm": gain(ks[9], (n_odd, C_Q_RANK)),
        "odd_w_cq_up": normal(ks[10], (n_odd, C_Q_RANK, C_HEADS * (C_NOPE + C_ROPE)), C_Q_RANK ** -0.5),
        "odd_ckv_norm": gain(ks[11], (n_odd, C_KV_RANK)),
        "odd_w_ckv_up": normal(ks[12], (n_odd, C_KV_RANK, C_HEADS * (C_NOPE + C_V)), C_KV_RANK ** -0.5),
        "odd_dq_norm": gain(ks[13], (n_odd, HEAD_DIM)),
        "odd_dk_norm": gain(ks[14], (n_odd, HEAD_DIM)),
        "odd_w_out": normal(ks[15], (n_odd, C_HEADS * C_V + D_HEADS * HEAD_DIM, D_MODEL), (C_HEADS * C_V + D_HEADS * HEAD_DIM) ** -0.5),
        "moe_w_router": normal(ks[16], (DEPTH, D_MODEL, N_EXPERTS), D_MODEL ** -0.5),
        "moe_w_gate": normal(ks[17], (DEPTH, N_EXPERTS, D_MODEL, EXPERT_FF), D_MODEL ** -0.5),
        "moe_w_up": normal(ks[18], (DEPTH, N_EXPERTS, D_MODEL, EXPERT_FF), D_MODEL ** -0.5),
        "moe_w_down": normal(ks[19], (DEPTH, N_EXPERTS, EXPERT_FF, D_MODEL), EXPERT_FF ** -0.5),
        "final_norm": gain(ks[20], (D_MODEL,)),
    }

def first_block(x, norm_mix, norm_ffn, even_w_in, even_gmlp_norm, even_w_spatial, even_b_spatial, even_w_out,
              odd_w_in, odd_cq_norm, odd_w_cq_up, odd_ckv_norm, odd_w_ckv_up, odd_dq_norm, odd_dk_norm, odd_w_out,
              moe_w_router, moe_w_gate, moe_w_up, moe_w_down, final_norm):
    b, s, _ = x.shape
    pos = jnp.arange(s, dtype=jnp.int32)
    rows = s // GRID_W
    row = jnp.repeat(jnp.arange(rows, dtype=jnp.int32), GRID_W)
    col = jnp.tile(jnp.arange(GRID_W, dtype=jnp.int32), rows)
    for i in range(DEPTH):
        j = i // 2
        h = rmsnorm(x, norm_mix[i])
        if i % 2 == 0:
            mix = mixer_even(h, pos, even_w_in[j], even_gmlp_norm[j], even_w_spatial[j], even_b_spatial[j], even_w_out[j])
        else:
            mix = mixer_odd(h, pos, row, col, odd_w_in[j], odd_cq_norm[j], odd_w_cq_up[j], odd_ckv_norm[j],
                            odd_w_ckv_up[j], odd_dq_norm[j], odd_dk_norm[j], odd_w_out[j])
        x = x + mix
        x = x + ec_moe(rmsnorm(x, norm_ffn[i]), moe_w_router[i], moe_w_gate[i], moe_w_up[i], moe_w_down[i])
    return rmsnorm(x, final_norm)


N_Q_HEADS = 8
N_KV_HEADS = 2
GROUP = N_Q_HEADS // N_KV_HEADS
WINDOW = 128
ATTN_BLOCK = WINDOW
Q_WIDTH = N_Q_HEADS * HEAD_DIM
KV_WIDTH = N_KV_HEADS * HEAD_DIM
NUM_BUCKETS = 32
MAX_DISTANCE = 128
CONV_CHANNELS = D_MODEL // 2
CONV_WIDTH = 31
EVEN_IN_2 = Q_WIDTH + 2 * KV_WIDTH + 2 * CONV_CHANNELS
EVEN_CAT = Q_WIDTH + CONV_CHANNELS
LRU_WIDTH = D_MODEL
LRU_HEADS = 8
LRU_BLOCK = LRU_WIDTH // LRU_HEADS
LRU_CONV_WIDTH = 4
RG_LRU_C = 8.0
D_FF = 2816
RMS_EPS = 1e-6
LN_EPS = 1e-5
NEG_INF_2 = -1e30
N_EVEN = (DEPTH + 1) // 2
N_ODD = DEPTH // 2


def _rmsnorm(x, g):
    xf = x.astype(jnp.float32)
    y = xf * lax.rsqrt(jnp.mean(xf * xf, axis=-1, keepdims=True) + RMS_EPS)
    return (y * g.astype(jnp.float32)).astype(x.dtype)

def _layernorm(x, g, b):
    xf = x.astype(jnp.float32)
    mu = jnp.mean(xf, axis=-1, keepdims=True)
    var = jnp.mean(jnp.square(xf - mu), axis=-1, keepdims=True)
    y = (xf - mu) * lax.rsqrt(var + LN_EPS)
    return (y * g.astype(jnp.float32) + b.astype(jnp.float32)).astype(x.dtype)

def _swiglu(x, wg, wu, wd):
    return (jax.nn.silu(x @ wg) * (x @ wu)) @ wd

def _causal_depthwise_conv(x, w, b):
    k_width, chans = w.shape
    y = lax.conv_general_dilated(
        x, w[:, None, :].astype(x.dtype), window_strides=(1,),
        padding=[(k_width - 1, 0)], dimension_numbers=("NWC", "WIO", "NWC"),
        feature_group_count=chans)
    return y + b.astype(x.dtype)

def _t5_bucket(dist):
    n = jnp.maximum(dist, 0)
    max_exact = NUM_BUCKETS // 2
    nf = jnp.maximum(n, max_exact).astype(jnp.float32)
    large = max_exact + (jnp.log(nf / max_exact) / math.log(MAX_DISTANCE / max_exact)
                         * (NUM_BUCKETS - max_exact)).astype(jnp.int32)
    large = jnp.minimum(large, NUM_BUCKETS - 1)
    return jnp.where(n < max_exact, n, large)

def _swa_sink_attention(q, k, v, sinks, rel_bias):
    bsz, seq = q.shape[:2]
    nb = seq // ATTN_BLOCK
    qb = q.reshape(bsz, nb, ATTN_BLOCK, N_KV_HEADS, GROUP, HEAD_DIM)
    kb = k.reshape(bsz, nb, ATTN_BLOCK, N_KV_HEADS, HEAD_DIM)
    vb = v.reshape(bsz, nb, ATTN_BLOCK, N_KV_HEADS, HEAD_DIM)
    kk = jnp.concatenate([jnp.concatenate([jnp.zeros_like(kb[:, :1]), kb[:, :-1]], axis=1), kb], axis=2)
    vv = jnp.concatenate([jnp.concatenate([jnp.zeros_like(vb[:, :1]), vb[:, :-1]], axis=1), vb], axis=2)
    scores = jnp.einsum("bnqhgd,bnshd->bnhgqs", qb, kk,
                        preferred_element_type=jnp.float32) * (1.0 / math.sqrt(HEAD_DIM))
    qi = jnp.arange(ATTN_BLOCK)[:, None]
    sj = jnp.arange(2 * ATTN_BLOCK)[None, :]
    dist = qi + ATTN_BLOCK - sj
    bias = rel_bias.astype(jnp.float32)[_t5_bucket(dist)]
    bias = jnp.transpose(bias, (2, 0, 1)).reshape(N_KV_HEADS, GROUP, ATTN_BLOCK, 2 * ATTN_BLOCK)
    in_window = (dist >= 0) & (dist < WINDOW)
    key_pos = jnp.arange(nb)[:, None, None] * ATTN_BLOCK + sj[None] - ATTN_BLOCK
    mask = in_window[None] & (key_pos >= 0)
    scores = jnp.where(mask[None, :, None, None], scores + bias[None, None], NEG_INF_2)
    sink = sinks.astype(jnp.float32).reshape(N_KV_HEADS, GROUP)[None, None, :, :, None, None]
    sink = jnp.broadcast_to(sink, scores.shape[:-1] + (1,))
    probs = jax.nn.softmax(jnp.concatenate([scores, sink], axis=-1), axis=-1)[..., :-1]
    out = jnp.einsum("bnhgqs,bnshd->bnqhgd", probs.astype(v.dtype), vv)
    return out.reshape(bsz, seq, Q_WIDTH)

def _attn_conv_mixer(h, w_in, sinks, conv_w, conv_b, ln_g, ln_b, w_out, rel_bias):
    bsz, seq, _ = h.shape
    u = h @ w_in
    o1 = Q_WIDTH
    o2 = o1 + KV_WIDTH
    o3 = o2 + KV_WIDTH
    o4 = o3 + CONV_CHANNELS
    q = u[..., :o1].reshape(bsz, seq, N_Q_HEADS, HEAD_DIM)
    k = u[..., o1:o2].reshape(bsz, seq, N_KV_HEADS, HEAD_DIM)
    v = u[..., o2:o3].reshape(bsz, seq, N_KV_HEADS, HEAD_DIM)
    attn = _swa_sink_attention(q, k, v, sinks, rel_bias)
    glu = u[..., o3:o4] * jax.nn.sigmoid(u[..., o4:])
    c = jax.nn.silu(_layernorm(_causal_depthwise_conv(glu, conv_w, conv_b), ln_g, ln_b))
    return jnp.concatenate([attn, c], axis=-1) @ w_out

def _rg_lru(x, ga_w, ga_b, gx_w, gx_b, lam):
    bsz, seq, width = x.shape
    xh = x.reshape(bsz, seq, LRU_HEADS, LRU_BLOCK)
    r = jax.nn.sigmoid(jnp.einsum("bshi,hij->bshj", xh, ga_w).reshape(bsz, seq, width) + ga_b)
    i = jax.nn.sigmoid(jnp.einsum("bshi,hij->bshj", xh, gx_w).reshape(bsz, seq, width) + gx_b)
    log_a = RG_LRU_C * r.astype(jnp.float32) * jax.nn.log_sigmoid(lam.astype(jnp.float32))
    a = jnp.exp(log_a)
    bx = jnp.sqrt(-jnp.expm1(2.0 * log_a)) * (i * x).astype(jnp.float32)

    def combine(left, right):
        a1, b1 = left
        a2, b2 = right
        return a1 * a2, a2 * b1 + b2

    _, hs = lax.associative_scan(combine, (a, bx), axis=1)
    return hs.astype(x.dtype)

def _recurrent_mixer(h, w_in, conv_w, conv_b, ga_w, ga_b, gx_w, gx_b, lam, w_out):
    u = h @ w_in
    gate = jax.nn.gelu(u[..., :LRU_WIDTH])
    rec = _causal_depthwise_conv(u[..., LRU_WIDTH:], conv_w, conv_b)
    rec = _rg_lru(rec, ga_w, ga_b, gx_w, gx_b, lam)
    return (gate * rec) @ w_out

def second_inputs(seed: int = 0) -> dict:
    key = jax.random.key(seed)
    ks = iter(jax.random.split(key, 40))

    def nrm(shape, scale):
        return jax.random.normal(next(ks), shape, jnp.float32) * scale

    def gain(shape):
        return 1.0 + nrm(shape, 0.02)

    x = nrm((BATCH, SEQ, D_MODEL), 1.0)
    u = jax.random.uniform(next(ks), (N_ODD, LRU_WIDTH), jnp.float32, 0.9, 0.999)
    a0 = u ** (1.0 / RG_LRU_C)
    lru_lambda = jnp.log(a0) - jnp.log1p(-a0)
    return {
        "x": x,
        "norm_ffn1": gain((DEPTH, D_MODEL)),
        "ffn1_wg": nrm((DEPTH, D_MODEL, D_FF), D_MODEL ** -0.5),
        "ffn1_wu": nrm((DEPTH, D_MODEL, D_FF), D_MODEL ** -0.5),
        "ffn1_wd": nrm((DEPTH, D_FF, D_MODEL), D_FF ** -0.5),
        "norm_mix": gain((DEPTH, D_MODEL)),
        "norm_ffn2": gain((DEPTH, D_MODEL)),
        "ffn2_wg": nrm((DEPTH, D_MODEL, D_FF), D_MODEL ** -0.5),
        "ffn2_wu": nrm((DEPTH, D_MODEL, D_FF), D_MODEL ** -0.5),
        "ffn2_wd": nrm((DEPTH, D_FF, D_MODEL), D_FF ** -0.5),
        "rel_bias": nrm((NUM_BUCKETS, N_Q_HEADS), 0.3),
        "even_w_in": nrm((N_EVEN, D_MODEL, EVEN_IN_2), D_MODEL ** -0.5),
        "attn_sinks": nrm((N_EVEN, N_Q_HEADS), 1.0),
        "conv_b_w": nrm((N_EVEN, CONV_WIDTH, CONV_CHANNELS), CONV_WIDTH ** -0.5),
        "conv_b_b": nrm((N_EVEN, CONV_CHANNELS), 0.02),
        "conv_ln_g": gain((N_EVEN, CONV_CHANNELS)),
        "conv_ln_b": nrm((N_EVEN, CONV_CHANNELS), 0.02),
        "even_w_out": nrm((N_EVEN, EVEN_CAT, D_MODEL), EVEN_CAT ** -0.5),
        "odd_w_in": nrm((N_ODD, D_MODEL, 2 * LRU_WIDTH), D_MODEL ** -0.5),
        "lru_conv_w": nrm((N_ODD, LRU_CONV_WIDTH, LRU_WIDTH), LRU_CONV_WIDTH ** -0.5),
        "lru_conv_b": nrm((N_ODD, LRU_WIDTH), 0.02),
        "gate_a_w": nrm((N_ODD, LRU_HEADS, LRU_BLOCK, LRU_BLOCK), LRU_BLOCK ** -0.5),
        "gate_a_b": nrm((N_ODD, LRU_WIDTH), 0.02),
        "gate_x_w": nrm((N_ODD, LRU_HEADS, LRU_BLOCK, LRU_BLOCK), LRU_BLOCK ** -0.5),
        "gate_x_b": nrm((N_ODD, LRU_WIDTH), 0.02),
        "lru_lambda": lru_lambda,
        "odd_w_out": nrm((N_ODD, LRU_WIDTH, D_MODEL), LRU_WIDTH ** -0.5),
        "norm_final": gain((D_MODEL,)),
    }

def second_block(x, norm_ffn1, ffn1_wg, ffn1_wu, ffn1_wd, norm_mix, norm_ffn2, ffn2_wg, ffn2_wu, ffn2_wd,
              rel_bias, even_w_in, attn_sinks, conv_b_w, conv_b_b, conv_ln_g, conv_ln_b, even_w_out,
              odd_w_in, lru_conv_w, lru_conv_b, gate_a_w, gate_a_b, gate_x_w, gate_x_b, lru_lambda,
              odd_w_out, norm_final):
    h = x
    for layer in range(DEPTH):
        h = h + 0.5 * _swiglu(_rmsnorm(h, norm_ffn1[layer]), ffn1_wg[layer], ffn1_wu[layer], ffn1_wd[layer])
        hn = _rmsnorm(h, norm_mix[layer])
        if layer % 2 == 0:
            e = layer // 2
            h = h + _attn_conv_mixer(hn, even_w_in[e], attn_sinks[e], conv_b_w[e], conv_b_b[e],
                                     conv_ln_g[e], conv_ln_b[e], even_w_out[e], rel_bias)
        else:
            o = layer // 2
            h = h + _recurrent_mixer(hn, odd_w_in[o], lru_conv_w[o], lru_conv_b[o], gate_a_w[o],
                                     gate_a_b[o], gate_x_w[o], gate_x_b[o], lru_lambda[o], odd_w_out[o])
        h = h + 0.5 * _swiglu(_rmsnorm(h, norm_ffn2[layer]), ffn2_wg[layer], ffn2_wu[layer], ffn2_wd[layer])
    return _rmsnorm(h, norm_final)


def setup_inputs(seed=0):
    out = dict(first_inputs(seed))
    for name, value in second_inputs(seed + 1).items():
        if name != "x":
            out[name + "_2"] = value
    return out


def reference(
    x, norm_mix, norm_ffn, even_w_in, even_gmlp_norm, even_w_spatial, even_b_spatial,
    even_w_out, odd_w_in, odd_cq_norm, odd_w_cq_up, odd_ckv_norm, odd_w_ckv_up, odd_dq_norm,
    odd_dk_norm, odd_w_out, moe_w_router, moe_w_gate, moe_w_up, moe_w_down, final_norm,
    norm_ffn1_2, ffn1_wg_2, ffn1_wu_2, ffn1_wd_2, norm_mix_2, norm_ffn2_2, ffn2_wg_2, ffn2_wu_2,
    ffn2_wd_2, rel_bias_2, even_w_in_2, attn_sinks_2, conv_b_w_2, conv_b_b_2, conv_ln_g_2,
    conv_ln_b_2, even_w_out_2, odd_w_in_2, lru_conv_w_2, lru_conv_b_2, gate_a_w_2, gate_a_b_2,
    gate_x_w_2, gate_x_b_2, lru_lambda_2, odd_w_out_2, norm_final_2,
):
    x = first_block(
        x, norm_mix, norm_ffn, even_w_in, even_gmlp_norm, even_w_spatial, even_b_spatial,
        even_w_out, odd_w_in, odd_cq_norm, odd_w_cq_up, odd_ckv_norm, odd_w_ckv_up, odd_dq_norm,
        odd_dk_norm, odd_w_out, moe_w_router, moe_w_gate, moe_w_up, moe_w_down, final_norm,
    )
    return second_block(
        x, norm_ffn1_2, ffn1_wg_2, ffn1_wu_2, ffn1_wd_2, norm_mix_2, norm_ffn2_2, ffn2_wg_2,
        ffn2_wu_2, ffn2_wd_2, rel_bias_2, even_w_in_2, attn_sinks_2, conv_b_w_2, conv_b_b_2,
        conv_ln_g_2, conv_ln_b_2, even_w_out_2, odd_w_in_2, lru_conv_w_2, lru_conv_b_2,
        gate_a_w_2, gate_a_b_2, gate_x_w_2, gate_x_b_2, lru_lambda_2, odd_w_out_2, norm_final_2,
    )


_drawn_inputs = setup_inputs


def setup_inputs(seed=0):
    import zlib

    import numpy as np

    out = dict(_drawn_inputs(seed))
    spreads = {}
    factors = {'even_gmlp_norm': 2.966,
     'even_b_spatial': 2.881,
     'odd_cq_norm': 8.0,
     'odd_ckv_norm': 8.0,
     'odd_dq_norm': 8.0,
     'odd_dk_norm': 8.0,
     'norm_ffn1_2': 4.677,
     'norm_mix_2': 3.495,
     'norm_ffn2_2': 5.541,
     'attn_sinks_2': 18.126,
     'conv_ln_g_2': 22.343,
     'conv_ln_b_2': 23.126,
     'gate_a_b_2': 51.319,
     'gate_x_b_2': 33.801,
     'norm_final_2': 22.141,
     'conv_b_b_2': 8.0,
     'lru_conv_b_2': 4.944,
     'rel_bias_2': 3.226}
    for name, (base, spread) in spreads.items():
        noise = np.random.default_rng([zlib.crc32(name.encode()), seed]).standard_normal(out[name].shape)
        drawn = base * np.exp(spread * noise) if base else spread * noise
        out[name] = jnp.asarray(drawn.astype(out[name].dtype))
    for name, factor in factors.items():
        out[name] = (out[name] * factor).astype(out[name].dtype)
    return out
```

```python
from contextlib import ExitStack

import concourse.bass as bass
import numpy as np
from concourse import mybir

F32 = mybir.dt.float32
BF16 = mybir.dt.bfloat16
ACT = mybir.ActivationFunctionType
ALU = mybir.AluOpType
AX = mybir.AxisListType

P = 128
T = 256
NT = T // P
D = 1024
KD = D // P
SLOT = 4096
RING = 6
EPS, LN_EPS = 1e-6, 1e-5
OFF = -1e30

E, CAP = 16, 32
GRP = P // CAP
FF = 2816
FT = FF // P
CHUNK = 4
HD = 64
A_HEADS, C_HEADS, G_HEADS, S_HEADS = 12, 8, 8, 8
C_DIM = 96
KW = 31
LW = 4

STAGES = [("a_in", 6), ("a_out", 2), ("moe0", 3 * E), ("c_in", 3), ("c_up", 1), ("c_out", 2), ("moe1", 3 * E),
          ("ffn0", 17), ("s_in", 4), ("s_out", 2), ("ffn1", 17), ("ffn2", 17), ("r_in", 4), ("r_gate", 1),
          ("r_out", 2), ("ffn3", 17)]
START, N_SLOTS = {}, 0
for _name, _n in STAGES:
    START[_name] = N_SLOTS
    N_SLOTS += _n

PARAMS = [("gains", 10 * KD), ("router", 2 * KD * E), ("gmlp", 256), ("wsT", 4 * P), ("bs", 4), ("cgain", 3),
          ("dgain", 640), ("sinks", 8), ("relb", 8), ("convw", 4 * KW), ("convb", 4), ("lng", 512), ("lnb", 512),
          ("rconvw", KD * LW), ("rconvb", KD), ("gab", KD), ("gxb", KD), ("lam", KD)]
CONSTS = [("ident", P), ("flip", P), ("band", 2 * T), ("ropeA", 4 * 16), ("ropeC", 4 * 32), ("ropeD", 4 * 64),
          ("iota", CAP), ("half", 32)]


def columns(parts):
    at, out = 0, {}
    for name, n in parts:
        out[name] = (at, at + n)
        at += n
    return out, at


PCOL, NPARAM = columns(PARAMS)
CCOL, NCONST = columns(CONSTS)
SPAN = 512


def build(nc, stream, params, consts, buckets, final_rows, x_in, out, debug):
    ctx = ExitStack()
    with ctx:
        def sb(name, shape, dt=F32):
            return ctx.enter_context(nc.sbuf_tensor(name, shape, dt))

        def sem(name):
            return ctx.enter_context(nc.semaphore(name))

        ring = sb("ring", [P, RING, SLOT])
        x = sb("x", [P, NT, D])
        xn = sb("xn", [P, NT, D])
        hT = sb("hT", [P, KD, T])
        cat = sb("cat", [P, NT, D])
        par = sb("par", [P, NPARAM])
        con = sb("con", [P, NCONST])
        work = sb("work", [P, 14848])
        stat = sb("stat", [P, 256])
        ones = sb("ones", [E, T])
        bank = [ctx.enter_context(nc.psum_tensor(f"bank{i}", [P, 512], F32)) for i in range(8)]
        spread = nc.dram_tensor("spread", [8, SPAN], F32)

        def pc(name):
            return par[:, PCOL[name][0]:PCOL[name][1]]

        def cc(name):
            return con[:, CCOL[name][0]:CCOL[name][1]]

        ident, flip = cc("ident"), cc("flip")
        gains = pc("gains").rearrange("p (n k) -> p n k", k=KD)
        W = work

        def region(at, shape):
            n = int(np.prod(shape))
            ap = W[:, at:at + n]
            if len(shape) == 2:
                return ap.rearrange("p (a b) -> p a b", a=shape[0])
            if len(shape) == 3:
                return ap.rearrange("p (a b c) -> p a b c", a=shape[0], b=shape[1])
            return ap

        TMP = 14848 - 3072
        masked = region(TMP, (2, 512))
        probs = region(TMP + 1024, (2, NT, T))
        probsT = region(TMP + 2048, (2, 512))

        const_in = sem("const_in")
        x_loaded = sem("x_loaded")
        slot_in = [sem(f"slot_in{i}") for i in range(RING)]
        slot_used = [sem(f"slot_used{i}") for i in range(RING)]
        x_ready = sem("x_ready")
        pow_ready = sem("pow_ready")
        sq_done = sem("sq_done")
        power_in = sem("power_in")
        power_out = sem("power_out")
        xn_done = sem("xn_done")
        turned = sem("turned")
        turn_out = [sem("turn_out_act"), sem("turn_out_dve")]
        turn_src = sem("turn_src")
        proj_done = [sem("proj0_done"), sem("proj1_done")]
        proj_free = [sem("proj0_free"), sem("proj1_free")]
        dve_step = sem("dve_step")
        gelu_done = sem("gelu_done")
        gating_in = sem("gating_in")
        gating_done = sem("gating_done")
        scores_done = sem("scores_done")
        masked_done = sem("masked_done")
        probs_done = sem("probs_done")
        probs_turned = sem("probs_turned")
        probsT_done = sem("probsT_done")
        heads_done = sem("heads_done")
        cat_done = sem("cat_done")
        route_pe, route_act, route_dve = sem("route_pe"), sem("route_act"), sem("route_dve")
        staged = sem("staged")
        expert_gu = sem("expert_gu")
        expert_silu = sem("expert_silu")
        expert_act = sem("expert_act")
        expert_turned = sem("expert_turned")
        expert_actT = sem("expert_actT")
        y_out = [sem("y_out_act"), sem("y_out_dve")]
        scattered = sem("scattered")
        scatter_added = sem("scatter_added")
        ffn_gu = sem("ffn_gu")
        ffn_silu = sem("ffn_silu")
        ffn_act = sem("ffn_act")
        ffn_down = sem("ffn_down")
        wide_done = sem("wide_done")
        wide_act, wide_dve = sem("wide_act"), sem("wide_dve")
        bucket_in = sem("bucket_in")
        spread_done = sem("spread_done")
        spread_ready = sem("spread_ready")
        spread_out = sem("spread_out")
        rows_in = sem("rows_in")
        bias_done = sem("bias_done")
        bias_out = [sem("bias_out_act"), sem("bias_out_dve")]
        tap_done = sem("tap_done")
        conv_done = sem("conv_done")
        conv_turned = sem("conv_turned")
        ln_done = sem("ln_done")
        conv_cat = sem("conv_cat")
        rec_done = sem("rec_done")
        rec_gates = sem("rec_gates")
        rec_act = sem("rec_act")
        rec_dve = sem("rec_dve")
        final_in = sem("final_in")
        stored = sem("stored")

        def ge(eng, s, v):
            if v > 0:
                eng.wait_ge(s, v)

        def slot(n):
            return ring[:, n % RING, :]

        def loaded(eng, n):
            eng.wait_ge(slot_in[n % RING], 16 * (n // RING + 1))

        def used(eng, n):
            eng.wait_ge(slot_used[n % RING], n // RING + 1)

        def release(ins, n):
            ins.then_inc(slot_used[n % RING], 1)

        dve_steps = [0]

        def step(eng, ins):
            ins.then_inc(dve_step, 1)
            dve_steps[0] += 1
            eng.wait_ge(dve_step, dve_steps[0])

        NORMS = [0, 1, 2, 3, 5, 6, 7, 8, 9, 10]
        FINALS = [4, 11]

        def norm_groups(q):
            groups = []
            for b in range(4):
                pieces = [(xn[:, t, (2 * b + kk) * P:(2 * b + kk + 1) * P], kk * T + t * P, P, P)
                          for kk in range(2) for t in range(NT)]
                outs = [(hT[:, 2 * b + kk, :], (P, kk * T, T), gains[:, q, 2 * b + kk:2 * b + kk + 1])
                        for kk in range(2)]
                groups.append((pieces, outs))
            return groups

        def cat_groups():
            groups = []
            for b in range(4):
                pieces = [(cat[:, t, (2 * b + kk) * P:(2 * b + kk + 1) * P], kk * T + t * P, P, P)
                          for kk in range(2) for t in range(NT)]
                groups.append((pieces, [(hT[:, 2 * b:2 * b + 2, :].rearrange("p a b -> p (a b)"), (P, 0, 512), None)]))
            return groups

        def pair_groups(blocks):
            groups = []
            for i in range(0, len(blocks), 2):
                pieces, outs = [], []
                for kk, (src, rows, dst) in enumerate(blocks[i:i + 2]):
                    pieces += [(src(t), kk * T + t * P, rows, P) for t in range(NT)]
                    outs.append((dst, (rows, kk * T, T), None))
                groups.append((pieces, outs))
            return groups

        uA = region(0, (NT, FF))
        qkA = region(5632, (12, T))
        A_GROUPS = pair_groups([(lambda t, b=b: uA[:, t, b * P:(b + 1) * P], P, qkA[:, b, :]) for b in range(12)])

        uC = region(0, (NT, 1280))
        upq = region(2560, (NT, 768))
        upkv = region(4096, (NT, D))
        qcT = region(6144, (C_HEADS, T))
        kcT = region(8192, (C_HEADS, T))
        dT = region(10240, (6, T))
        cT = region(TMP, (3, T))
        xnf = xn[:, :, :].rearrange("p a b -> p (a b)")
        kc = xnf[:, 0:1536].rearrange("p (t h c) -> p t h c", t=NT, h=C_HEADS)
        dkk = xnf[:, 1536:2048].rearrange("p (t h c) -> p t h c", t=NT, h=4)
        cg = pc("cgain")
        C1_GROUPS = [
            ([(uC[:, t, k * P:(k + 1) * P], k * T + t * P, P, P) for k in range(2) for t in range(NT)],
             [(cT[:, k, :], (P, k * T, T), cg[:, k:k + 1]) for k in range(2)]),
            ([(uC[:, t, 256:384], t * P, P, P) for t in range(NT)], [(cT[:, 2, :], (P, 0, T), cg[:, 2:3])]),
        ]
        C2_GROUPS = pair_groups(
            [(lambda t, h=h: upq[:, t, h * C_DIM:(h + 1) * C_DIM], C_DIM, qcT[0:C_DIM, h, :]) for h in range(C_HEADS)]
            + [(lambda t, h=h: kc[:, t, h, :], C_DIM, kcT[0:C_DIM, h, :]) for h in range(C_HEADS)]
            + [(lambda t, b=b: uC[:, t, 512 + b * P:640 + b * P], P, dT[:, b, :]) for b in range(4)]
            + [(lambda t, b=b: dkk[:, t, 2 * b:2 * b + 2, :].rearrange("p a b -> p (a b)"), P, dT[:, 4 + b, :])
               for b in range(2)])

        uS = region(0, (NT, 768))
        glu = region(1536, (4, T + KW - 1))
        gluf = W[:, 1536:1536 + 4 * (T + KW - 1)]
        gate_s = region(2680, (2, T))
        qkS = region(3192, (6, T))
        bias_s = region(4728, (S_HEADS, 2 * T))
        rows_s = region(TMP - 1024, (S_HEADS, 2 * T))
        conv_s = region(TMP - 1024, (4, T))
        onehot = W[0:32, 8824:8824 + SPAN]
        off_mask = W[0:8, 9336:9336 + SPAN]
        spread_sb = W[0:8, 9848:9848 + SPAN]
        S1_GROUPS = pair_groups([(lambda t, b=b: uS[:, t, b * P:(b + 1) * P], P, qkS[:, b, :]) for b in range(4)]
                                + [(lambda t, b=b: dkk[:, t, 2 * b:2 * b + 2, :].rearrange("p a b -> p (a b)"), P,
                                    qkS[:, 4 + b, :]) for b in range(2)])

        gate_r = region(0, (KD, T))
        pad_r = region(2048, (KD, T + LW - 1))
        pad_rf = W[:, 2048:2048 + KD * (T + LW - 1)]
        rec = region(4120, (KD, T))
        dec = region(6168, (KD, T))
        inp = region(8216, (KD, T))
        tnh = region(10264, (KD, T))
        spare = pad_rf[:, 0:2048].rearrange("p (a b) -> p a b", a=KD)

        hsel = region(0, (GRP, KD, P))
        pick = region(4096, (NT, 512))
        pickg = region(5120, (NT, 512))
        putT = region(6144, (GRP, T))
        hcur = region(7168, (KD, P))
        pcur = region(8192, (T,))
        ybuf = region(8448, (D,))
        silu_e = region(9472, (2, P))
        act_e = region(9728, (2, P))
        actT_e = region(9984, (2, P))
        aff = region(10240, (NT, E))
        scan_a = W[0:E, 10272:10272 + T]
        scan_b = W[0:E, 10528:10528 + T]
        chosen = W[0:E, 10784:10784 + T]
        placed = W[0:E, 11040:11040 + T]
        top8 = W[0:E, 11296:11304]
        posT = region(11304, (NT, E))

        silu_f = region(0, (2, T))
        act_f = region(512, (2, T))

        TURNS, TURN_AT = [], {}
        for name, groups in (("n0", norm_groups(0)), ("a", A_GROUPS), ("cat_a", cat_groups()), ("n1", norm_groups(1)),
                             ("n2", norm_groups(2)), ("c1", C1_GROUPS), ("c2", C2_GROUPS), ("cat_c", cat_groups()),
                             ("n3", norm_groups(3)), ("n4", norm_groups(4)), ("n5", norm_groups(5)),
                             ("s1", S1_GROUPS), ("cat_s", cat_groups()), ("n6", norm_groups(6)),
                             ("n7", norm_groups(7)), ("n8", norm_groups(8)), ("n9", norm_groups(9))):
            TURN_AT[name] = (len(TURNS), len(TURNS) + len(groups))
            TURNS += groups

        def turn_pe(pe, name):
            for g in range(*TURN_AT[name]):
                ge(pe, turn_out[g % 2], g // 2 - 1)
                for src, at, rows, cols in TURNS[g][0]:
                    last = nc.tensor.transpose(bank[g % 4][0:rows, at:at + cols], src, ident)
                last.then_inc(turned, 1)

        def turn_evac(eng, which, name):
            for g in range(*TURN_AT[name]):
                if g % 2 != which:
                    continue
                eng.wait_ge(turned, g + 1)
                for dst, (rows, at, n), gain in TURNS[g][1]:
                    src = bank[g % 4][0:rows, at:at + n]
                    if which == 0:
                        last = nc.scalar.activation(dst, src, ACT.Copy, scale=1.0 if gain is None else gain)
                    elif gain is None:
                        last = nc.vector.tensor_copy(dst, src)
                    else:
                        last = nc.vector.tensor_scalar(dst, src, gain, None, ALU.mult)
                last.then_inc(turn_out[which], 1)

        def turns_out(eng, name):
            end = TURN_AT[name][1]
            ge(eng, turn_out[0], (end + 1) // 2)
            ge(eng, turn_out[1], end // 2)


        PROJ, PROJ_AT = [], {}

        def plain(n, width, last=True):
            w = slot(n).rearrange("p (k n) -> p k n", k=KD)
            return (n, KD, lambda k: w[:, k, 0:width], lambda k, t: hT[:, k, t * P:(t + 1) * P], width, last)

        def up(n, tiles, first, base, stride, width, last):
            return (n, tiles, lambda k: slot(n)[:, base + k * stride:base + k * stride + width],
                    lambda k, t: cT[:, first + k, t * P:(t + 1) * P], width, last)

        def stage(name, items):
            PROJ_AT[name] = (len(PROJ), len(PROJ) + len(items))
            PROJ.extend(items)

        n = START["a_in"]
        stage("a_in", [plain(n + c, 512 if c < 5 else 256) for c in range(6)])
        stage("a_out", [plain(START["a_out"] + c, 512) for c in range(2)])
        n = START["c_in"]
        stage("c_in", [plain(n, 512), plain(n + 1, 512), plain(n + 2, 256)])
        n = START["c_up"]
        stage("c_up", [up(n, 2, 0, 0, 768, 512, False), up(n, 2, 0, 512, 768, 256, False),
                       up(n, 1, 2, 1536, 0, 512, False), up(n, 1, 2, 2048, 0, 512, True)])
        stage("c_out", [plain(START["c_out"] + c, 512) for c in range(2)])
        n = START["s_in"]
        stage("s_in", [plain(n, 512), plain(n + 1, 256, last=False)])
        stage("s_out", [plain(START["s_out"] + c, 512) for c in range(2)])
        stage("r_out", [plain(START["r_out"] + c, 512) for c in range(2)])
        LAST_ADDS = {PROJ_AT[s][1] - 1 for s in ("a_out", "c_out", "s_out", "r_out")}

        def freed(m, t):
            return sum(1 for i in range(m + 1) if not (t == 1 and i in LAST_ADDS))

        def proj_pe(pe, name):
            for m in range(*PROJ_AT[name]):
                n, tiles, rhs, lhs, width, last_use = PROJ[m]
                loaded(pe, n)
                for t in range(NT):
                    if m >= 2:
                        ge(pe, proj_free[t], freed(m - 2, t))
                    for k in range(tiles):
                        mm = nc.tensor.matmul(bank[2 * t + m % 2][:, 0:width], lhs(k, t), rhs(k),
                                              start=(k == 0), stop=(k == tiles - 1))
                    if t == 1 and last_use:
                        release(mm, n)
                    else:
                        mm.then_inc(proj_done[t], 1)

        def proj_out(eng, m, t):
            if t == 1 and PROJ[m][5]:
                used(eng, PROJ[m][0])
            else:
                eng.wait_ge(proj_done[t], sum(1 for i in range(m + 1) if not (t == 1 and PROJ[i][5])))

        def proj_copy(eng, name, t, dst):
            first, end = PROJ_AT[name]
            for m in range(first, end):
                proj_out(eng, m, t)
                src = bank[2 * t + m % 2][:, 0:PROJ[m][4]]
                if t == 0:
                    nc.scalar.activation(dst(m - first), src, ACT.Copy).then_inc(proj_free[t], 1)
                else:
                    nc.vector.tensor_copy(dst(m - first), src).then_inc(proj_free[t], 1)

        def projected(eng, name):
            m = PROJ_AT[name][1] - 1
            eng.wait_ge(proj_free[0], freed(m, 0))
            eng.wait_ge(proj_free[1], freed(m, 1))

        def residual_add(v, name):
            first, end = PROJ_AT[name]
            for m in range(first, end):
                for t in range(NT):
                    proj_out(v, m, t)
                    xs = x[:, t, (m - first) * 512:(m - first + 1) * 512]
                    add = nc.vector.tensor_tensor(xs, bank[2 * t + m % 2][:, :], xs, ALU.add)
                    add.then_inc(x_ready if m == end - 1 and t == 1 else proj_free[t], 1)

        X_SOURCE = [(x_loaded, 16), (x_ready, 1), (scatter_added, 4), (x_ready, 2), (scatter_added, 8), (x_ready, 3),
                    (x_ready, 4), (x_ready, 5), (x_ready, 6), (x_ready, 7), (x_ready, 8), (x_ready, 9)]
        POWERS = {name: i for i, name in enumerate(
            ["n0", "gmlp", "n1", "n2", "heads", "n3", "f0", "n4", "n5", "ln", "n6", "n7", "n8", "n9", "f1"])}
        SS, MS, RS = 64, 66, 68

        def norm_act(act, p):
            act.wait_ge(*X_SOURCE[p])
            nc.scalar.activation(xn[:, 0, :], x[:, 0, :], ACT.Square, accum_out=stat[:, SS:SS + 1]).then_inc(sq_done, 1)

        def power_pool(pool, name, src, dst, w):
            pool.wait_ge(power_in, POWERS[name] + 1)
            nc.gpsimd.tensor_tensor(stat[:, dst:dst + w], stat[:, src:src + w], cc("half")[:, 0:w],
                                    ALU.pow).then_inc(power_out, 1)

        def norm_root(v, p, name):
            v.wait_ge(*X_SOURCE[p])
            nc.vector.tensor_tensor_reduce(xn[:, 1, :], x[:, 1, :], x[:, 1, :], 1.0, 0.0, ALU.mult, ALU.add,
                                           stat[:, SS + 1:SS + 2]).then_inc(sq_done, 1)
            v.wait_ge(sq_done, 2 * (p + 1))
            nc.vector.tensor_scalar(stat[:, MS:MS + 2], stat[:, SS:SS + 2], 1.0 / D, EPS, ALU.mult,
                                    ALU.add).then_inc(power_in, 1)
            v.wait_ge(power_out, POWERS[name] + 1)

        def norm_dve(v, p, q):
            norm_root(v, p, f"n{q}")
            for t in range(NT):
                nc.vector.tensor_scalar(xn[:, t, :], x[:, t, :], stat[:, RS + t:RS + t + 1], None,
                                        ALU.mult).then_inc(xn_done, 1)
            turn_evac(v, 1, f"n{q}")

        def norm_pe(pe, q):
            pe.wait_ge(xn_done, 2 * (q + 1))
            turn_pe(pe, f"n{q}")
            turns_out(pe, f"n{q}")

        def final_norm(v, p, i):
            norm_root(v, p, f"f{i}")
            v.wait_ge(final_in, 16 * (i + 1))
            for t in range(NT):
                last = nc.vector.scalar_tensor_tensor(x[:, t, :], x[:, t, :], stat[:, RS + t:RS + t + 1],
                                                      cat[:, 0, :], ALU.mult, ALU.mult)
            last.then_inc(x_ready, 1)

        def half_rows(h):
            return slice(64 * (h % 2), 64 * (h % 2) + 64)

        band = cc("band")
        HEADS = {
            "a": [(qkA[half_rows(h), h // 2, :], qkA[half_rows(h), 6 + h // 2, :],
                   lambda s, h=h: uA[:, s, 1536 + h * HD:1536 + (h + 1) * HD], HD ** -0.5, band, None, h * HD)
                  for h in range(A_HEADS)],
            "c": [(qcT[0:C_DIM, h, :], kcT[0:C_DIM, h, :], lambda s, h=h: upkv[:, s, h * P + HD:(h + 1) * P],
                   C_DIM ** -0.5, None, None, h * HD) for h in range(C_HEADS)]
                 + [(dT[half_rows(h), h // 2, :], dT[half_rows(h), 4 + h // 4, :],
                     lambda s, h=h: uC[:, s, 1152 + (h // 4) * HD:1152 + (h // 4 + 1) * HD],
                     HD ** -0.5, None, None, 512 + h * HD) for h in range(G_HEADS)],
            "s": [(qkS[half_rows(h), h // 2, :], qkS[half_rows(h), 4 + h // 4, :],
                   lambda s, h=h: uS[:, s, 640 + (h // 4) * HD:640 + (h // 4 + 1) * HD],
                   HD ** -0.5, bias_s[:, h, :], h, h * HD) for h in range(S_HEADS)],
        }
        HEAD_AT = {"a": 0, "c": A_HEADS, "s": A_HEADS + C_HEADS + G_HEADS}
        SINK_NEG = 128

        def attend_pe(pe, name):
            g0, heads = HEAD_AT[name], HEADS[name]
            for i in range(len(heads) + 2):
                if i < len(heads):
                    g, (q, k, *_) = g0 + i, heads[i]
                    ge(pe, masked_done, g - 1)
                    for t in range(NT):
                        mm = nc.tensor.matmul(bank[4 + g % 2][:, t * T:(t + 1) * T], q[:, t * P:(t + 1) * P], k,
                                              start=True, stop=True)
                    mm.then_inc(scores_done, 1)
                if 1 <= i <= len(heads):
                    g = g0 + i - 1
                    pe.wait_ge(probs_done, g + 1)
                    ge(pe, probsT_done, g - 1)
                    for s in range(NT):
                        for t in range(NT):
                            mm = nc.tensor.transpose(bank[6 + g % 2][:, s * T + t * P:s * T + (t + 1) * P],
                                                     probs[:, g % 2, t, s * P:(s + 1) * P], ident)
                    mm.then_inc(probs_turned, 1)
                if i >= 2:
                    g, v = g0 + i - 2, heads[i - 2][2]
                    pe.wait_ge(probsT_done, g + 1)
                    ge(pe, cat_done, g - 1)
                    for t in range(NT):
                        for s in range(NT):
                            mm = nc.tensor.matmul(bank[2 + g % 2][:, t * HD:(t + 1) * HD],
                                                  probsT[:, g % 2, s * T + t * P:s * T + (t + 1) * P], v(s),
                                                  start=(s == 0), stop=(s == NT - 1))
                    mm.then_inc(heads_done, 1)

        def attend_act(act, name):
            g0, heads = HEAD_AT[name], HEADS[name]
            for i in range(len(heads) + 1):
                if i < len(heads):
                    g, at = g0 + i, 16 * ((g0 + i) % 4)
                    act.wait_ge(masked_done, g + 1)
                    ge(act, probs_turned, g - 1)
                    for t in range(NT):
                        last = nc.scalar.activation(probs[:, g % 2, t, :], masked[:, g % 2, t * T:(t + 1) * T],
                                                    ACT.Exp, bias=stat[:, at + t:at + t + 1],
                                                    accum_out=stat[:, at + 2 + t:at + 3 + t])
                    if heads[i][5] is not None:
                        last = nc.scalar.activation(stat[:, at + 6:at + 8], stat[:, at + 4:at + 6], ACT.Exp)
                    last.then_inc(probs_done, 1)
                if i >= 1:
                    g = g0 + i - 1
                    act.wait_ge(probs_turned, g + 1)
                    ge(act, heads_done, g - 1)
                    nc.scalar.activation(probsT[:, g % 2, :], bank[6 + g % 2][:, :], ACT.Copy).then_inc(probsT_done, 1)

        def attend_dve(v, name):
            g0, heads = HEAD_AT[name], HEADS[name]
            for i in range(len(heads) + 2):
                if i < len(heads):
                    scale, bias, sink = heads[i][3:6]
                    g, at = g0 + i, 16 * ((g0 + i) % 4)
                    v.wait_ge(scores_done, g + 1)
                    ge(v, probs_done, g - 1)
                    if bias is None:
                        step(v, nc.vector.tensor_scalar(masked[:, g % 2, :], bank[4 + g % 2][:, :], scale, None,
                                                        ALU.mult))
                    else:
                        step(v, nc.vector.scalar_tensor_tensor(masked[:, g % 2, :], bank[4 + g % 2][:, :], scale,
                                                               bias, ALU.mult, ALU.add))
                    top = nc.vector.tensor_reduce(stat[:, at:at + 2],
                                                  masked[:, g % 2, :].rearrange("p (t s) -> p t s", t=NT), AX.X,
                                                  ALU.max, negate=True)
                    if sink is not None:
                        step(v, top)
                        step(v, nc.vector.tensor_scalar(stat[:, at:at + 2], stat[:, at:at + 2],
                                                        stat[:, SINK_NEG + sink:SINK_NEG + sink + 1], None, ALU.min))
                        top = nc.vector.tensor_scalar(stat[:, at + 4:at + 6], stat[:, at:at + 2],
                                                      pc("sinks")[:, sink:sink + 1], None, ALU.add)
                    top.then_inc(masked_done, 1)
                if i >= 2:
                    g, at = g0 + i - 2, 16 * ((g0 + i - 2) % 4)
                    v.wait_ge(probs_done, g + 1)
                    sums = stat[:, at + 2:at + 4]
                    if heads[i - 2][5] is not None:
                        step(v, nc.vector.tensor_tensor(sums, sums, stat[:, at + 6:at + 8], ALU.add))
                    step(v, nc.vector.reciprocal(stat[:, at + 8:at + 10], sums))
                    v.wait_ge(heads_done, g + 1)
                    col = heads[i - 2][6]
                    nc.vector.tensor_tensor(cat[:, :, col:col + HD],
                                            bank[2 + g % 2][:, 0:NT * HD].rearrange("p (t c) -> p t c", t=NT),
                                            stat[:, at + 8:at + 10].unsqueeze(2).to_broadcast([P, NT, HD]),
                                            ALU.mult).then_inc(cat_done, 1)

        def rope(v, items, half, signal=None):
            at, temps = TMP, []
            for view, cos, sin in items:
                h, r = view.shape[1], view.shape[2]
                a, b = region(at, (h, r)), region(at + h * r, (h, r))
                at += 2 * h * r
                temps.append((a, b))
                nc.vector.tensor_tensor(a, view, cos.unsqueeze(1).to_broadcast([P, h, r]), ALU.mult)
                for lo in range(0, r, 2 * half):
                    mid, hi = lo + half, lo + 2 * half
                    nc.vector.tensor_tensor(b[:, :, lo:mid], view[:, :, mid:hi],
                                            sin[:, lo:mid].unsqueeze(1).to_broadcast([P, h, half]), ALU.mult)
                    last = nc.vector.tensor_tensor(b[:, :, mid:hi], view[:, :, lo:mid],
                                                   sin[:, mid:hi].unsqueeze(1).to_broadcast([P, h, half]), ALU.mult)
            step(v, last)
            for (view, _, _), (a, b) in zip(items, temps):
                last = nc.vector.tensor_tensor(view, a, b, ALU.add)
            if signal is None:
                step(v, last)
            else:
                last.then_inc(signal, 1)

        ropeA = cc("ropeA").rearrange("p (n t c) -> p n t c", n=2, t=NT)
        gate_u = uA[:, :, 2304:2560]
        gate_v = uA[:, :, 2560:2816]

        def a_mix_dve(v):
            proj_copy(v, "a_in", 1, lambda c: uA[:, 1, c * 512:c * 512 + PROJ[PROJ_AT["a_in"][0] + c][4]])
            projected(v, "a_in")
            for t in range(NT):
                rope(v, [(uA[:, t, 0:1536].rearrange("p (h c) -> p h c", c=HD)[:, :, 0:16], ropeA[:, 0, t, :],
                          ropeA[:, 1, t, :])], 8, turn_src if t else None)
            v.wait_ge(gelu_done, 1)
            v.wait_ge(turn_src, 1)
            sq = region(TMP, (NT, 256))
            step(v, nc.vector.tensor_tensor(sq, gate_v, gate_v, ALU.mult))
            step(v, nc.vector.tensor_reduce(stat[:, 80:88].rearrange("p (t g) -> p t g", t=NT),
                                            sq.rearrange("p t (g c) -> p t g c", g=4), AX.X, ALU.add))
            nc.vector.tensor_scalar(stat[:, 80:88], stat[:, 80:88], 1.0 / HD, EPS, ALU.mult,
                                    ALU.add).then_inc(power_in, 1)
            v.wait_ge(power_out, POWERS["gmlp"] + 1)
            for t in range(NT):
                gv = gate_v[:, t, :].rearrange("p (g c) -> p g c", g=4)
                last = nc.vector.tensor_tensor(gv, gv, stat[:, 104 + 4 * t:108 + 4 * t].unsqueeze(2)
                                               .to_broadcast([P, 4, HD]), ALU.mult)
            step(v, last)
            nc.vector.tensor_tensor(gate_v, gate_v, pc("gmlp").unsqueeze(1).to_broadcast([P, NT, 256]),
                                    ALU.mult).then_inc(gating_in, 1)
            turn_evac(v, 1, "a")
            v.wait_ge(gating_done, 1)
            for g in range(4):
                mixed = bank[0][:, :].rearrange("p (t c) -> p t c", t=NT)[:, :, g * HD:(g + 1) * HD]
                last = nc.vector.scalar_tensor_tensor(cat[:, :, 768 + g * HD:768 + (g + 1) * HD], mixed,
                                                      pc("bs")[:, g:g + 1], gate_u[:, :, g * HD:(g + 1) * HD],
                                                      ALU.add, ALU.mult)
            last.then_inc(turn_src, 1)
            attend_dve(v, "a")
            turn_evac(v, 1, "cat_a")
            residual_add(v, "a_out")

        def a_mix_act(act):
            proj_copy(act, "a_in", 0, lambda c: uA[:, 0, c * 512:c * 512 + PROJ[PROJ_AT["a_in"][0] + c][4]])
            projected(act, "a_in")
            nc.scalar.activation(uA[:, :, 2304:2816], uA[:, :, 2304:2816], ACT.Gelu_apprx_tanh).then_inc(gelu_done, 1)
            turn_evac(act, 0, "a")
            attend_act(act, "a")
            turn_evac(act, 0, "cat_a")

        def a_mix_pe(pe):
            proj_pe(pe, "a_in")
            pe.wait_ge(turn_src, 1)
            turn_pe(pe, "a")
            turns_out(pe, "a")
            pe.wait_ge(gating_in, 1)
            wsT = pc("wsT").rearrange("p (g q) -> p g q", g=4)
            for t in range(NT):
                for g in range(4):
                    mm = nc.tensor.matmul(bank[0][:, t * 256 + g * HD:t * 256 + (g + 1) * HD], wsT[:, g, :],
                                          gate_v[:, t, g * HD:(g + 1) * HD], start=True, stop=True)
            mm.then_inc(gating_done, 1)
            attend_pe(pe, "a")
            pe.wait_ge(turn_src, 2)
            pe.wait_ge(cat_done, HEAD_AT["a"] + A_HEADS)
            turn_pe(pe, "cat_a")
            turns_out(pe, "cat_a")
            proj_pe(pe, "a_out")

        ropeC = cc("ropeC").rearrange("p (n t c) -> p n t c", n=2, t=NT)
        ropeD = cc("ropeD").rearrange("p (n t c) -> p n t c", n=2, t=NT)

        def c_mix_dve(v):
            proj_copy(v, "c_in", 1, lambda c: uC[:, 1, c * 512:c * 512 + PROJ[PROJ_AT["c_in"][0] + c][4]])
            projected(v, "c_in")
            sq = W[:, 6144:6144 + 2304].rearrange("p (t c) -> p t c", t=NT)
            for t in range(NT):
                last = nc.vector.tensor_tensor(sq[:, t, :], uC[:, t, 0:1152], uC[:, t, 0:1152], ALU.mult)
            step(v, last)
            nc.vector.tensor_reduce(stat[:, 80:82], sq[:, :, 0:256], AX.X, ALU.add)
            nc.vector.tensor_reduce(stat[:, 82:84], sq[:, :, 256:384], AX.X, ALU.add)
            for t in range(NT):
                last = nc.vector.tensor_reduce(stat[:, 84 + 10 * t:94 + 10 * t],
                                               sq[:, t, 512:1152].rearrange("p (h c) -> p h c", c=HD), AX.X, ALU.add)
            step(v, last)
            nc.vector.tensor_scalar(stat[:, 80:82], stat[:, 80:82], 1.0 / 256, EPS, ALU.mult, ALU.add)
            nc.vector.tensor_scalar(stat[:, 82:84], stat[:, 82:84], 1.0 / 128, EPS, ALU.mult, ALU.add)
            nc.vector.tensor_scalar(stat[:, 84:104], stat[:, 84:104], 1.0 / HD, EPS, ALU.mult,
                                    ALU.add).then_inc(power_in, 1)
            v.wait_ge(power_out, POWERS["heads"] + 1)
            for t in range(NT):
                nc.vector.tensor_scalar(uC[:, t, 0:256], uC[:, t, 0:256], stat[:, 104 + t:105 + t], None, ALU.mult)
                last = nc.vector.tensor_scalar(uC[:, t, 256:384], uC[:, t, 256:384], stat[:, 106 + t:107 + t], None,
                                               ALU.mult)
            last.then_inc(turn_src, 1)
            for t in range(NT):
                dv = uC[:, t, 512:1152].rearrange("p (h c) -> p h c", c=HD)
                last = nc.vector.tensor_tensor(dv, dv, stat[:, 108 + 10 * t:118 + 10 * t].unsqueeze(2)
                                               .to_broadcast([P, 10, HD]), ALU.mult)
            step(v, last)
            step(v, nc.vector.tensor_tensor(uC[:, :, 512:1152], uC[:, :, 512:1152],
                                            pc("dgain").unsqueeze(1).to_broadcast([P, NT, 640]), ALU.mult))
            turn_evac(v, 1, "c1")
            turns_out(v, "c1")
            proj_copy(v, "c_up", 1, lambda c: (upq[:, 1, 0:512], upq[:, 1, 512:768], upkv[:, 1, 0:512],
                                               upkv[:, 1, 512:1024])[c])
            projected(v, "c_up")
            for t in range(NT):
                rope(v, [(uC[:, t, 512:1152].rearrange("p (h c) -> p h c", c=HD), ropeD[:, 0, t, :],
                          ropeD[:, 1, t, :])], 16)
                rope(v, [(upq[:, t, :].rearrange("p (h c) -> p h c", c=C_DIM)[:, :, HD:C_DIM], ropeC[:, 0, t, :],
                          ropeC[:, 1, t, :]),
                         (uC[:, t, 384:416].unsqueeze(1), ropeC[:, 0, t, :], ropeC[:, 1, t, :])], 16)
            for t in range(NT):
                nc.vector.tensor_copy(kc[:, t, :, 0:HD], upkv[:, t, :].rearrange("p (h c) -> p h c", h=8)[:, :, 0:HD])
                nc.vector.tensor_copy(kc[:, t, :, HD:C_DIM],
                                      uC[:, t, 384:416].unsqueeze(1).to_broadcast([P, C_HEADS, C_DIM - HD]))
                for b in range(4):
                    last = nc.vector.tensor_copy(dkk[:, t, b, :], uC[:, t, 1024 + (b // 2) * HD:1088 + (b // 2) * HD])
            last.then_inc(turn_src, 1)
            turn_evac(v, 1, "c2")
            attend_dve(v, "c")
            turn_evac(v, 1, "cat_c")
            residual_add(v, "c_out")

        def c_mix_act(act):
            proj_copy(act, "c_in", 0, lambda c: uC[:, 0, c * 512:c * 512 + PROJ[PROJ_AT["c_in"][0] + c][4]])
            turn_evac(act, 0, "c1")
            proj_copy(act, "c_up", 0, lambda c: (upq[:, 0, 0:512], upq[:, 0, 512:768], upkv[:, 0, 0:512],
                                                 upkv[:, 0, 512:1024])[c])
            turn_evac(act, 0, "c2")
            attend_act(act, "c")
            turn_evac(act, 0, "cat_c")

        def c_mix_pe(pe):
            proj_pe(pe, "c_in")
            pe.wait_ge(turn_src, 3)
            turn_pe(pe, "c1")
            turns_out(pe, "c1")
            proj_pe(pe, "c_up")
            pe.wait_ge(turn_src, 4)
            turn_pe(pe, "c2")
            turns_out(pe, "c2")
            attend_pe(pe, "c")
            pe.wait_ge(cat_done, HEAD_AT["c"] + C_HEADS + G_HEADS)
            turn_pe(pe, "cat_c")
            turns_out(pe, "cat_c")
            proj_pe(pe, "c_out")

        router = pc("router").rearrange("p (l k e) -> p l k e", l=2, k=KD)
        iota = cc("iota")

        def moe_pe(pe, l, n0):
            q = 1 if l == 0 else 3
            s, a, d = 13 * l, 6 * l, 10 * l
            for t in range(NT):
                for k in range(KD):
                    mm = nc.tensor.matmul(bank[4][:, t * E:(t + 1) * E], hT[:, k, t * P:(t + 1) * P],
                                          router[:, l, k, :], start=(k == 0), stop=(k == KD - 1))
            mm.then_inc(route_pe, 1)
            pe.wait_ge(route_dve, d + 2)
            for t in range(NT):
                mm = nc.tensor.transpose(bank[5][0:E, t * P:(t + 1) * P], aff[:, t, :], ident)
            mm.then_inc(route_pe, 1)
            pe.wait_ge(route_dve, d + 3)
            for t in range(NT):
                mm = nc.tensor.transpose(bank[4][:, t * E:(t + 1) * E], placed[:, t * P:(t + 1) * P], ident[0:E, 0:E])
            mm.then_inc(route_pe, 1)
            pe.wait_ge(route_dve, d + 4)
            for k in range(KD):
                if k >= 4:
                    pe.wait_ge(*((route_act, a + 2 + (k - 4) // 2) if k % 2 == 0 else (route_dve, d + 6 + (k - 4) // 2)))
                for t in range(NT):
                    mm = nc.tensor.matmul(bank[k % 4][:, :], xn[:, t, k * P:(k + 1) * P], pick[:, t, :],
                                          start=(t == 0), stop=(t == NT - 1))
                mm.then_inc(route_pe, 1)
            pe.wait_ge(route_dve, d + 5)
            for b in range(2):
                for gg in range(2):
                    for t in range(NT):
                        mm = nc.tensor.transpose(bank[6 + b][:, gg * T + t * P:gg * T + (t + 1) * P],
                                                 pickg[:, t, (2 * b + gg) * P:(2 * b + gg + 1) * P], ident)
                mm.then_inc(route_pe, 1)
            pe.wait_ge(route_act, a + 6)
            pe.wait_ge(route_dve, d + 10)
            with pe.Fori(0, E // GRP) as g:
                seen = 4 * l + g
                pe.wait_ge(staged, seen + 1)
                for e in range(GRP):
                    na, nb, nd = n0 + 3 * e, n0 + 3 * e + 1, n0 + 3 * e + 2
                    for half, n in enumerate((na, nb)):
                        pe.wait_ge(slot_in[n % RING], 16 * (n // RING + 1) + 32 * g)
                        w = slot(n).rearrange("p (k m c) -> p k m c", k=4, m=2)
                        for kk in range(4):
                            for j in range(4):
                                mm = nc.tensor.matmul(bank[4 + e % 2][32 * j:32 * j + 32, 0:256],
                                                      hcur[:, 4 * half + kk, e * CAP:(e + 1) * CAP],
                                                      w[:, kk, :, j * P:(j + 1) * P],
                                                      start=(half == 0 and kk == 0), stop=(half == 1 and kk == 3),
                                                      skip_group_check=True)
                        if half == 0:
                            release(mm, na)
                        else:
                            mm.then_inc(expert_gu, 1)
                    pe.wait_ge(expert_act, 4 * seen + e + 1)
                    nc.tensor.transpose(bank[6][:, 0:P], act_e[:, e % 2, :], ident).then_inc(expert_turned, 1)
                    pe.wait_ge(expert_actT, 4 * seen + e + 1)
                    pe.wait_ge(slot_in[nd % RING], 16 * (nd // RING + 1) + 32 * g)
                    if e >= 1:
                        pe.wait_ge(y_out[0], 4 * seen + e)
                        pe.wait_ge(y_out[1], 4 * seen + e)
                    w = slot(nd).rearrange("p (j c) -> p j c", j=4)
                    for j in range(4):
                        for i in range(4):
                            mm = nc.tensor.matmul(bank[7][32 * i:32 * i + 32, 0:256],
                                                  actT_e[:, e % 2, j * CAP:(j + 1) * CAP],
                                                  w[:, j, i * 256:(i + 1) * 256], start=(j == 0), stop=(j == 3),
                                                  skip_group_check=True)
                            if j == 0 and i == 0:
                                release(mm, nb)
                    release(mm, nd)
                pe.wait_ge(y_out[0], 4 * seen + 4)
                pe.wait_ge(y_out[1], 4 * seen + 4)
                for t in range(NT):
                    for half in range(2):
                        mm = nc.tensor.matmul(bank[2 * t + half][:, :], pcur[:, t * P:(t + 1) * P],
                                              ybuf[:, half * 512:(half + 1) * 512], start=True, stop=True)
                mm.then_inc(scattered, 1)

        def moe_act(act, l, n0):
            q = 1 if l == 0 else 3
            s, d = 13 * l, 10 * l
            act.wait_ge(route_dve, d + 1)
            for t in range(NT):
                last = nc.scalar.activation(aff[:, t, :], bank[4][:, t * E:(t + 1) * E], ACT.Exp,
                                            bias=stat[:, 72 + t:73 + t], accum_out=stat[:, 74 + t:75 + t])
            last.then_inc(route_act, 1)
            for k in range(0, KD, 2):
                act.wait_ge(route_pe, s + 4 + k)
                nc.scalar.activation(hsel[:, :, k, :], bank[k % 4][:, :].rearrange("p (g c) -> p g c", g=GRP),
                                     ACT.Copy, scale=gains[:, q, k:k + 1]).then_inc(route_act, 1)
            act.wait_ge(route_pe, s + 12)
            nc.scalar.activation(putT[:, 0:2, :].rearrange("p a b -> p (a b)"), bank[6][:, :],
                                 ACT.Copy).then_inc(route_act, 1)
            with act.Fori(0, E // GRP) as g:
                seen = 4 * l + g
                for e in range(GRP):
                    nd = n0 + 3 * e + 2
                    act.wait_ge(expert_gu, 4 * seen + e + 1)
                    nc.scalar.activation(silu_e[:, e % 2, :], bank[4 + e % 2][:, 0:P], ACT.Silu).then_inc(expert_silu, 1)
                    if e == 0:
                        act.wait_ge(scattered, seen + 1)
                    act.wait_ge(slot_used[nd % RING], nd // RING + 1 + 2 * g)
                    for i in range(2):
                        last = nc.scalar.activation(ybuf[32 * e:32 * e + 32, i * 256:(i + 1) * 256],
                                                    bank[7][32 * i:32 * i + 32, 0:256], ACT.Copy)
                    last.then_inc(y_out[0], 1)

        def moe_dve(v, l, n0):
            q = 1 if l == 0 else 3
            s, a = 13 * l, 6 * l
            v.wait_ge(route_pe, s + 1)
            nc.vector.tensor_reduce(stat[:, 72:74], bank[4][:, 0:NT * E].rearrange("p (t e) -> p t e", t=NT), AX.X,
                                    ALU.max, negate=True).then_inc(route_dve, 1)
            v.wait_ge(route_act, a + 1)
            step(v, nc.vector.reciprocal(stat[:, 76:78], stat[:, 74:76]))
            nc.vector.tensor_tensor(aff, aff, stat[:, 76:78].unsqueeze(2).to_broadcast([P, NT, E]),
                                    ALU.mult).then_inc(route_dve, 1)
            v.wait_ge(route_pe, s + 2)
            step(v, nc.vector.tensor_copy(scan_a, bank[5][0:E, 0:T]))
            src, dst = scan_a, scan_b
            for _ in range(CAP // 8):
                step(v, nc.vector.max(top8, src))
                step(v, nc.vector.match_replace(dst, top8, src, -1.0))
                src, dst = dst, src
            step(v, nc.vector.tensor_scalar(chosen, src, -1.0, None, ALU.is_equal))
            step(v, nc.vector.tensor_tensor_scan(dst, ones[:, :], chosen, 0.0, ALU.mult, ALU.add))
            step(v, nc.vector.tensor_tensor(placed, dst, chosen, ALU.mult))
            nc.vector.tensor_scalar(placed, placed, -1.0, None, ALU.add).then_inc(route_dve, 1)
            v.wait_ge(route_pe, s + 3)
            step(v, nc.vector.tensor_copy(posT.rearrange("p t e -> p (t e)"), bank[4][:, 0:NT * E]))
            for t in range(NT):
                last = nc.vector.tensor_tensor(pick[:, t, :].rearrange("p (e c) -> p e c", e=E),
                                               iota.unsqueeze(1).to_broadcast([P, E, CAP]),
                                               posT[:, t, :].unsqueeze(2).to_broadcast([P, E, CAP]), ALU.is_equal)
            last.then_inc(route_dve, 1)
            v.wait_ge(route_dve, 10 * l + 4)
            for t in range(NT):
                last = nc.vector.tensor_tensor(pickg[:, t, :].rearrange("p (e c) -> p e c", e=E),
                                               pick[:, t, :].rearrange("p (e c) -> p e c", e=E),
                                               aff[:, t, :].unsqueeze(2).to_broadcast([P, E, CAP]), ALU.mult)
            last.then_inc(route_dve, 1)
            for k in range(1, KD, 2):
                v.wait_ge(route_pe, s + 4 + k)
                nc.vector.tensor_scalar(hsel[:, :, k, :], bank[k % 4][:, :].rearrange("p (g c) -> p g c", g=GRP),
                                        gains[:, q, k:k + 1], None, ALU.mult).then_inc(route_dve, 1)
            v.wait_ge(route_pe, s + 13)
            nc.vector.tensor_copy(putT[:, 2:4, :].rearrange("p a b -> p (a b)"),
                                  bank[7][:, :]).then_inc(route_dve, 1)
            with v.Fori(0, E // GRP) as g:
                seen = 4 * l + g
                for e in range(GRP):
                    nd = n0 + 3 * e + 2
                    v.wait_ge(expert_silu, 4 * seen + e + 1)
                    nc.vector.tensor_tensor(act_e[:, e % 2, :], silu_e[:, e % 2, :], bank[4 + e % 2][:, P:2 * P],
                                            ALU.mult).then_inc(expert_act, 1)
                    v.wait_ge(expert_turned, 4 * seen + e + 1)
                    nc.vector.tensor_copy(actT_e[:, e % 2, :], bank[6][:, 0:P]).then_inc(expert_actT, 1)
                    if e == 0:
                        v.wait_ge(scattered, seen + 1)
                    v.wait_ge(slot_used[nd % RING], nd // RING + 1 + 2 * g)
                    for i in range(2, 4):
                        last = nc.vector.tensor_copy(ybuf[32 * e:32 * e + 32, i * 256:(i + 1) * 256],
                                                     bank[7][32 * i:32 * i + 32, 0:256])
                    last.then_inc(y_out[1], 1)
                v.wait_ge(scattered, seen + 2)
                for t in range(NT):
                    for half in range(2):
                        xs = x[:, t, half * 512:(half + 1) * 512]
                        last = nc.vector.tensor_tensor(xs, bank[2 * t + half][:, :], xs, ALU.add)
                last.then_inc(scatter_added, 1)

        def moe_pool(pool, l):
            pool.wait_ge(route_act, 6 * l + 6)
            pool.wait_ge(route_dve, 10 * l + 10)
            with pool.Fori(0, E // GRP) as g:
                pool.wait_ge(scattered, 4 * l + g + 1)
                nc.gpsimd.tensor_copy(hcur.rearrange("p k c -> p (k c)"), W[:, bass.ds(g * (KD * P), KD * P)])
                nc.gpsimd.tensor_copy(pcur, W[:, bass.ds(g * T + 6144, T)]).then_inc(staged, 1)

        def ffn_slots(n0, f):
            c = f // CHUNK
            last = c == FT // CHUNK
            return (n0 + 3 * c, n0 + 3 * c + (0 if last else 1), n0 + 3 * c + (1 if last else 2)), last

        def ffn_pe(pe, i, n0):
            base, dbase = FT * i, (FT - 1) * i

            def gate_up(f, it=0):
                (ng, nu, _), last = ffn_slots(n0, f)
                if f % CHUNK == 0:
                    for n in sorted({ng, nu}):
                        pe.wait_ge(slot_in[n % RING], 16 * (n // RING + 1) + 16 * it)
                if f >= 4:
                    pe.wait_ge(ffn_act, base + f - 3 + 8 * it)
                wg, wu = (slot(n).rearrange("p (k c) -> p k c", k=KD) for n in (ng, nu))
                for w, at, col in ((wg, 0, f % CHUNK), (wu, T, f % CHUNK + (2 if last else 0))):
                    for k in range(KD):
                        mm = nc.tensor.matmul(bank[4 + f % 4][:, at:at + T], w[:, k, col * P:(col + 1) * P],
                                              hT[:, k, :], start=(k == 0), stop=(k == KD - 1))
                mm.then_inc(ffn_gu, 1)

            def down(f, it=0):
                (ng, nu, nd), last = ffn_slots(n0, f)
                if f % CHUNK == 0:
                    pe.wait_ge(slot_in[nd % RING], 16 * (nd // RING + 1) + 16 * it)
                pe.wait_ge(ffn_act, base + f + 1 + 8 * it)
                w = slot(nd).rearrange("p (j c) -> p j c", j=CHUNK)
                for j in range(4):
                    t, half = j // 2, j % 2
                    mm = nc.tensor.matmul(bank[j][:, :], act_f[:, f % 2, t * P:(t + 1) * P],
                                          w[:, f % CHUNK, half * 512:(half + 1) * 512], start=(f == 0),
                                          stop=(f == FT - 1), skip_group_check=True)
                    if j == 0 and (f % CHUNK == CHUNK - 1 or f == FT - 1):
                        release(mm, ng)
                    if j == 1 and f % CHUNK == CHUNK - 1:
                        release(mm, nu)
                    if j == 2 and f % CHUNK == 0 and f > 0:
                        release(mm, nd - (2 if last else 3))
                if f == FT - 1:
                    release(mm, nd)
                else:
                    mm.then_inc(ffn_down, 1)

            gate_up(0)
            gate_up(1)
            down(0)
            with pe.Fori(0, 2) as it:
                for f in range(1, 9):
                    gate_up(f + 1, it)
                    down(f, it)
            for f in range(17, FT):
                if f + 1 < FT:
                    gate_up(f + 1)
                down(f)

        def ffn_act_engine(act, i):
            base = FT * i

            def silu(f, it=0):
                act.wait_ge(ffn_gu, base + f + 1 + 4 * it)
                if f >= 2:
                    act.wait_ge(ffn_act, base + f - 1 + 4 * it)
                nc.scalar.activation(silu_f[:, f % 2, :], bank[4 + f % 4][:, 0:T], ACT.Silu).then_inc(ffn_silu, 1)

            silu(0)
            silu(1)
            with act.Fori(0, 5) as it:
                for f in range(2, 6):
                    silu(f, it)

        def ffn_dve(v, i, n0):
            base, dbase = FT * i, (FT - 1) * i

            def multiply(f, it=0):
                v.wait_ge(ffn_silu, base + f + 1 + 4 * it)
                if f >= 2:
                    v.wait_ge(ffn_down, dbase + f - 1 + 4 * it)
                nc.vector.tensor_tensor(act_f[:, f % 2, :], silu_f[:, f % 2, :], bank[4 + f % 4][:, T:2 * T],
                                        ALU.mult).then_inc(ffn_act, 1)

            multiply(0)
            multiply(1)
            with v.Fori(0, 5) as it:
                for f in range(2, 6):
                    multiply(f, it)
            used(v, n0 + 16)
            for j in range(4):
                t, half = j // 2, j % 2
                xs = x[:, t, half * 512:(half + 1) * 512]
                last = nc.vector.scalar_tensor_tensor(xs, bank[j][:, :], 0.5, xs, ALU.mult, ALU.add)
            last.then_inc(x_ready, 1)

        onehot_sp = W[0:32, 8824:8824 + SPAN]

        def s_mix_pe(pe):
            n0 = START["s_in"]
            proj_pe(pe, "s_in")
            places = [(n0 + 1, 256, 384), (n0 + 2, 0, P), (n0 + 2, 256, 384), (n0 + 3, 0, P)]
            for c, (n, av, ag) in enumerate(places):
                loaded(pe, n)
                w = slot(n).rearrange("p (k c) -> p k c", k=KD)
                for at, col in ((0, av), (T, ag)):
                    for k in range(KD):
                        mm = nc.tensor.matmul(bank[4 + c][:, at:at + T], w[:, k, col:col + P], hT[:, k, :],
                                              start=(k == 0), stop=(k == KD - 1))
                if c == 1:
                    mm.then_inc(wide_done, 1)
                else:
                    release(mm, n)
            pe.wait_ge(turn_src, 5)
            turn_pe(pe, "s1")
            turns_out(pe, "s1")
            pe.wait_ge(bucket_in, 32)
            pe.wait_ge(wide_act, 4)
            pe.wait_ge(wide_dve, 4)
            nc.tensor.matmul(bank[4][0:8, :], pc("relb")[0:32, :], onehot, start=True, stop=True).then_inc(spread_done, 1)
            pe.wait_ge(rows_in, 32)
            for h in range(S_HEADS):
                ge(pe, bias_out[h % 2], h // 2 - 1)
                nc.tensor.matmul(bank[4 + h % 4][:, :], flip, rows_s[:, h, :], start=True,
                                 stop=True).then_inc(bias_done, 1)
            pe.wait_ge(bias_out[0], 4)
            pe.wait_ge(bias_out[1], 4)
            attend_pe(pe, "s")
            pe.wait_ge(conv_done, 1)
            for t in range(NT):
                for c in range(4):
                    mm = nc.tensor.transpose(bank[t][:, c * P:(c + 1) * P], conv_s[:, c, t * P:(t + 1) * P], ident)
            mm.then_inc(conv_turned, 1)
            pe.wait_ge(conv_cat, 1)
            pe.wait_ge(cat_done, HEAD_AT["s"] + S_HEADS)
            turn_pe(pe, "cat_s")
            turns_out(pe, "cat_s")
            proj_pe(pe, "s_out")

        def s_mix_act(act):
            n0 = START["s_in"]
            act.wait_ge(*X_SOURCE[6])
            act.dma_start(onehot, buckets[0:32, :]).then_inc(bucket_in, 16)
            act.dma_start(off_mask, buckets[32:40, :]).then_inc(bucket_in, 16)
            proj_copy(act, "s_in", 0, lambda c: (uS[:, 0, 0:512], uS[:, 0, 512:768])[c])
            for c in range(4):
                if c == 1:
                    act.wait_ge(wide_done, 1)
                else:
                    used(act, n0 + (1, 2, 2, 3)[c])
                ge(act, wide_dve, c - 1)
                nc.scalar.activation(gate_s[:, c % 2, :], bank[4 + c][:, T:2 * T], ACT.Sigmoid).then_inc(wide_act, 1)
            turn_evac(act, 0, "s1")
            act.wait_ge(spread_ready, 1)
            act.dma_start(spread.ap(), spread_sb).then_inc(spread_out, 16)
            act.wait_ge(spread_out, 16)
            for t in range(NT):
                src = bass.AP(tensor=spread, offset=P - P * t, ap=[[1, P], [SPAN, S_HEADS], [1, T]])
                act.dma_start(rows_s[:, :, t * T:(t + 1) * T], src).then_inc(rows_in, 16)
            for h in range(0, S_HEADS, 2):
                act.wait_ge(bias_done, h + 1)
                nc.scalar.activation(bias_s[:, h, :], bank[4 + h % 4][:, :], ACT.Copy).then_inc(bias_out[0], 1)
            attend_act(act, "s")
            act.wait_ge(ln_done, 1)
            nc.scalar.activation(cat[:, :, 512:1024], cat[:, :, 512:1024], ACT.Silu).then_inc(conv_cat, 1)
            turn_evac(act, 0, "cat_s")

        def s_mix_dve(v):
            v.wait_ge(x_ready, 4)
            step(v, nc.vector.tensor_scalar(stat[:, SINK_NEG:SINK_NEG + 8], pc("sinks"), -1.0, None, ALU.mult))
            nc.vector.memset(gluf, 0.0)
            proj_copy(v, "s_in", 1, lambda c: (uS[:, 1, 0:512], uS[:, 1, 512:768])[c])
            projected(v, "s_in")
            for t in range(NT):
                for b in range(4):
                    last = nc.vector.tensor_copy(dkk[:, t, b, :], uS[:, t, 512 + (b // 2) * HD:576 + (b // 2) * HD])
            last.then_inc(turn_src, 1)
            for c in range(4):
                v.wait_ge(wide_act, c + 1)
                nc.vector.tensor_tensor(glu[:, c, KW - 1:], gate_s[:, c % 2, :], bank[4 + c][:, 0:T],
                                        ALU.mult).then_inc(wide_dve, 1)
            turn_evac(v, 1, "s1")
            v.wait_ge(spread_done, 1)
            v.wait_ge(bucket_in, 32)
            nc.vector.tensor_tensor(spread_sb, bank[4][0:8, :], off_mask, ALU.add).then_inc(spread_ready, 1)
            for h in range(1, S_HEADS, 2):
                v.wait_ge(bias_done, h + 1)
                nc.vector.tensor_copy(bias_s[:, h, :], bank[4 + h % 4][:, :]).then_inc(bias_out[1], 1)
            attend_dve(v, "s")
            v.wait_ge(bias_done, 8)
            v.wait_ge(wide_dve, 4)
            convw = pc("convw").rearrange("p (c j) -> p c j", c=4)
            for i in range(4 * KW):
                j, c = i // 4, i % 4
                g = glu[:, c, j:j + T]
                if j == 0:
                    tap = nc.vector.tensor_scalar(conv_s[:, c, :], g, convw[:, c, 0:1], pc("convb")[:, c:c + 1],
                                                  ALU.mult, ALU.add)
                else:
                    v.wait_ge(tap_done, i - 3)
                    tap = nc.vector.scalar_tensor_tensor(conv_s[:, c, :], g, convw[:, c, j:j + 1], conv_s[:, c, :],
                                                         ALU.mult, ALU.add)
                tap.then_inc(conv_done if i == 4 * KW - 1 else tap_done, 1)
            v.wait_ge(conv_turned, 1)
            for t in range(NT):
                last = nc.vector.bn_stats(stat[:, 136 + 6 * t:142 + 6 * t], bank[t][:, :])
            step(v, last)
            for t in range(NT):
                last = nc.vector.bn_aggr(stat[:, 148 + 2 * t:150 + 2 * t], stat[:, 136 + 6 * t:142 + 6 * t])
            step(v, last)
            nc.vector.tensor_scalar(stat[:, 80:84], stat[:, 148:152], LN_EPS, None, ALU.add).then_inc(power_in, 1)
            v.wait_ge(power_out, POWERS["ln"] + 1)
            ct = cat[:, :, 512:1024]
            for t in range(NT):
                last = nc.vector.tensor_scalar(ct[:, t, :], bank[t][:, :], stat[:, 148 + 2 * t:149 + 2 * t],
                                               stat[:, 105 + 2 * t:106 + 2 * t], ALU.subtract, ALU.mult)
            step(v, last)
            step(v, nc.vector.tensor_tensor(ct, ct, pc("lng").unsqueeze(1).to_broadcast([P, NT, 512]), ALU.mult))
            nc.vector.tensor_tensor(ct, ct, pc("lnb").unsqueeze(1).to_broadcast([P, NT, 512]), ALU.add)\
                .then_inc(ln_done, 1)
            turn_evac(v, 1, "cat_s")
            residual_add(v, "s_out")

        gab, gxb, lam = pc("gab"), pc("gxb"), pc("lam")
        rconvw = pc("rconvw").rearrange("p (k j) -> p k j", k=KD)
        C8 = 160

        def r_mix_pe(pe):
            n0 = START["r_in"]
            for g in range(8):
                n = n0 + g // 2
                loaded(pe, n)
                if g >= 4:
                    pe.wait_ge(wide_act, 4 + g - 3)
                w = slot(n).rearrange("p (k c) -> p k c", k=KD)
                for i in range(2):
                    col = (g % 2) * 256 + i * P
                    for k in range(KD):
                        mm = nc.tensor.matmul(bank[g % 4][:, i * T:(i + 1) * T], w[:, k, col:col + P], hT[:, k, :],
                                              start=(k == 0), stop=(k == KD - 1))
                if g % 2:
                    release(mm, n)
                else:
                    mm.then_inc(wide_done, 1)
            n = START["r_gate"]
            loaded(pe, n)
            for h in range(KD):
                pe.wait_ge(rec_done, h + 1)
                if h >= 4:
                    pe.wait_ge(rec_act, h - 1)
                for m in range(2):
                    mm = nc.tensor.matmul(bank[4 + h % 4][:, m * T:(m + 1) * T],
                                          slot(n)[:, (m * KD + h) * P:(m * KD + h + 1) * P], rec[:, h, :],
                                          start=True, stop=True)
                if h == KD - 1:
                    release(mm, n)
                else:
                    mm.then_inc(rec_gates, 1)
            pe.wait_ge(rec_dve, 5)
            proj_pe(pe, "r_out")

        def r_mix_act(act):
            n0 = START["r_in"]
            for g in range(4):
                if g % 2:
                    used(act, n0 + g // 2)
                else:
                    act.wait_ge(wide_done, 2 + g // 2)
                nc.scalar.activation(gate_r[:, 2 * g:2 * g + 2, :].rearrange("p a b -> p (a b)"), bank[g][:, :],
                                     ACT.Gelu_apprx_tanh).then_inc(wide_act, 1)
            act.wait_ge(rec_dve, 1)
            nc.scalar.activation(stat[:, 176:184], stat[:, 168:176], ACT.Exp).then_inc(rec_act, 1)
            act.wait_ge(rec_dve, 2)
            nc.scalar.activation(stat[:, 192:200], stat[:, 184:192], ACT.Ln).then_inc(rec_act, 1)

        def r_gates_act(act):
            for h in range(KD):
                if h == KD - 1:
                    used(act, START["r_gate"])
                else:
                    act.wait_ge(rec_gates, h + 1)
                nc.scalar.activation(dec[:, h, :], bank[4 + h % 4][:, 0:T], ACT.Sigmoid, bias=gab[:, h:h + 1])
                nc.scalar.activation(inp[:, h, :], bank[4 + h % 4][:, T:2 * T], ACT.Sigmoid,
                                     bias=gxb[:, h:h + 1]).then_inc(rec_act, 1)
            act.wait_ge(rec_dve, 3)
            nc.scalar.activation(tnh, dec, ACT.Tanh).then_inc(rec_act, 1)
            act.wait_ge(rec_act, 11)
            nc.scalar.activation(dec, dec, ACT.Exp).then_inc(rec_act, 1)
            act.wait_ge(rec_dve, 4)
            nc.scalar.activation(tnh, tnh, ACT.Sqrt).then_inc(rec_act, 1)

        def r_mix_dve(v):
            n0 = START["r_in"]
            v.wait_ge(x_ready, 7)
            e, u, ln, d, z = stat[:, 176:184], stat[:, 184:192], stat[:, 192:200], stat[:, 200:208], stat[:, 208:216]
            step(v, nc.vector.tensor_scalar(d, lam, -1.0, None, ALU.mult))
            nc.vector.tensor_tensor(stat[:, 168:176], d, lam, ALU.min).then_inc(rec_dve, 1)
            v.wait_ge(rec_act, 1)
            nc.vector.tensor_scalar(u, e, 1.0, None, ALU.add).then_inc(rec_dve, 1)
            v.wait_ge(rec_dve, 2)
            step(v, nc.vector.tensor_scalar(d, u, 1.0, None, ALU.subtract))
            step(v, nc.vector.tensor_scalar(z, d, 0.0, None, ALU.is_equal))
            step(v, nc.vector.tensor_tensor(d, d, z, ALU.add))
            step(v, nc.vector.reciprocal(d, d))
            step(v, nc.vector.tensor_tensor(d, d, e, ALU.mult))
            v.wait_ge(rec_act, 2)
            step(v, nc.vector.tensor_tensor(d, d, ln, ALU.mult))
            step(v, nc.vector.tensor_tensor(z, z, e, ALU.mult))
            step(v, nc.vector.tensor_tensor(d, d, z, ALU.add))
            step(v, nc.vector.tensor_scalar(z, lam, 0.0, None, ALU.min))
            step(v, nc.vector.tensor_tensor(z, z, d, ALU.subtract))
            nc.vector.tensor_scalar(stat[:, C8:C8 + 8], z, 8.0, None, ALU.mult)
            step(v, nc.vector.memset(pad_rf, 0.0))
            for g in range(4, 8):
                if g % 2:
                    used(v, n0 + g // 2)
                else:
                    v.wait_ge(wide_done, 2 + g // 2)
                last = nc.vector.tensor_copy(pad_r[:, 2 * (g - 4):2 * (g - 4) + 2, LW - 1:],
                                             bank[g % 4][:, :].rearrange("p (a b) -> p a b", a=2))
            step(v, last)
            base = 4 * KW - 1
            for j in range(LW):
                for k in range(KD):
                    src = pad_r[:, k, j:j + T]
                    if j == 0:
                        tap = nc.vector.tensor_scalar(rec[:, k, :], src, rconvw[:, k, 0:1],
                                                      pc("rconvb")[:, k:k + 1], ALU.mult, ALU.add)
                    else:
                        v.wait_ge(tap_done, base + KD * j + k - 7)
                        tap = nc.vector.scalar_tensor_tensor(rec[:, k, :], src, rconvw[:, k, j:j + 1], rec[:, k, :],
                                                             ALU.mult, ALU.add)
                    tap.then_inc(rec_done if j == LW - 1 else tap_done, 1)
            v.wait_ge(rec_act, 10)
            for k in range(KD):
                last = nc.vector.tensor_scalar(dec[:, k, :], dec[:, k, :], stat[:, C8 + k:C8 + k + 1], None, ALU.mult)
            last.then_inc(rec_dve, 1)
            v.wait_ge(rec_done, 8)
            step(v, nc.vector.tensor_tensor(inp, inp, rec, ALU.mult))
            v.wait_ge(rec_act, 12)
            step(v, nc.vector.tensor_scalar(spare, tnh, -1.0, 1.0, ALU.mult, ALU.add))
            step(v, nc.vector.reciprocal(spare, spare))
            step(v, nc.vector.scalar_tensor_tensor(tnh, tnh, -2.0, spare, ALU.mult, ALU.mult))
            nc.vector.tensor_scalar(tnh, tnh, 1.3e-35, None, ALU.max).then_inc(rec_dve, 1)
            v.wait_ge(rec_act, 13)
            step(v, nc.vector.tensor_tensor(tnh, tnh, inp, ALU.mult))
            for k in range(KD):
                last = nc.vector.tensor_tensor_scan(rec[:, k, :], dec[:, k, :], tnh[:, k, :], 0.0, ALU.mult, ALU.add)
            step(v, last)
            nc.vector.tensor_tensor(hT[:, :, :], rec, gate_r, ALU.mult).then_inc(rec_dve, 1)
            residual_add(v, "r_out")

        block = ctx.enter_context(nc.Block())

        @block.sync
        def _(sp):
            sp.dma_start(x[:, :, :], x_in.rearrange("(t p) d -> p t d", p=P)).then_inc(x_loaded, 16)
            for s in range(RING):
                sp.dma_start(ring[:, s, :], stream[s, :, :]).then_inc(slot_in[s], 16)
            turns = N_SLOTS // RING
            with sp.Fori(1, turns) as r:
                for s in range(RING):
                    sp.wait_ge(slot_used[s], r)
                    sp.dma_start(ring[:, s, :], stream[bass.ds(r * RING + s, 1), :, :]
                                 .rearrange("a p n -> (a p) n")).then_inc(slot_in[s], 16)
            for n in range(turns * RING, N_SLOTS):
                sp.wait_ge(slot_used[n % RING], n // RING)
                sp.dma_start(ring[:, n % RING, :], stream[n, :, :]).then_inc(slot_in[n % RING], 16)
            sp.wait_ge(x_ready, 10)
            sp.dma_start(out.rearrange("(t p) d -> p t d", p=P), x[:, :, :]).then_inc(stored, 16)
            sp.wait_ge(stored, 16)

        @block.scalar
        def _(act):
            act.dma_start(con[:, :], consts).then_inc(const_in, 16)
            act.dma_start(par[:, :], params).then_inc(const_in, 16)
            act.wait_ge(const_in, 32)

            def save(p):
                if debug is not None:
                    act.wait_ge(*X_SOURCE[p])
                    act.dma_start(debug[p].rearrange("(t p) d -> p t d", p=P), x[:, :, :]).then_inc(stored, 16)
                    act.wait_ge(stored, 16 * (p + 1))

            def norm(p, q):
                save(p)
                norm_act(act, p)
                turn_evac(act, 0, f"n{q}")

            norm(0, 0)
            a_mix_act(act)
            norm(1, 1)
            moe_act(act, 0, START["moe0"])
            norm(2, 2)
            c_mix_act(act)
            norm(3, 3)
            act.dma_start(cat[:, 0, :], bass.AP(tensor=final_rows.tensor, offset=0, ap=[[0, P], [1, D]]))\
               .then_inc(final_in, 16)
            moe_act(act, 1, START["moe1"])
            save(4)
            norm_act(act, 4)
            norm(5, 4)
            ffn_act_engine(act, 0)
            norm(6, 5)
            s_mix_act(act)
            norm(7, 6)
            act.dma_start(cat[:, 0, :], bass.AP(tensor=final_rows.tensor, offset=D, ap=[[0, P], [1, D]]))\
               .then_inc(final_in, 16)
            ffn_act_engine(act, 1)
            norm(8, 7)
            ffn_act_engine(act, 2)
            norm(9, 8)
            r_mix_act(act)
            r_gates_act(act)
            norm(10, 9)
            ffn_act_engine(act, 3)
            save(11)
            norm_act(act, 11)

        @block.vector
        def _(v):
            nc.vector.memset(ones[:, :], 1.0).then_inc(scattered, 1)
            v.wait_ge(const_in, 32)
            norm_dve(v, 0, 0)
            a_mix_dve(v)
            norm_dve(v, 1, 1)
            moe_dve(v, 0, START["moe0"])
            norm_dve(v, 2, 2)
            c_mix_dve(v)
            norm_dve(v, 3, 3)
            moe_dve(v, 1, START["moe1"])
            final_norm(v, 4, 0)
            norm_dve(v, 5, 4)
            ffn_dve(v, 0, START["ffn0"])
            norm_dve(v, 6, 5)
            s_mix_dve(v)
            norm_dve(v, 7, 6)
            ffn_dve(v, 1, START["ffn1"])
            norm_dve(v, 8, 7)
            ffn_dve(v, 2, START["ffn2"])
            norm_dve(v, 9, 8)
            r_mix_dve(v)
            norm_dve(v, 10, 9)
            ffn_dve(v, 3, START["ffn3"])
            final_norm(v, 11, 1)

        @block.gpsimd
        def _(pool):
            pool.wait_ge(const_in, 32)
            for name in POWERS:
                src, dst, w = {"gmlp": (80, 104, 8), "heads": (80, 104, 24), "ln": (80, 104, 4)}.get(name, (MS, RS, 2))
                power_pool(pool, name, src, dst, w)
                if name == "n1":
                    moe_pool(pool, 0)
                if name == "n3":
                    moe_pool(pool, 1)

        @block.tensor
        def _(pe):
            pe.wait_ge(const_in, 32)
            norm_pe(pe, 0)
            a_mix_pe(pe)
            norm_pe(pe, 1)
            moe_pe(pe, 0, START["moe0"])
            norm_pe(pe, 2)
            c_mix_pe(pe)
            norm_pe(pe, 3)
            moe_pe(pe, 1, START["moe1"])
            norm_pe(pe, 4)
            ffn_pe(pe, 0, START["ffn0"])
            norm_pe(pe, 5)
            s_mix_pe(pe)
            norm_pe(pe, 6)
            ffn_pe(pe, 1, START["ffn1"])
            norm_pe(pe, 7)
            ffn_pe(pe, 2, START["ffn2"])
            norm_pe(pe, 8)
            r_mix_pe(pe)
            norm_pe(pe, 9)
            ffn_pe(pe, 3, START["ffn3"])


def rope_table(pos, width, theta):
    half = width // 2
    inv = np.power(np.float32(theta), -np.arange(half, dtype=np.float32) * np.float32(2.0 / width)).astype(np.float32)
    ang = pos.astype(np.float32)[:, None] * inv[None, :]
    cos, sin = np.cos(ang).astype(np.float32), np.sin(ang).astype(np.float32)
    return np.concatenate([cos, cos], 1), np.concatenate([-sin, sin], 1)


def constant_columns():
    pos = np.arange(T)

    def tiles(a):
        return a.reshape(NT, P, -1).transpose(1, 0, 2).reshape(P, -1)

    def table(pairs):
        cos, sin = (np.concatenate([pair[i] for pair in pairs], 1) for i in range(2))
        return np.concatenate([tiles(cos), tiles(sin)], 1)

    gap = pos[:, None] - pos[None, :]
    count = sum(((gap % d == 0) & (np.abs(gap) // d <= w // (2 * d))).astype(np.int64)
                for w, d in ((128, 1), (512, 4), (2048, 16)))
    band = np.where(count > 0, np.log(np.maximum(count, 1)), OFF).astype(np.float32)
    parts = {
        "ident": np.eye(P), "flip": np.eye(P)[::-1], "band": tiles(band),
        "ropeA": table([rope_table(pos, 16, 500000.0)]), "ropeC": table([rope_table(pos, 32, 500000.0)]),
        "ropeD": table([rope_table(pos // 64, 32, 10000.0), rope_table(pos % 64, 32, 10000.0)]),
        "iota": np.tile(np.arange(CAP), (P, 1)), "half": np.full((P, 32), -0.5),
    }
    return np.concatenate([parts[name].reshape(P, n) for name, n in CONSTS], 1).astype(np.float32)


def bucket_rows():
    dist = 255 - np.arange(SPAN)
    n = np.maximum(dist, 0)
    nf = np.maximum(n, 16).astype(np.float32)
    large = 16 + (np.log(nf / np.float32(16)) / np.float32(np.log(8.0)) * np.float32(16)).astype(np.int32)
    bucket = np.where(n < 16, n, np.minimum(large, 31))
    onehot = (bucket[None, :] == np.arange(32)[:, None]).astype(np.float32)
    window = np.where((dist >= 0) & (dist < 128), 0.0, OFF).astype(np.float32)
    return np.concatenate([onehot, np.tile(window, (8, 1))], 0)


def by_tile(v):
    return v.reshape(-1, P).T


def rows(v):
    return np.broadcast_to(v.reshape(1, -1), (P, v.size))


def param_columns(i):
    gains = [i["norm_mix"][0], i["norm_ffn"][0], i["norm_mix"][1], i["norm_ffn"][1], i["norm_ffn1_2"][0],
             i["norm_mix_2"][0], i["norm_ffn2_2"][0], i["norm_ffn1_2"][1], i["norm_mix_2"][1], i["norm_ffn2_2"][1]]
    relb = np.zeros((P, 8), np.float32)
    relb[0:32] = i["rel_bias_2"]
    parts = {
        "gains": np.concatenate([by_tile(g) for g in gains], 1),
        "router": i["moe_w_router"].reshape(2, KD, P, E).transpose(2, 0, 1, 3),
        "gmlp": rows(i["even_gmlp_norm"][0]),
        "wsT": i["even_w_spatial"][0].transpose(2, 0, 1), "bs": i["even_b_spatial"][0].T,
        "cgain": np.concatenate([by_tile(i["odd_cq_norm"][0]), by_tile(i["odd_ckv_norm"][0])], 1),
        "dgain": np.concatenate([rows(i["odd_dq_norm"][0])] * 8 + [rows(i["odd_dk_norm"][0])] * 2, 1),
        "sinks": rows(i["attn_sinks_2"][0]), "relb": relb,
        "convw": i["conv_b_w_2"][0].reshape(KW, 4, P).transpose(2, 1, 0), "convb": by_tile(i["conv_b_b_2"][0]),
        "lng": rows(i["conv_ln_g_2"][0]), "lnb": rows(i["conv_ln_b_2"][0]),
        "rconvw": i["lru_conv_w_2"][0].reshape(LW, KD, P).transpose(2, 1, 0), "rconvb": by_tile(i["lru_conv_b_2"][0]),
        "gab": by_tile(i["gate_a_b_2"][0]), "gxb": by_tile(i["gate_x_b_2"][0]), "lam": by_tile(i["lru_lambda_2"][0]),
    }
    return np.ascontiguousarray(np.concatenate([parts[name].reshape(P, n) for name, n in PARAMS], 1))


def weight_stream(i):
    s = np.zeros((N_SLOTS, P, SLOT), np.float32)

    def put(n, pieces):
        w, at = s[n].reshape(P, KD, 512), 0
        for m in pieces:
            w[:, :, at:at + m.shape[1]] = m.reshape(KD, P, -1).transpose(1, 0, 2)
            at += m.shape[1]

    def wide(name, m):
        for c in range(0, m.shape[1], 512):
            put(START[name] + c // 512, [m[:, c:c + 512]])

    def experts(name, l):
        for e in range(E):
            n = START[name] + 3 * e
            for m, w in enumerate((i["moe_w_gate"][l, e], i["moe_w_up"][l, e])):
                for half in range(2):
                    s[n + half].reshape(P, 4, 2, 512)[:, :, m] = w[512 * half:512 * half + 512].reshape(4, P, 512)\
                        .transpose(1, 0, 2)
            s[n + 2].reshape(P, 4, D)[:] = i["moe_w_down"][l, e].reshape(4, P, D).transpose(1, 0, 2)

    def ffn(name, g, u, d):
        n, c = START[name], CHUNK * P
        for k in range(5):
            put(n + 3 * k, [g[:, k * c:(k + 1) * c]])
            put(n + 3 * k + 1, [u[:, k * c:(k + 1) * c]])
            s[n + 3 * k + 2].reshape(P, CHUNK, D)[:] = d[k * c:(k + 1) * c].reshape(CHUNK, P, D).transpose(1, 0, 2)
        put(n + 15, [g[:, 5 * c:], u[:, 5 * c:]])
        s[n + 16].reshape(P, CHUNK, D)[:, 0:2] = d[5 * c:].reshape(2, P, D).transpose(1, 0, 2)

    wide("a_in", i["even_w_in"][0])
    wide("a_out", i["even_w_out"][0])
    experts("moe0", 0)
    w, n = i["odd_w_in"][0], START["c_in"]
    put(n, [w[:, 0:416]])
    put(n + 1, [w[:, 416:928]])
    put(n + 2, [w[:, 928:1184]])
    n = START["c_up"]
    s[n][:, 0:1536].reshape(P, 2, 768)[:] = i["odd_w_cq_up"][0].reshape(2, P, 768).transpose(1, 0, 2)
    s[n][:, 1536:2560] = i["odd_w_ckv_up"][0]
    wide("c_out", i["odd_w_out"][0])
    experts("moe1", 1)
    ffn("ffn0", i["ffn1_wg_2"][0], i["ffn1_wu_2"][0], i["ffn1_wd_2"][0])
    w, n = i["even_w_in_2"][0], START["s_in"]
    a, g = (lambda c: w[:, 768 + c * P:896 + c * P]), (lambda c: w[:, 1280 + c * P:1408 + c * P])
    put(n, [w[:, 0:512]])
    put(n + 1, [w[:, 512:768], a(0), g(0)])
    put(n + 2, [a(1), g(1), a(2), g(2)])
    put(n + 3, [a(3), g(3)])
    wide("s_out", i["even_w_out_2"][0])
    ffn("ffn1", i["ffn2_wg_2"][0], i["ffn2_wu_2"][0], i["ffn2_wd_2"][0])
    ffn("ffn2", i["ffn1_wg_2"][1], i["ffn1_wu_2"][1], i["ffn1_wd_2"][1])
    wide("r_in", i["odd_w_in_2"][0])
    n = START["r_gate"]
    s[n][:, 0:1024].reshape(P, KD, P)[:] = i["gate_a_w_2"][0].transpose(1, 0, 2)
    s[n][:, 1024:2048].reshape(P, KD, P)[:] = i["gate_x_w_2"][0].transpose(1, 0, 2)
    wide("r_out", i["odd_w_out_2"][0])
    ffn("ffn3", i["ffn2_wg_2"][1], i["ffn2_wu_2"][1], i["ffn2_wd_2"][1])
    return s


DEBUG = False


def kernel(**inputs):
    import concourse.bacc as bacc
    from concourse.bass_utils import run_bass_kernel_spmd as run

    i = {name: np.asarray(a) for name, a in inputs.items()}
    arrays = {
        "stream": weight_stream(i), "params": param_columns(i), "consts": constant_columns(),
        "buckets": bucket_rows(), "final_rows": np.stack([i["final_norm"], i["norm_final_2"]]),
        "x_in": np.ascontiguousarray(i["x"][0]),
    }
    nc = bacc.Bacc("TRN2", target_bir_lowering=False, num_devices=1)
    args = {name: nc.dram_tensor(name, a.shape, mybir.dt.from_np(a.dtype), kind="ExternalInput").ap()
            for name, a in arrays.items()}
    out = nc.dram_tensor("out", (T, D), F32, kind="ExternalOutput").ap()
    debug = [nc.dram_tensor(f"debug{p}", (T, D), F32, kind="ExternalOutput").ap() for p in range(12)] if DEBUG else None
    build(nc, args["stream"], args["params"], args["consts"], args["buckets"], args["final_rows"], args["x_in"], out,
          debug)
    r = run(nc, [arrays], core_ids=[0]).results[0]
    y = r["out"].reshape(1, T, D)
    return (y, *[r[f"debug{p}"].reshape(1, T, D) for p in range(12)]) if DEBUG else y
```

```python
from contextlib import ExitStack

import concourse.bass as bass
import numpy as np
from concourse import mybir

F32 = mybir.dt.float32
F32R = mybir.dt.float32r
BF16 = mybir.dt.bfloat16
ACT = mybir.ActivationFunctionType
ALU = mybir.AluOpType
AX = mybir.AxisListType

P = 128
T = 256
NT = T // P
D = 1024
KD = D // P
SLOT = 4096
RING = 6
EPS, LN_EPS = 1e-6, 1e-5
OFF = -1e30

E, CAP = 16, 32
GRP = P // CAP
FF = 2816
FT = FF // P
UNITS = 3 * FT
UNIT = SLOT // 4
SPLIT = 4
HD = 64
A_HEADS, C_HEADS, G_HEADS, S_HEADS = 12, 8, 8, 8
C_DIM = 96
KW = 31
LW = 4

STAGES = [("a_in", 6), ("a_out", 2), ("moe0", 3 * E), ("c_in", 3), ("c_up", 1), ("c_out", 2), ("moe1", 3 * E),
          ("ffn0", 17), ("s_in", 4), ("s_out", 2), ("ffn1", 17), ("ffn2", 17), ("r_in", 4), ("r_gate", 1),
          ("r_out", 2), ("ffn3", 17)]
START, N_SLOTS = {}, 0
for _name, _n in STAGES:
    START[_name] = N_SLOTS
    N_SLOTS += _n

PARAMS = [("gains", 10 * KD), ("router", 2 * KD * E), ("gmlp", 256), ("wsT", 4 * P), ("bs", 4), ("cgain", 3),
          ("dgain", 640), ("sinks", 8), ("relb", 8), ("convw", 4 * KW), ("convb", 4), ("lng", 512), ("lnb", 512),
          ("rconvw", KD * LW), ("rconvb", KD), ("gab", KD), ("gxb", KD), ("lam", KD)]
CONSTS = [("ident", P), ("flip", P), ("band", 2 * T), ("ropeA", 4 * 16), ("ropeC", 4 * 32), ("ropeD", 4 * 64),
          ("iota", CAP), ("half", 32)]


def columns(parts):
    at, out = 0, {}
    for name, n in parts:
        out[name] = (at, at + n)
        at += n
    return out, at


PCOL, NPARAM = columns(PARAMS)
CCOL, NCONST = columns(CONSTS)
SPAN = 512


def build(nc, stream, params, consts, buckets, final_rows, x_in, out, debug):
    ctx = ExitStack()
    with ctx:
        def sb(name, shape, dt=F32):
            return ctx.enter_context(nc.sbuf_tensor(name, shape, dt))

        def sem(name):
            return ctx.enter_context(nc.semaphore(name))

        ring = sb("ring", [P, RING, SLOT])
        x = sb("x", [P, NT, D])
        xn = sb("xn", [P, NT, D])
        hT_base = nc.sbuf_base
        hT = sb("hT", [P, KD, T])
        cat = sb("cat", [P, NT, D])
        par = sb("par", [P, NPARAM])
        con = sb("con", [P, NCONST])
        work_base = nc.sbuf_base
        work = sb("work", [P, 14848])
        stat = sb("stat", [P, 256])
        ones = sb("ones", [E, T])
        bank = [ctx.enter_context(nc.psum_tensor(f"bank{i}", [P, 512], F32)) for i in range(8)]
        spread = nc.dram_tensor("spread", [8, SPAN], F32)

        def pc(name):
            return par[:, PCOL[name][0]:PCOL[name][1]]

        def cc(name):
            return con[:, CCOL[name][0]:CCOL[name][1]]

        ident, flip = cc("ident"), cc("flip")
        gains = pc("gains").rearrange("p (n k) -> p n k", k=KD)
        W = work

        def region(at, shape):
            n = int(np.prod(shape))
            ap = W[:, at:at + n]
            if len(shape) == 2:
                return ap.rearrange("p (a b) -> p a b", a=shape[0])
            if len(shape) == 3:
                return ap.rearrange("p (a b c) -> p a b c", a=shape[0], b=shape[1])
            return ap

        def part(name, base, at, shape):
            return nc.alloc_sbuf_tensor_at(name, [P] + shape, F32R, offset=base + 4 * at)

        hT_hi, hT_lo = part("hT_hi", hT_base, 0, [KD, T]), part("hT_lo", work_base, 0, [KD, T])
        act_hi, act_lo = part("act_hi", work_base, 3072, [2, T]), part("act_lo", work_base, 3584, [2, T])
        unit_hi, unit_lo = part("unit_hi", work_base, 4096, [SPLIT, UNIT]), part("unit_lo", work_base, 10240, [SPLIT, UNIT])

        TMP = 14848 - 3072
        probs = region(TMP, (3, NT * T))
        probsT = region(TMP + 2048, (2, 512))

        const_in = sem("const_in")
        x_loaded = sem("x_loaded")
        slot_in = [sem(f"slot_in{i}") for i in range(RING)]
        slot_used = [sem(f"slot_used{i}") for i in range(RING)]
        x_ready = sem("x_ready")
        pow_ready = sem("pow_ready")
        sq_done = sem("sq_done")
        power_in = sem("power_in")
        power_out = sem("power_out")
        xn_done = sem("xn_done")
        turned = sem("turned")
        turn_out = [sem("turn_out_act"), sem("turn_out_dve")]
        turn_src = sem("turn_src")
        proj_done = [sem("proj0_done"), sem("proj1_done")]
        proj_free = [sem("proj0_free"), sem("proj1_free")]
        dve_step = sem("dve_step")
        gelu_done = sem("gelu_done")
        gating_in = sem("gating_in")
        gating_done = sem("gating_done")
        scores_done = sem("scores_done")
        masked_done = sem("masked_done")
        probs_done = sem("probs_done")
        probs_turned = sem("probs_turned")
        probsT_done = sem("probsT_done")
        heads_done = sem("heads_done")
        cat_done = sem("cat_done")
        route_pe, route_act, route_dve = sem("route_pe"), sem("route_act"), sem("route_dve")
        staged = sem("staged")
        expert_gu = sem("expert_gu")
        expert_silu = sem("expert_silu")
        expert_act = sem("expert_act")
        expert_turned = sem("expert_turned")
        expert_actT = sem("expert_actT")
        y_out = [sem("y_out_act"), sem("y_out_dve")]
        scattered = sem("scattered")
        scatter_added = sem("scatter_added")
        turn_hi = sem("turn_hi")
        turn_lo = sem("turn_lo")
        hi_done = sem("hi_done")
        lo_done = sem("lo_done")
        unit_used = sem("unit_used")
        ffn_product = sem("ffn_product")
        ffn_silu = sem("ffn_silu")
        ffn_act = sem("ffn_act")
        wide_done = sem("wide_done")
        wide_act, wide_dve = sem("wide_act"), sem("wide_dve")
        bucket_in = sem("bucket_in")
        spread_done = sem("spread_done")
        spread_ready = sem("spread_ready")
        spread_out = sem("spread_out")
        rows_in = sem("rows_in")
        rec_in = sem("rec_in")
        bias_done = sem("bias_done")
        bias_out = sem("bias_out")
        tap_done = sem("tap_done")
        conv_done = sem("conv_done")
        conv_turned = sem("conv_turned")
        ln_done = sem("ln_done")
        conv_cat = sem("conv_cat")
        rec_done = sem("rec_done")
        rec_gates = sem("rec_gates")
        rec_act = sem("rec_act")
        rec_dve = sem("rec_dve")
        final_in = sem("final_in")
        stored = sem("stored")

        def ge(eng, s, v):
            if v > 0:
                eng.wait_ge(s, v)

        def slot(n):
            return ring[:, n % RING, :]

        def loaded(eng, n):
            eng.wait_ge(slot_in[n % RING], 16 * (n // RING + 1))

        def used(eng, n):
            eng.wait_ge(slot_used[n % RING], n // RING + 1)

        def release(ins, n):
            ins.then_inc(slot_used[n % RING], 1)

        dve_steps = [0]

        def step(eng, ins):
            ins.then_inc(dve_step, 1)
            dve_steps[0] += 1
            eng.wait_ge(dve_step, dve_steps[0])

        NORMS = [0, 1, 2, 3, 5, 6, 7, 8, 9, 10]
        FINALS = [4, 11]

        def norm_groups(q):
            groups = []
            for b in range(4):
                pieces = [(xn[:, t, (2 * b + kk) * P:(2 * b + kk + 1) * P], kk * T + t * P, P, P)
                          for kk in range(2) for t in range(NT)]
                outs = [(hT[:, 2 * b + kk, :], (P, kk * T, T), gains[:, q, 2 * b + kk:2 * b + kk + 1])
                        for kk in range(2)]
                groups.append((pieces, outs))
            return groups

        def cat_groups():
            groups = []
            for b in range(4):
                pieces = [(cat[:, t, (2 * b + kk) * P:(2 * b + kk + 1) * P], kk * T + t * P, P, P)
                          for kk in range(2) for t in range(NT)]
                groups.append((pieces, [(hT[:, 2 * b:2 * b + 2, :].rearrange("p a b -> p (a b)"), (P, 0, 512), None)]))
            return groups

        def pair_groups(blocks):
            groups = []
            for i in range(0, len(blocks), 2):
                pieces, outs = [], []
                for kk, (src, rows, dst) in enumerate(blocks[i:i + 2]):
                    pieces += [(src(t), kk * T + t * P, rows, P) for t in range(NT)]
                    outs.append((dst, (rows, kk * T, T), None))
                groups.append((pieces, outs))
            return groups

        uA = region(0, (NT, FF))
        qkA = region(5632, (12, T))
        A_GROUPS = pair_groups([(lambda t, b=b: uA[:, t, b * P:(b + 1) * P], P, qkA[:, b, :]) for b in range(12)])

        uC = region(0, (NT, 1280))
        upq = region(2560, (NT, 768))
        upkv = region(4096, (NT, D))
        qcT = region(6144, (C_HEADS, T))
        kcT = region(8192, (C_HEADS, T))
        dT = region(10240, (6, T))
        cT = region(TMP, (3, T))
        xnf = xn[:, :, :].rearrange("p a b -> p (a b)")
        kc = xnf[:, 0:1536].rearrange("p (t h c) -> p t h c", t=NT, h=C_HEADS)
        dkk = xnf[:, 1536:2048].rearrange("p (t h c) -> p t h c", t=NT, h=4)
        cg = pc("cgain")
        C1_GROUPS = [
            ([(uC[:, t, k * P:(k + 1) * P], k * T + t * P, P, P) for k in range(2) for t in range(NT)],
             [(cT[:, k, :], (P, k * T, T), cg[:, k:k + 1]) for k in range(2)]),
            ([(uC[:, t, 256:384], t * P, P, P) for t in range(NT)], [(cT[:, 2, :], (P, 0, T), cg[:, 2:3])]),
        ]
        C2_GROUPS = pair_groups(
            [(lambda t, h=h: upq[:, t, h * C_DIM:(h + 1) * C_DIM], C_DIM, qcT[0:C_DIM, h, :]) for h in range(C_HEADS)]
            + [(lambda t, h=h: kc[:, t, h, :], C_DIM, kcT[0:C_DIM, h, :]) for h in range(C_HEADS)]
            + [(lambda t, b=b: uC[:, t, 512 + b * P:640 + b * P], P, dT[:, b, :]) for b in range(4)]
            + [(lambda t, b=b: dkk[:, t, 2 * b:2 * b + 2, :].rearrange("p a b -> p (a b)"), P, dT[:, 4 + b, :])
               for b in range(2)])

        uS = region(0, (NT, 768))
        glu = region(1536, (4, T + KW - 1))
        gluf = W[:, 1536:1536 + 4 * (T + KW - 1)]
        gate_s = region(2680, (2, T))
        qkS = region(3192, (6, T))
        bias_s = region(4728, (S_HEADS, 2 * T))
        rows_s = region(TMP - 1024, (S_HEADS, 2 * T))
        conv_s = [cat[:, c // 2, 512 + (c % 2) * T:512 + (c % 2 + 1) * T] for c in range(4)]
        onehot = W[0:32, 8824:8824 + SPAN]
        off_mask = W[0:8, 9336:9336 + SPAN]
        spread_sb = W[0:8, 9848:9848 + SPAN]
        S1_GROUPS = pair_groups([(lambda t, b=b: uS[:, t, b * P:(b + 1) * P], P, qkS[:, b, :]) for b in range(4)]
                                + [(lambda t, b=b: dkk[:, t, 2 * b:2 * b + 2, :].rearrange("p a b -> p (a b)"), P,
                                    qkS[:, 4 + b, :]) for b in range(2)])

        gate_r = region(0, (KD, T))
        pad_r = region(2048, (KD, T + LW - 1))
        pad_rf = W[:, 2048:2048 + KD * (T + LW - 1)]
        rec = region(4120, (KD, T))
        dec = region(6168, (KD, T))
        inp = region(8216, (KD, T))
        tnh = region(10264, (KD, T))
        spare = pad_rf[:, 0:2048].rearrange("p (a b) -> p a b", a=KD)

        hsel = region(0, (GRP, KD, P))
        pick = region(4096, (NT, 512))
        pickg = region(5120, (NT, 512))
        putT = region(6144, (GRP, T))
        hcur = region(7168, (KD, P))
        pcur = region(8192, (T,))
        ybuf = region(8448, (D,))
        silu_e = region(9472, (2, P))
        act_e = region(9728, (2, P))
        actT_e = region(9984, (2, P))
        aff = region(10240, (NT, E))
        scan_a = W[0:E, 10272:10272 + T]
        scan_b = W[0:E, 10528:10528 + T]
        chosen = W[0:E, 10784:10784 + T]
        placed = W[0:E, 11040:11040 + T]
        top8 = W[0:E, 11296:11304]
        posT = region(11304, (NT, E))

        silu_f = region(2048, (2, T))
        act_f = region(2560, (2, T))

        TURNS, TURN_AT = [], {}
        for name, groups in (("n0", norm_groups(0)), ("a", A_GROUPS), ("cat_a", cat_groups()), ("n1", norm_groups(1)),
                             ("n2", norm_groups(2)), ("c1", C1_GROUPS), ("c2", C2_GROUPS), ("cat_c", cat_groups()),
                             ("n3", norm_groups(3)), ("n4", norm_groups(4)), ("n5", norm_groups(5)),
                             ("s1", S1_GROUPS), ("cat_s", cat_groups()), ("n6", norm_groups(6)),
                             ("n7", norm_groups(7)), ("n8", norm_groups(8)), ("n9", norm_groups(9))):
            TURN_AT[name] = (len(TURNS), len(TURNS) + len(groups))
            TURNS += groups

        SPLIT_TURNS = ("n4", "n6", "n7", "n9")
        TURN_DONE, totals = [], {}
        for name, (first, end) in TURN_AT.items():
            for g in range(first, end):
                signal = turn_lo if name in SPLIT_TURNS else turn_out[g % 2]
                totals[signal.name] = totals.get(signal.name, 0) + 1
                TURN_DONE.append((signal, totals[signal.name]))

        def turn_pe(pe, name):
            for g in range(*TURN_AT[name]):
                if g >= 4:
                    pe.wait_ge(*TURN_DONE[g - 4])
                for src, at, rows, cols in TURNS[g][0]:
                    last = nc.tensor.transpose(bank[g % 4][0:rows, at:at + cols], src, ident)
                last.then_inc(turned, 1)

        def turn_evac(eng, which, name):
            for g in range(*TURN_AT[name]):
                if g % 2 != which:
                    continue
                eng.wait_ge(turned, g + 1)
                for dst, (rows, at, n), gain in TURNS[g][1]:
                    src = bank[g % 4][0:rows, at:at + n]
                    if which == 0:
                        last = nc.scalar.activation(dst, src, ACT.Copy, scale=1.0 if gain is None else gain)
                    elif gain is None:
                        last = nc.vector.tensor_copy(dst, src)
                    else:
                        last = nc.vector.tensor_scalar(dst, src, gain, None, ALU.mult)
                last.then_inc(turn_out[which], 1)

        def split_evac(eng, which, name, q):
            first, end = TURN_AT[name]
            for g in range(first, end):
                done = TURN_DONE[g][1]
                if which == 0:
                    eng.wait_ge(turned, g + 1)
                else:
                    eng.wait_ge(turn_hi, done)
                for kk in range(2):
                    k = 2 * (g - first) + kk
                    src, gain = bank[g % 4][:, kk * T:(kk + 1) * T], gains[:, q, k:k + 1]
                    if which == 0:
                        last = nc.scalar.activation(hT_hi[:, k, :], src, ACT.Copy, scale=gain)
                    else:
                        last = nc.vector.scalar_tensor_tensor(hT_lo[:, k, :], src, gain, hT_hi[:, k, :].bitcast(F32),
                                                              ALU.mult, ALU.subtract)
                last.then_inc(turn_lo if which else turn_hi, 1)

        def turns_out(eng, name):
            first, end = TURN_AT[name]
            for g in range(max(first, end - 2), end):
                eng.wait_ge(*TURN_DONE[g])

        PROJ, PROJ_AT = [], {}

        def plain(n, width, last=True):
            w = slot(n).rearrange("p (k n) -> p k n", k=KD)
            return (n, KD, lambda k: w[:, k, 0:width], lambda k, t: hT[:, k, t * P:(t + 1) * P], width, last)

        def up(n, tiles, first, base, stride, width, last):
            return (n, tiles, lambda k: slot(n)[:, base + k * stride:base + k * stride + width],
                    lambda k, t: cT[:, first + k, t * P:(t + 1) * P], width, last)

        def stage(name, items):
            PROJ_AT[name] = (len(PROJ), len(PROJ) + len(items))
            PROJ.extend(items)

        n = START["a_in"]
        stage("a_in", [plain(n + c, 512 if c < 5 else 256) for c in range(6)])
        stage("a_out", [plain(START["a_out"] + c, 512) for c in range(2)])
        n = START["c_in"]
        stage("c_in", [plain(n, 512), plain(n + 1, 512), plain(n + 2, 256)])
        n = START["c_up"]
        stage("c_up", [up(n, 2, 0, 0, 768, 512, False), up(n, 2, 0, 512, 768, 256, False),
                       up(n, 1, 2, 1536, 0, 512, False), up(n, 1, 2, 2048, 0, 512, True)])
        stage("c_out", [plain(START["c_out"] + c, 512) for c in range(2)])
        n = START["s_in"]
        stage("s_in", [plain(n + 2, 512), plain(n + 3, 256)])
        stage("s_out", [plain(START["s_out"] + c, 512) for c in range(2)])
        stage("r_out", [plain(START["r_out"] + c, 512) for c in range(2)])
        LAST_ADDS = {PROJ_AT[s][1] - 1 for s in ("a_out", "c_out", "s_out", "r_out")}

        def freed(m, t):
            return sum(1 for i in range(m + 1) if not (t == 1 and i in LAST_ADDS))

        def proj_pe(pe, name):
            for m in range(*PROJ_AT[name]):
                n, tiles, rhs, lhs, width, last_use = PROJ[m]
                loaded(pe, n)
                for t in range(NT):
                    if m >= 2:
                        ge(pe, proj_free[t], freed(m - 2, t))
                    for k in range(tiles):
                        mm = nc.tensor.matmul(bank[2 * t + m % 2][:, 0:width], lhs(k, t), rhs(k),
                                              start=(k == 0), stop=(k == tiles - 1))
                    if t == 1 and last_use:
                        release(mm, n)
                    else:
                        mm.then_inc(proj_done[t], 1)

        def proj_out(eng, m, t):
            if t == 1 and PROJ[m][5]:
                used(eng, PROJ[m][0])
            else:
                eng.wait_ge(proj_done[t], sum(1 for i in range(m + 1) if not (t == 1 and PROJ[i][5])))

        def proj_copy(eng, name, t, dst):
            first, end = PROJ_AT[name]
            for m in range(first, end):
                proj_out(eng, m, t)
                src = bank[2 * t + m % 2][:, 0:PROJ[m][4]]
                if t == 0:
                    nc.scalar.activation(dst(m - first), src, ACT.Copy).then_inc(proj_free[t], 1)
                else:
                    nc.vector.tensor_copy(dst(m - first), src).then_inc(proj_free[t], 1)

        def projected(eng, name):
            m = PROJ_AT[name][1] - 1
            eng.wait_ge(proj_free[0], freed(m, 0))
            eng.wait_ge(proj_free[1], freed(m, 1))

        def residual_add(v, name):
            first, end = PROJ_AT[name]
            for m in range(first, end):
                for t in range(NT):
                    proj_out(v, m, t)
                    xs = x[:, t, (m - first) * 512:(m - first + 1) * 512]
                    add = nc.vector.tensor_tensor(xs, bank[2 * t + m % 2][:, :], xs, ALU.add)
                    add.then_inc(x_ready if m == end - 1 and t == 1 else proj_free[t], 1)

        X_SOURCE = [(x_loaded, 16), (x_ready, 1), (scatter_added, 4), (x_ready, 2), (scatter_added, 8), (x_ready, 3),
                    (x_ready, 4), (x_ready, 5), (x_ready, 6), (x_ready, 7), (x_ready, 8), (x_ready, 9)]
        POWERS = {name: i for i, name in enumerate(
            ["n0", "gmlp", "n1", "n2", "heads", "n3", "f0", "n4", "n5", "ln", "n6", "n7", "n8", "n9", "f1"])}
        SS, MS, RS = 64, 66, 68

        def norm_act(act, p):
            act.wait_ge(*X_SOURCE[p])
            nc.scalar.activation(xn[:, 0, :], x[:, 0, :], ACT.Square, accum_out=stat[:, SS:SS + 1]).then_inc(sq_done, 1)

        def power_pool(pool, name, src, dst, w):
            pool.wait_ge(power_in, POWERS[name] + 1)
            nc.gpsimd.tensor_tensor(stat[:, dst:dst + w], stat[:, src:src + w], cc("half")[:, 0:w],
                                    ALU.pow).then_inc(power_out, 1)

        def norm_root(v, p, name):
            v.wait_ge(*X_SOURCE[p])
            nc.vector.tensor_tensor_reduce(xn[:, 1, :], x[:, 1, :], x[:, 1, :], 1.0, 0.0, ALU.mult, ALU.add,
                                           stat[:, SS + 1:SS + 2]).then_inc(sq_done, 1)
            v.wait_ge(sq_done, 2 * (p + 1))
            nc.vector.tensor_scalar(stat[:, MS:MS + 2], stat[:, SS:SS + 2], 1.0 / D, EPS, ALU.mult,
                                    ALU.add).then_inc(power_in, 1)
            v.wait_ge(power_out, POWERS[name] + 1)

        def norm_dve(v, p, q):
            norm_root(v, p, f"n{q}")
            for t in range(NT):
                nc.vector.tensor_scalar(xn[:, t, :], x[:, t, :], stat[:, RS + t:RS + t + 1], None,
                                        ALU.mult).then_inc(xn_done, 1)
            if f"n{q}" in SPLIT_TURNS:
                split_evac(v, 1, f"n{q}", q)
            else:
                turn_evac(v, 1, f"n{q}")

        def norm_pe(pe, q):
            pe.wait_ge(xn_done, 2 * (q + 1))
            turn_pe(pe, f"n{q}")
            turns_out(pe, f"n{q}")

        def final_norm(v, p, i):
            norm_root(v, p, f"f{i}")
            v.wait_ge(final_in, 16 * (i + 1))
            for t in range(NT):
                last = nc.vector.scalar_tensor_tensor(x[:, t, :], x[:, t, :], stat[:, RS + t:RS + t + 1],
                                                      cat[:, 0, :], ALU.mult, ALU.mult)
            last.then_inc(x_ready, 1)

        def half_rows(h):
            return slice(64 * (h % 2), 64 * (h % 2) + 64)

        band = cc("band")
        HEADS = {
            "a": [(qkA[half_rows(h), h // 2, :], qkA[half_rows(h), 6 + h // 2, :],
                   lambda s, h=h: uA[:, s, 1536 + h * HD:1536 + (h + 1) * HD], HD ** -0.5, band, None, h * HD)
                  for h in range(A_HEADS)],
            "c": [(qcT[0:C_DIM, h, :], kcT[0:C_DIM, h, :], lambda s, h=h: upkv[:, s, h * P + HD:(h + 1) * P],
                   C_DIM ** -0.5, None, None, h * HD) for h in range(C_HEADS)]
                 + [(dT[half_rows(h), h // 2, :], dT[half_rows(h), 4 + h // 4, :],
                     lambda s, h=h: uC[:, s, 1152 + (h // 4) * HD:1152 + (h // 4 + 1) * HD],
                     HD ** -0.5, None, None, 512 + h * HD) for h in range(G_HEADS)],
            "s": [(qkS[half_rows(h), h // 2, :], qkS[half_rows(h), 4 + h // 4, :],
                   lambda s, h=h: uS[:, s, 640 + (h // 4) * HD:640 + (h // 4 + 1) * HD],
                   HD ** -0.5, bias_s[:, h, :], h, h * HD) for h in range(S_HEADS)],
        }
        HEAD_AT = {"a": 0, "c": A_HEADS, "s": A_HEADS + C_HEADS + G_HEADS}
        SINK_NEG = 128

        def attend_pe(pe, name):
            g0, heads = HEAD_AT[name], HEADS[name]
            for i in range(len(heads) + 3):
                if i < len(heads):
                    g, (q, k, *_) = g0 + i, heads[i]
                    ge(pe, masked_done, g - 1)
                    for t in range(NT):
                        mm = nc.tensor.matmul(bank[4 + g % 2][:, t * T:(t + 1) * T], q[:, t * P:(t + 1) * P], k,
                                              start=True, stop=True)
                    mm.then_inc(scores_done, 1)
                if 2 <= i < len(heads) + 2:
                    g = g0 + i - 2
                    pe.wait_ge(probs_done, g + 1)
                    ge(pe, probsT_done, g - 1)
                    for s in range(NT):
                        for t in range(NT):
                            mm = nc.tensor.transpose(bank[6 + g % 2][:, s * T + t * P:s * T + (t + 1) * P],
                                                     probs[:, g % 3, t * T + s * P:t * T + (s + 1) * P], ident)
                    mm.then_inc(probs_turned, 1)
                if i >= 3:
                    g, v = g0 + i - 3, heads[i - 3][2]
                    pe.wait_ge(probsT_done, g + 1)
                    ge(pe, cat_done, g - 1)
                    for t in range(NT):
                        for s in range(NT):
                            mm = nc.tensor.matmul(bank[2 + g % 2][:, t * HD:(t + 1) * HD],
                                                  probsT[:, g % 2, s * T + t * P:s * T + (t + 1) * P], v(s),
                                                  start=(s == 0), stop=(s == NT - 1))
                    mm.then_inc(heads_done, 1)

        def attend_act(act, name):
            g0, heads = HEAD_AT[name], HEADS[name]
            for i in range(len(heads) + 2):
                if i < len(heads):
                    g, at = g0 + i, 16 * ((g0 + i) % 4)
                    act.wait_ge(masked_done, g + 1)
                    for t in range(NT):
                        row = probs[:, g % 3, t * T:(t + 1) * T]
                        last = nc.scalar.activation(row, row, ACT.Exp, bias=stat[:, at + t:at + t + 1],
                                                    accum_out=stat[:, at + 2 + t:at + 3 + t])
                    if heads[i][5] is not None:
                        last = nc.scalar.activation(stat[:, at + 6:at + 8], stat[:, at + 4:at + 6], ACT.Exp)
                    last.then_inc(probs_done, 1)
                if i >= 2:
                    g = g0 + i - 2
                    act.wait_ge(probs_turned, g + 1)
                    ge(act, heads_done, g - 1)
                    nc.scalar.activation(probsT[:, g % 2, :], bank[6 + g % 2][:, :], ACT.Copy).then_inc(probsT_done, 1)

        def attend_dve(v, name):
            g0, heads = HEAD_AT[name], HEADS[name]
            for i in range(len(heads) + 3):
                if i < len(heads):
                    scale, bias, sink = heads[i][3:6]
                    g, at = g0 + i, 16 * ((g0 + i) % 4)
                    v.wait_ge(scores_done, g + 1)
                    ge(v, probs_turned, g - 2)
                    if bias is None:
                        step(v, nc.vector.tensor_scalar(probs[:, g % 3, :], bank[4 + g % 2][:, :], scale, None,
                                                        ALU.mult))
                    else:
                        step(v, nc.vector.scalar_tensor_tensor(probs[:, g % 3, :], bank[4 + g % 2][:, :], scale,
                                                               bias, ALU.mult, ALU.add))
                    top = nc.vector.tensor_reduce(stat[:, at:at + 2],
                                                  probs[:, g % 3, :].rearrange("p (t s) -> p t s", t=NT), AX.X,
                                                  ALU.max, negate=True)
                    if sink is not None:
                        step(v, top)
                        step(v, nc.vector.tensor_scalar(stat[:, at:at + 2], stat[:, at:at + 2],
                                                        stat[:, SINK_NEG + sink:SINK_NEG + sink + 1], None, ALU.min))
                        top = nc.vector.tensor_scalar(stat[:, at + 4:at + 6], stat[:, at:at + 2],
                                                      pc("sinks")[:, sink:sink + 1], None, ALU.add)
                    top.then_inc(masked_done, 1)
                if i >= 3:
                    g, at = g0 + i - 3, 16 * ((g0 + i - 3) % 4)
                    v.wait_ge(probs_done, g + 1)
                    sums = stat[:, at + 2:at + 4]
                    if heads[i - 3][5] is not None:
                        step(v, nc.vector.tensor_tensor(sums, sums, stat[:, at + 6:at + 8], ALU.add))
                    step(v, nc.vector.reciprocal(stat[:, at + 8:at + 10], sums))
                    v.wait_ge(heads_done, g + 1)
                    col = heads[i - 3][6]
                    nc.vector.tensor_tensor(cat[:, :, col:col + HD],
                                            bank[2 + g % 2][:, 0:NT * HD].rearrange("p (t c) -> p t c", t=NT),
                                            stat[:, at + 8:at + 10].unsqueeze(2).to_broadcast([P, NT, HD]),
                                            ALU.mult).then_inc(cat_done, 1)

        def rope(v, items, half, signal=None):
            at, temps = TMP, []
            for view, cos, sin in items:
                h, r = view.shape[1], view.shape[2]
                a, b = region(at, (h, r)), region(at + h * r, (h, r))
                at += 2 * h * r
                temps.append((a, b))
                nc.vector.tensor_tensor(a, view, cos.unsqueeze(1).to_broadcast([P, h, r]), ALU.mult)
                for lo in range(0, r, 2 * half):
                    mid, hi = lo + half, lo + 2 * half
                    nc.vector.tensor_tensor(b[:, :, lo:mid], view[:, :, mid:hi],
                                            sin[:, lo:mid].unsqueeze(1).to_broadcast([P, h, half]), ALU.mult)
                    last = nc.vector.tensor_tensor(b[:, :, mid:hi], view[:, :, lo:mid],
                                                   sin[:, mid:hi].unsqueeze(1).to_broadcast([P, h, half]), ALU.mult)
            step(v, last)
            for (view, _, _), (a, b) in zip(items, temps):
                last = nc.vector.tensor_tensor(view, a, b, ALU.add)
            if signal is None:
                step(v, last)
            else:
                last.then_inc(signal, 1)

        ropeA = cc("ropeA").rearrange("p (n t c) -> p n t c", n=2, t=NT)
        gate_u = uA[:, :, 2304:2560]
        gate_v = uA[:, :, 2560:2816]

        def a_mix_dve(v):
            proj_copy(v, "a_in", 1, lambda c: uA[:, 1, c * 512:c * 512 + PROJ[PROJ_AT["a_in"][0] + c][4]])
            projected(v, "a_in")
            for t in range(NT):
                rope(v, [(uA[:, t, 0:1536].rearrange("p (h c) -> p h c", c=HD)[:, :, 0:16], ropeA[:, 0, t, :],
                          ropeA[:, 1, t, :])], 8, turn_src if t else None)
            v.wait_ge(gelu_done, 1)
            v.wait_ge(turn_src, 1)
            sq = region(TMP, (NT, 256))
            step(v, nc.vector.tensor_tensor(sq, gate_v, gate_v, ALU.mult))
            step(v, nc.vector.tensor_reduce(stat[:, 80:88].rearrange("p (t g) -> p t g", t=NT),
                                            sq.rearrange("p t (g c) -> p t g c", g=4), AX.X, ALU.add))
            nc.vector.tensor_scalar(stat[:, 80:88], stat[:, 80:88], 1.0 / HD, EPS, ALU.mult,
                                    ALU.add).then_inc(power_in, 1)
            v.wait_ge(power_out, POWERS["gmlp"] + 1)
            for t in range(NT):
                gv = gate_v[:, t, :].rearrange("p (g c) -> p g c", g=4)
                last = nc.vector.tensor_tensor(gv, gv, stat[:, 104 + 4 * t:108 + 4 * t].unsqueeze(2)
                                               .to_broadcast([P, 4, HD]), ALU.mult)
            step(v, last)
            nc.vector.tensor_tensor(gate_v, gate_v, pc("gmlp").unsqueeze(1).to_broadcast([P, NT, 256]),
                                    ALU.mult).then_inc(gating_in, 1)
            turn_evac(v, 1, "a")
            v.wait_ge(gating_done, 1)
            for g in range(4):
                mixed = bank[0][:, :].rearrange("p (t c) -> p t c", t=NT)[:, :, g * HD:(g + 1) * HD]
                last = nc.vector.scalar_tensor_tensor(cat[:, :, 768 + g * HD:768 + (g + 1) * HD], mixed,
                                                      pc("bs")[:, g:g + 1], gate_u[:, :, g * HD:(g + 1) * HD],
                                                      ALU.add, ALU.mult)
            last.then_inc(turn_src, 1)
            attend_dve(v, "a")
            turn_evac(v, 1, "cat_a")
            residual_add(v, "a_out")

        def a_mix_act(act):
            proj_copy(act, "a_in", 0, lambda c: uA[:, 0, c * 512:c * 512 + PROJ[PROJ_AT["a_in"][0] + c][4]])
            projected(act, "a_in")
            nc.scalar.activation(uA[:, :, 2304:2816], uA[:, :, 2304:2816], ACT.Gelu_apprx_tanh).then_inc(gelu_done, 1)
            turn_evac(act, 0, "a")
            attend_act(act, "a")
            turn_evac(act, 0, "cat_a")

        def a_mix_pe(pe):
            proj_pe(pe, "a_in")
            pe.wait_ge(turn_src, 1)
            turn_pe(pe, "a")
            turns_out(pe, "a")
            pe.wait_ge(gating_in, 1)
            wsT = pc("wsT").rearrange("p (g q) -> p g q", g=4)
            for t in range(NT):
                for g in range(4):
                    mm = nc.tensor.matmul(bank[0][:, t * 256 + g * HD:t * 256 + (g + 1) * HD], wsT[:, g, :],
                                          gate_v[:, t, g * HD:(g + 1) * HD], start=True, stop=True)
            mm.then_inc(gating_done, 1)
            attend_pe(pe, "a")
            pe.wait_ge(turn_src, 2)
            pe.wait_ge(cat_done, HEAD_AT["a"] + A_HEADS)
            turn_pe(pe, "cat_a")
            turns_out(pe, "cat_a")
            proj_pe(pe, "a_out")

        ropeC = cc("ropeC").rearrange("p (n t c) -> p n t c", n=2, t=NT)
        ropeD = cc("ropeD").rearrange("p (n t c) -> p n t c", n=2, t=NT)

        def c_mix_dve(v):
            proj_copy(v, "c_in", 1, lambda c: uC[:, 1, c * 512:c * 512 + PROJ[PROJ_AT["c_in"][0] + c][4]])
            projected(v, "c_in")
            sq = W[:, 6144:6144 + 2304].rearrange("p (t c) -> p t c", t=NT)
            for t in range(NT):
                last = nc.vector.tensor_tensor(sq[:, t, :], uC[:, t, 0:1152], uC[:, t, 0:1152], ALU.mult)
            step(v, last)
            nc.vector.tensor_reduce(stat[:, 80:82], sq[:, :, 0:256], AX.X, ALU.add)
            nc.vector.tensor_reduce(stat[:, 82:84], sq[:, :, 256:384], AX.X, ALU.add)
            for t in range(NT):
                last = nc.vector.tensor_reduce(stat[:, 84 + 10 * t:94 + 10 * t],
                                               sq[:, t, 512:1152].rearrange("p (h c) -> p h c", c=HD), AX.X, ALU.add)
            step(v, last)
            nc.vector.tensor_scalar(stat[:, 80:82], stat[:, 80:82], 1.0 / 256, EPS, ALU.mult, ALU.add)
            nc.vector.tensor_scalar(stat[:, 82:84], stat[:, 82:84], 1.0 / 128, EPS, ALU.mult, ALU.add)
            nc.vector.tensor_scalar(stat[:, 84:104], stat[:, 84:104], 1.0 / HD, EPS, ALU.mult,
                                    ALU.add).then_inc(power_in, 1)
            v.wait_ge(power_out, POWERS["heads"] + 1)
            for t in range(NT):
                nc.vector.tensor_scalar(uC[:, t, 0:256], uC[:, t, 0:256], stat[:, 104 + t:105 + t], None, ALU.mult)
                last = nc.vector.tensor_scalar(uC[:, t, 256:384], uC[:, t, 256:384], stat[:, 106 + t:107 + t], None,
                                               ALU.mult)
            last.then_inc(turn_src, 1)
            for t in range(NT):
                dv = uC[:, t, 512:1152].rearrange("p (h c) -> p h c", c=HD)
                last = nc.vector.tensor_tensor(dv, dv, stat[:, 108 + 10 * t:118 + 10 * t].unsqueeze(2)
                                               .to_broadcast([P, 10, HD]), ALU.mult)
            step(v, last)
            step(v, nc.vector.tensor_tensor(uC[:, :, 512:1152], uC[:, :, 512:1152],
                                            pc("dgain").unsqueeze(1).to_broadcast([P, NT, 640]), ALU.mult))
            turn_evac(v, 1, "c1")
            turns_out(v, "c1")
            proj_copy(v, "c_up", 1, lambda c: (upq[:, 1, 0:512], upq[:, 1, 512:768], upkv[:, 1, 0:512],
                                               upkv[:, 1, 512:1024])[c])
            projected(v, "c_up")
            for t in range(NT):
                rope(v, [(uC[:, t, 512:1152].rearrange("p (h c) -> p h c", c=HD), ropeD[:, 0, t, :],
                          ropeD[:, 1, t, :])], 16)
                rope(v, [(upq[:, t, :].rearrange("p (h c) -> p h c", c=C_DIM)[:, :, HD:C_DIM], ropeC[:, 0, t, :],
                          ropeC[:, 1, t, :]),
                         (uC[:, t, 384:416].unsqueeze(1), ropeC[:, 0, t, :], ropeC[:, 1, t, :])], 16)
            for t in range(NT):
                nc.vector.tensor_copy(kc[:, t, :, 0:HD], upkv[:, t, :].rearrange("p (h c) -> p h c", h=8)[:, :, 0:HD])
                nc.vector.tensor_copy(kc[:, t, :, HD:C_DIM],
                                      uC[:, t, 384:416].unsqueeze(1).to_broadcast([P, C_HEADS, C_DIM - HD]))
                for b in range(4):
                    last = nc.vector.tensor_copy(dkk[:, t, b, :], uC[:, t, 1024 + (b // 2) * HD:1088 + (b // 2) * HD])
            last.then_inc(turn_src, 1)
            turn_evac(v, 1, "c2")
            attend_dve(v, "c")
            turn_evac(v, 1, "cat_c")
            residual_add(v, "c_out")

        def c_mix_act(act):
            proj_copy(act, "c_in", 0, lambda c: uC[:, 0, c * 512:c * 512 + PROJ[PROJ_AT["c_in"][0] + c][4]])
            turn_evac(act, 0, "c1")
            proj_copy(act, "c_up", 0, lambda c: (upq[:, 0, 0:512], upq[:, 0, 512:768], upkv[:, 0, 0:512],
                                                 upkv[:, 0, 512:1024])[c])
            turn_evac(act, 0, "c2")
            attend_act(act, "c")
            turn_evac(act, 0, "cat_c")

        def c_mix_pe(pe):
            proj_pe(pe, "c_in")
            pe.wait_ge(turn_src, 3)
            turn_pe(pe, "c1")
            turns_out(pe, "c1")
            proj_pe(pe, "c_up")
            pe.wait_ge(turn_src, 4)
            turn_pe(pe, "c2")
            turns_out(pe, "c2")
            attend_pe(pe, "c")
            pe.wait_ge(cat_done, HEAD_AT["c"] + C_HEADS + G_HEADS)
            turn_pe(pe, "cat_c")
            turns_out(pe, "cat_c")
            proj_pe(pe, "c_out")

        router = pc("router").rearrange("p (l k e) -> p l k e", l=2, k=KD)
        iota = cc("iota")

        def moe_pe(pe, l, n0):
            q = 1 if l == 0 else 3
            s, a, d = 13 * l, 6 * l, 10 * l
            for t in range(NT):
                for k in range(KD):
                    mm = nc.tensor.matmul(bank[4][:, t * E:(t + 1) * E], hT[:, k, t * P:(t + 1) * P],
                                          router[:, l, k, :], start=(k == 0), stop=(k == KD - 1))
            mm.then_inc(route_pe, 1)
            pe.wait_ge(route_dve, d + 2)
            for t in range(NT):
                mm = nc.tensor.transpose(bank[5][0:E, t * P:(t + 1) * P], aff[:, t, :], ident)
            mm.then_inc(route_pe, 1)
            pe.wait_ge(route_dve, d + 3)
            for t in range(NT):
                mm = nc.tensor.transpose(bank[4][:, t * E:(t + 1) * E], placed[:, t * P:(t + 1) * P], ident[0:E, 0:E])
            mm.then_inc(route_pe, 1)
            pe.wait_ge(route_dve, d + 4)
            for k in range(KD):
                if k >= 4:
                    pe.wait_ge(*((route_act, a + 2 + (k - 4) // 2) if k % 2 == 0 else (route_dve, d + 6 + (k - 4) // 2)))
                for t in range(NT):
                    mm = nc.tensor.matmul(bank[k % 4][:, :], xn[:, t, k * P:(k + 1) * P], pick[:, t, :],
                                          start=(t == 0), stop=(t == NT - 1))
                mm.then_inc(route_pe, 1)
            pe.wait_ge(route_dve, d + 5)
            for b in range(2):
                for gg in range(2):
                    for t in range(NT):
                        mm = nc.tensor.transpose(bank[6 + b][:, gg * T + t * P:gg * T + (t + 1) * P],
                                                 pickg[:, t, (2 * b + gg) * P:(2 * b + gg + 1) * P], ident)
                mm.then_inc(route_pe, 1)
            pe.wait_ge(route_act, a + 6)
            pe.wait_ge(route_dve, d + 10)
            with pe.Fori(0, E // GRP) as g:
                seen = 4 * l + g
                pe.wait_ge(staged, seen + 1)
                for e in range(GRP):
                    na, nb, nd = n0 + 3 * e, n0 + 3 * e + 1, n0 + 3 * e + 2
                    for half, n in enumerate((na, nb)):
                        pe.wait_ge(slot_in[n % RING], 16 * (n // RING + 1) + 32 * g)
                        w = slot(n).rearrange("p (k m c) -> p k m c", k=4, m=2)
                        for kk in range(4):
                            for j in range(4):
                                mm = nc.tensor.matmul(bank[4 + e % 2][32 * j:32 * j + 32, 0:256],
                                                      hcur[:, 4 * half + kk, e * CAP:(e + 1) * CAP],
                                                      w[:, kk, :, j * P:(j + 1) * P],
                                                      start=(half == 0 and kk == 0), stop=(half == 1 and kk == 3),
                                                      skip_group_check=True)
                        if half == 0:
                            release(mm, na)
                        else:
                            mm.then_inc(expert_gu, 1)
                    pe.wait_ge(expert_act, 4 * seen + e + 1)
                    nc.tensor.transpose(bank[6][:, 0:P], act_e[:, e % 2, :], ident).then_inc(expert_turned, 1)
                    pe.wait_ge(expert_actT, 4 * seen + e + 1)
                    pe.wait_ge(slot_in[nd % RING], 16 * (nd // RING + 1) + 32 * g)
                    if e >= 1:
                        pe.wait_ge(y_out[0], 4 * seen + e)
                        pe.wait_ge(y_out[1], 4 * seen + e)
                    w = slot(nd).rearrange("p (j c) -> p j c", j=4)
                    for j in range(4):
                        for i in range(4):
                            mm = nc.tensor.matmul(bank[7][32 * i:32 * i + 32, 0:256],
                                                  actT_e[:, e % 2, j * CAP:(j + 1) * CAP],
                                                  w[:, j, i * 256:(i + 1) * 256], start=(j == 0), stop=(j == 3),
                                                  skip_group_check=True)
                            if j == 0 and i == 0:
                                release(mm, nb)
                    release(mm, nd)
                pe.wait_ge(y_out[0], 4 * seen + 4)
                pe.wait_ge(y_out[1], 4 * seen + 4)
                for t in range(NT):
                    for half in range(2):
                        mm = nc.tensor.matmul(bank[2 * t + half][:, :], pcur[:, t * P:(t + 1) * P],
                                              ybuf[:, half * 512:(half + 1) * 512], start=True, stop=True)
                mm.then_inc(scattered, 1)

        def moe_act(act, l, n0):
            q = 1 if l == 0 else 3
            s, d = 13 * l, 10 * l
            act.wait_ge(route_dve, d + 1)
            for t in range(NT):
                last = nc.scalar.activation(aff[:, t, :], bank[4][:, t * E:(t + 1) * E], ACT.Exp,
                                            bias=stat[:, 72 + t:73 + t], accum_out=stat[:, 74 + t:75 + t])
            last.then_inc(route_act, 1)
            for k in range(0, KD, 2):
                act.wait_ge(route_pe, s + 4 + k)
                nc.scalar.activation(hsel[:, :, k, :], bank[k % 4][:, :].rearrange("p (g c) -> p g c", g=GRP),
                                     ACT.Copy, scale=gains[:, q, k:k + 1]).then_inc(route_act, 1)
            act.wait_ge(route_pe, s + 12)
            nc.scalar.activation(putT[:, 0:2, :].rearrange("p a b -> p (a b)"), bank[6][:, :],
                                 ACT.Copy).then_inc(route_act, 1)
            with act.Fori(0, E // GRP) as g:
                seen = 4 * l + g
                for e in range(GRP):
                    nd = n0 + 3 * e + 2
                    act.wait_ge(expert_gu, 4 * seen + e + 1)
                    nc.scalar.activation(silu_e[:, e % 2, :], bank[4 + e % 2][:, 0:P], ACT.Silu).then_inc(expert_silu, 1)
                    if e == 0:
                        act.wait_ge(scattered, seen + 1)
                    act.wait_ge(slot_used[nd % RING], nd // RING + 1 + 2 * g)
                    for i in range(2):
                        last = nc.scalar.activation(ybuf[32 * e:32 * e + 32, i * 256:(i + 1) * 256],
                                                    bank[7][32 * i:32 * i + 32, 0:256], ACT.Copy)
                    last.then_inc(y_out[0], 1)

        def moe_dve(v, l, n0):
            q = 1 if l == 0 else 3
            s, a = 13 * l, 6 * l
            v.wait_ge(route_pe, s + 1)
            nc.vector.tensor_reduce(stat[:, 72:74], bank[4][:, 0:NT * E].rearrange("p (t e) -> p t e", t=NT), AX.X,
                                    ALU.max, negate=True).then_inc(route_dve, 1)
            v.wait_ge(route_act, a + 1)
            step(v, nc.vector.reciprocal(stat[:, 76:78], stat[:, 74:76]))
            nc.vector.tensor_tensor(aff, aff, stat[:, 76:78].unsqueeze(2).to_broadcast([P, NT, E]),
                                    ALU.mult).then_inc(route_dve, 1)
            v.wait_ge(route_pe, s + 2)
            step(v, nc.vector.tensor_copy(scan_a, bank[5][0:E, 0:T]))
            src, dst = scan_a, scan_b
            for _ in range(CAP // 8):
                step(v, nc.vector.max(top8, src))
                step(v, nc.vector.match_replace(dst, top8, src, -1.0))
                src, dst = dst, src
            step(v, nc.vector.tensor_scalar(chosen, src, -1.0, None, ALU.is_equal))
            step(v, nc.vector.tensor_tensor_scan(dst, ones[:, :], chosen, 0.0, ALU.mult, ALU.add))
            step(v, nc.vector.tensor_tensor(placed, dst, chosen, ALU.mult))
            nc.vector.tensor_scalar(placed, placed, -1.0, None, ALU.add).then_inc(route_dve, 1)
            v.wait_ge(route_pe, s + 3)
            step(v, nc.vector.tensor_copy(posT.rearrange("p t e -> p (t e)"), bank[4][:, 0:NT * E]))
            for t in range(NT):
                last = nc.vector.tensor_tensor(pick[:, t, :].rearrange("p (e c) -> p e c", e=E),
                                               iota.unsqueeze(1).to_broadcast([P, E, CAP]),
                                               posT[:, t, :].unsqueeze(2).to_broadcast([P, E, CAP]), ALU.is_equal)
            last.then_inc(route_dve, 1)
            v.wait_ge(route_dve, 10 * l + 4)
            for t in range(NT):
                last = nc.vector.tensor_tensor(pickg[:, t, :].rearrange("p (e c) -> p e c", e=E),
                                               pick[:, t, :].rearrange("p (e c) -> p e c", e=E),
                                               aff[:, t, :].unsqueeze(2).to_broadcast([P, E, CAP]), ALU.mult)
            last.then_inc(route_dve, 1)
            for k in range(1, KD, 2):
                v.wait_ge(route_pe, s + 4 + k)
                nc.vector.tensor_scalar(hsel[:, :, k, :], bank[k % 4][:, :].rearrange("p (g c) -> p g c", g=GRP),
                                        gains[:, q, k:k + 1], None, ALU.mult).then_inc(route_dve, 1)
            v.wait_ge(route_pe, s + 13)
            nc.vector.tensor_copy(putT[:, 2:4, :].rearrange("p a b -> p (a b)"),
                                  bank[7][:, :]).then_inc(route_dve, 1)
            with v.Fori(0, E // GRP) as g:
                seen = 4 * l + g
                for e in range(GRP):
                    nd = n0 + 3 * e + 2
                    v.wait_ge(expert_silu, 4 * seen + e + 1)
                    nc.vector.tensor_tensor(act_e[:, e % 2, :], silu_e[:, e % 2, :], bank[4 + e % 2][:, P:2 * P],
                                            ALU.mult).then_inc(expert_act, 1)
                    v.wait_ge(expert_turned, 4 * seen + e + 1)
                    nc.vector.tensor_copy(actT_e[:, e % 2, :], bank[6][:, 0:P]).then_inc(expert_actT, 1)
                    if e == 0:
                        v.wait_ge(scattered, seen + 1)
                    v.wait_ge(slot_used[nd % RING], nd // RING + 1 + 2 * g)
                    for i in range(2, 4):
                        last = nc.vector.tensor_copy(ybuf[32 * e:32 * e + 32, i * 256:(i + 1) * 256],
                                                     bank[7][32 * i:32 * i + 32, 0:256])
                    last.then_inc(y_out[1], 1)
                v.wait_ge(scattered, seen + 2)
                for t in range(NT):
                    for half in range(2):
                        xs = x[:, t, half * 512:(half + 1) * 512]
                        last = nc.vector.tensor_tensor(xs, bank[2 * t + half][:, :], xs, ALU.add)
                last.then_inc(scatter_added, 1)

        def moe_pool(pool, l):
            pool.wait_ge(route_act, 6 * l + 6)
            pool.wait_ge(route_dve, 10 * l + 10)
            with pool.Fori(0, E // GRP) as g:
                pool.wait_ge(scattered, 4 * l + g + 1)
                nc.gpsimd.tensor_copy(hcur.rearrange("p k c -> p (k c)"), W[:, bass.ds(g * (KD * P), KD * P)])
                nc.gpsimd.tensor_copy(pcur, W[:, bass.ds(g * T + 6144, T)]).then_inc(staged, 1)

        def gate_unit(f):
            return max(3 * f - 1, 0)

        def up_unit(f):
            return max(3 * f, 1)

        def down_unit(f):
            return min(3 * f + 4, UNITS - 1)

        def slot_end(u):
            return u % 4 == 3 or u == UNITS - 1

        def low_count(u):
            return sum(1 for i in range(u + 1) if not slot_end(i))

        PASS = 8
        PASS_UNITS = 3 * PASS

        def raw_unit(n0, u):
            return slot(n0 + u // 4)[:, (u % 4) * UNIT:(u % 4 + 1) * UNIT]

        def split_high(act, i, n0, u, it=0):
            n = n0 + u // 4
            if u % 4 == 0:
                act.wait_ge(slot_in[n % RING], 16 * (n // RING + 1) + 16 * it)
            if u >= SPLIT:
                act.wait_ge(unit_used, UNITS * i + u - SPLIT + 1 + PASS_UNITS * it)
            nc.scalar.activation(unit_hi[:, u % SPLIT, :], raw_unit(n0, u), ACT.Copy).then_inc(hi_done, 1)

        def split_low(v, i, n0, u, it=0):
            n = n0 + u // 4
            v.wait_ge(hi_done, UNITS * i + u + 1 + PASS_UNITS * it)
            low = nc.vector.tensor_tensor(unit_lo[:, u % SPLIT, :], raw_unit(n0, u), unit_hi[:, u % SPLIT, :].bitcast(F32),
                                          ALU.subtract)
            low.then_inc(slot_used[n % RING] if slot_end(u) else lo_done, 1)

        def high_ready(pe, i, u, it):
            pe.wait_ge(hi_done, UNITS * i + u + 1 + PASS_UNITS * it)

        def low_ready(pe, i, n0, u, it):
            n = n0 + u // 4
            if slot_end(u):
                pe.wait_ge(slot_used[n % RING], n // RING + 1 + it)
            else:
                pe.wait_ge(lo_done, low_count(UNITS - 1) * i + low_count(u) + 18 * it)

        def ffn_pe(pe, i, n0):
            base = FT * i

            def hidden(f, u, at, it):
                out = bank[4 + f % 4][:, at:at + T]
                high = unit_hi[:, u % SPLIT, :].rearrange("p (k c) -> p k c", k=KD)
                low = unit_lo[:, u % SPLIT, :].rearrange("p (k c) -> p k c", k=KD)
                high_ready(pe, i, u, it)
                for k in range(KD):
                    nc.tensor.matmul(out, high[:, k, :], hT_hi[:, k, :], start=(k == 0), stop=False)
                    nc.tensor.matmul(out, high[:, k, :], hT_lo[:, k, :], start=False, stop=False)
                low_ready(pe, i, n0, u, it)
                for k in range(KD):
                    mm = nc.tensor.matmul(out, low[:, k, :], hT_hi[:, k, :], start=False, stop=(k == KD - 1))
                mm.then_inc(unit_used, 1)

            def gate_up(f, it=0):
                if f >= 4:
                    pe.wait_ge(ffn_act, base + f - 3 + PASS * it)
                hidden(f, gate_unit(f), 0, it)
                hidden(f, up_unit(f), T, it)

            def down(f, it=0):
                u = down_unit(f)
                high_ready(pe, i, u, it)
                pe.wait_ge(ffn_act, base + f + 1 + PASS * it)
                for j in range(4):
                    t, half = j // 2, j % 2
                    for left in (act_hi, act_lo):
                        nc.tensor.matmul(bank[j][:, :], left[:, f % 2, t * P:(t + 1) * P],
                                         unit_hi[:, u % SPLIT, half * 512:(half + 1) * 512],
                                         start=(f == 0 and left is act_hi), stop=False, skip_group_check=True)
                low_ready(pe, i, n0, u, it)
                for j in range(4):
                    t, half = j // 2, j % 2
                    mm = nc.tensor.matmul(bank[j][:, :], act_hi[:, f % 2, t * P:(t + 1) * P],
                                          unit_lo[:, u % SPLIT, half * 512:(half + 1) * 512], start=False,
                                          stop=(f == FT - 1), skip_group_check=True)
                mm.then_inc(unit_used, 1)

            gate_up(0)
            gate_up(1)
            down(0)
            with pe.Fori(0, 2) as it:
                for f in range(2, 2 + PASS):
                    gate_up(f, it)
                    down(f - 1, it)
            for f in range(2 + 2 * PASS, FT):
                gate_up(f)
                down(f - 1)
            down(FT - 1)

        def ffn_act_engine(act, i, n0):
            base = FT * i

            def tile(f, it=0):
                if f + 1 < FT:
                    split_high(act, i, n0, gate_unit(f + 1), it)
                    split_high(act, i, n0, up_unit(f + 1), it)
                split_high(act, i, n0, down_unit(f), it)
                act.wait_ge(unit_used, UNITS * i + up_unit(f) + 1 + PASS_UNITS * it)
                if f >= 2:
                    act.wait_ge(ffn_act, base + f - 1 + PASS * it)
                nc.scalar.activation(silu_f[:, f % 2, :], bank[4 + f % 4][:, 0:T], ACT.Silu).then_inc(ffn_silu, 1)

            split_high(act, i, n0, 0)
            split_high(act, i, n0, 1)
            tile(0)
            tile(1)
            with act.Fori(0, 2) as it:
                for f in range(2, 2 + PASS):
                    tile(f, it)
            for f in range(2 + 2 * PASS, FT):
                tile(f)

        def ffn_dve(v, i, n0):
            base = FT * i

            def tile(f, it=0):
                if f + 1 < FT:
                    split_low(v, i, n0, gate_unit(f + 1), it)
                    split_low(v, i, n0, up_unit(f + 1), it)
                split_low(v, i, n0, down_unit(f), it)
                v.wait_ge(ffn_silu, base + f + 1 + PASS * it)
                if f >= 2:
                    v.wait_ge(unit_used, UNITS * i + down_unit(f - 2) + 1 + PASS_UNITS * it)
                up = bank[4 + f % 4][:, T:2 * T]
                nc.vector.tensor_tensor(act_f[:, f % 2, :], silu_f[:, f % 2, :], up, ALU.mult).then_inc(ffn_product, 1)
                nc.vector.tensor_tensor(act_hi[:, f % 2, :], silu_f[:, f % 2, :], up, ALU.mult).then_inc(ffn_product, 1)
                v.wait_ge(ffn_product, 2 * (base + f + 1) + 2 * PASS * it)
                nc.vector.tensor_tensor(act_lo[:, f % 2, :], act_f[:, f % 2, :], act_hi[:, f % 2, :].bitcast(F32),
                                        ALU.subtract).then_inc(ffn_act, 1)

            split_low(v, i, n0, 0)
            split_low(v, i, n0, 1)
            tile(0)
            tile(1)
            with v.Fori(0, 2) as it:
                for f in range(2, 2 + PASS):
                    tile(f, it)
            for f in range(2 + 2 * PASS, FT):
                tile(f)
            v.wait_ge(unit_used, UNITS * (i + 1))
            for j in range(4):
                t, half = j // 2, j % 2
                xs = x[:, t, half * 512:(half + 1) * 512]
                last = nc.vector.scalar_tensor_tensor(xs, bank[j][:, :], 0.5, xs, ALU.mult, ALU.add)
            last.then_inc(x_ready, 1)

        TAPS = [(j, 2 * pair + c) for pair in range(2) for j in range(KW) for c in range(2)]

        def s_mix_pe(pe):
            n0 = START["s_in"]
            pe.wait_ge(bucket_in, 32)
            nc.tensor.matmul(bank[0][0:8, :], pc("relb")[0:32, :], onehot, start=True, stop=True).then_inc(spread_done, 1)
            places = [(n0, 0, P), (n0, 2 * P, 3 * P), (n0 + 1, 0, P), (n0 + 1, 2 * P, 3 * P)]
            for c, (n, av, ag) in enumerate(places):
                if c % 2 == 0:
                    loaded(pe, n)
                w = slot(n).rearrange("p (k c) -> p k c", k=KD)
                for at, col in ((0, av), (T, ag)):
                    for k in range(KD):
                        mm = nc.tensor.matmul(bank[4 + c][:, at:at + T], w[:, k, col:col + P], hT[:, k, :],
                                              start=(k == 0), stop=(k == KD - 1))
                if c % 2 == 0:
                    mm.then_inc(wide_done, 1)
                else:
                    release(mm, n)
            pe.wait_ge(spread_ready, 1)
            proj_pe(pe, "s_in")
            pe.wait_ge(rows_in, 32)
            pe.wait_ge(wide_act, 4)
            pe.wait_ge(wide_dve, 4)
            for h in range(S_HEADS):
                ge(pe, bias_out, h - 3)
                nc.tensor.matmul(bank[4 + h % 4][:, :], flip, rows_s[:, h, :], start=True,
                                 stop=True).then_inc(bias_done, 1)
            pe.wait_ge(turn_src, 5)
            turn_pe(pe, "s1")
            turns_out(pe, "s1")
            pe.wait_ge(bias_out, S_HEADS)
            attend_pe(pe, "s")
            pe.wait_ge(conv_done, 1)
            for t in range(NT):
                for c in range(4):
                    mm = nc.tensor.transpose(bank[t][:, c * P:(c + 1) * P], conv_s[c][:, t * P:(t + 1) * P], ident)
            mm.then_inc(conv_turned, 1)
            pe.wait_ge(conv_cat, 1)
            pe.wait_ge(cat_done, HEAD_AT["s"] + S_HEADS)
            turn_pe(pe, "cat_s")
            turns_out(pe, "cat_s")
            proj_pe(pe, "s_out")

        def s_mix_act(act):
            n0 = START["s_in"]
            act.wait_ge(spread_ready, 1)
            act.dma_start(spread.ap(), spread_sb).then_inc(spread_out, 16)
            act.wait_ge(spread_out, 16)
            for t in range(NT):
                src = bass.AP(tensor=spread, offset=P - P * t, ap=[[1, P], [SPAN, S_HEADS], [1, T]])
                act.dma_start(rows_s[:, :, t * T:(t + 1) * T], src).then_inc(rows_in, 16)
            for c in range(4):
                if c % 2 == 0:
                    act.wait_ge(wide_done, 1 + c // 2)
                else:
                    used(act, n0 + c // 2)
                ge(act, wide_dve, c - 1)
                nc.scalar.activation(gate_s[:, c % 2, :], bank[4 + c][:, T:2 * T], ACT.Sigmoid).then_inc(wide_act, 1)
            proj_copy(act, "s_in", 0, lambda c: (uS[:, 0, 0:512], uS[:, 0, 512:768])[c])
            for h in range(S_HEADS):
                act.wait_ge(bias_done, h + 1)
                nc.scalar.activation(bias_s[:, h, :], bank[4 + h % 4][:, :], ACT.Copy).then_inc(bias_out, 1)
            turn_evac(act, 0, "s1")
            attend_act(act, "s")
            act.wait_ge(ln_done, 1)
            nc.scalar.activation(cat[:, :, 512:1024], cat[:, :, 512:1024], ACT.Silu).then_inc(conv_cat, 1)
            turn_evac(act, 0, "cat_s")

        def s_mix_dve(v):
            v.wait_ge(x_ready, 4)
            step(v, nc.vector.tensor_scalar(stat[:, SINK_NEG:SINK_NEG + 8], pc("sinks"), -1.0, None, ALU.mult))
            nc.vector.memset(gluf, 0.0)
            v.wait_ge(spread_done, 1)
            v.wait_ge(bucket_in, 32)
            nc.vector.tensor_tensor(spread_sb, bank[0][0:8, :], off_mask, ALU.add).then_inc(spread_ready, 1)

            def gated(c):
                v.wait_ge(wide_act, c + 1)
                nc.vector.tensor_tensor(glu[:, c, KW - 1:], gate_s[:, c % 2, :], bank[4 + c][:, 0:T],
                                        ALU.mult).then_inc(wide_dve, 1)

            convw = pc("convw").rearrange("p (c j) -> p c j", c=4)

            def taps(first, end):
                for i in range(first, end):
                    j, c = TAPS[i]
                    g = glu[:, c, j:j + T]
                    if j == 0:
                        v.wait_ge(wide_dve, c + 1)
                        tap = nc.vector.tensor_scalar(conv_s[c], g, convw[:, c, 0:1], pc("convb")[:, c:c + 1],
                                                      ALU.mult, ALU.add)
                    else:
                        v.wait_ge(tap_done, i - 1)
                        tap = nc.vector.scalar_tensor_tensor(conv_s[c], g, convw[:, c, j:j + 1], conv_s[c],
                                                             ALU.mult, ALU.add)
                    tap.then_inc(conv_done if i == 4 * KW - 1 else tap_done, 1)

            gated(0)
            gated(1)
            taps(0, 28)
            gated(2)
            gated(3)
            taps(28, 84)
            proj_copy(v, "s_in", 1, lambda c: (uS[:, 1, 0:512], uS[:, 1, 512:768])[c])
            projected(v, "s_in")
            for t in range(NT):
                for b in range(4):
                    last = nc.vector.tensor_copy(dkk[:, t, b, :], uS[:, t, 512 + (b // 2) * HD:576 + (b // 2) * HD])
            last.then_inc(turn_src, 1)
            taps(84, 104)
            turn_evac(v, 1, "s1")
            attend_dve(v, "s")
            taps(104, 4 * KW)
            v.wait_ge(conv_turned, 1)
            for t in range(NT):
                last = nc.vector.bn_stats(stat[:, 136 + 6 * t:142 + 6 * t], bank[t][:, :])
            step(v, last)
            for t in range(NT):
                last = nc.vector.bn_aggr(stat[:, 148 + 2 * t:150 + 2 * t], stat[:, 136 + 6 * t:142 + 6 * t])
            step(v, last)
            nc.vector.tensor_scalar(stat[:, 80:84], stat[:, 148:152], LN_EPS, None, ALU.add).then_inc(power_in, 1)
            v.wait_ge(power_out, POWERS["ln"] + 1)
            ct = cat[:, :, 512:1024]
            for t in range(NT):
                last = nc.vector.tensor_scalar(ct[:, t, :], bank[t][:, :], stat[:, 148 + 2 * t:149 + 2 * t],
                                               stat[:, 105 + 2 * t:106 + 2 * t], ALU.subtract, ALU.mult)
            step(v, last)
            step(v, nc.vector.tensor_tensor(ct, ct, pc("lng").unsqueeze(1).to_broadcast([P, NT, 512]), ALU.mult))
            nc.vector.tensor_tensor(ct, ct, pc("lnb").unsqueeze(1).to_broadcast([P, NT, 512]), ALU.add)\
                .then_inc(ln_done, 1)
            turn_evac(v, 1, "cat_s")
            residual_add(v, "s_out")

        gab, gxb, lam = pc("gab"), pc("gxb"), pc("lam")
        rconvw = pc("rconvw").rearrange("p (k j) -> p k j", k=KD)
        C8 = 160

        def r_mix_pe(pe):
            n0 = START["r_in"]
            def halves(g):
                n = n0 + g // 2
                if g % 2 == 0:
                    loaded(pe, n)
                if g >= 4:
                    pe.wait_ge(rec_in, g - 3)
                w = slot(n).rearrange("p (k c) -> p k c", k=KD)
                for i in range(2):
                    col = (g % 2) * 256 + i * P
                    for k in range(KD):
                        mm = nc.tensor.matmul(bank[g % 4][:, i * T:(i + 1) * T], w[:, k, col:col + P], hT[:, k, :],
                                              start=(k == 0), stop=(k == KD - 1))
                if g % 2:
                    release(mm, n)
                else:
                    mm.then_inc(wide_done, 1)

            for g in range(6):
                halves(g)
            n = START["r_gate"]
            loaded(pe, n)
            for h in range(KD):
                pe.wait_ge(rec_done, h + 1)
                if h >= 4:
                    pe.wait_ge(rec_act, h - 1)
                for m in range(2):
                    mm = nc.tensor.matmul(bank[4 + h % 4][:, m * T:(m + 1) * T],
                                          slot(n)[:, (m * KD + h) * P:(m * KD + h + 1) * P], rec[:, h, :],
                                          start=True, stop=True)
                if h == KD - 1:
                    release(mm, n)
                else:
                    mm.then_inc(rec_gates, 1)
            for g in range(6, 8):
                halves(g)
            pe.wait_ge(rec_dve, 5)
            proj_pe(pe, "r_out")

        def r_mix_act(act):
            n0 = START["r_in"]
            act.wait_ge(rec_dve, 1)
            nc.scalar.activation(stat[:, 176:184], stat[:, 168:176], ACT.Exp).then_inc(rec_act, 1)
            act.wait_ge(rec_dve, 2)
            nc.scalar.activation(stat[:, 192:200], stat[:, 184:192], ACT.Ln).then_inc(rec_act, 1)

            for g in range(2):
                r_gelu_act(act, g)

        def r_gelu_act(act, g):
            if g % 2:
                used(act, START["r_in"] + 2 + g // 2)
            else:
                act.wait_ge(wide_done, 5 + g // 2)
            nc.scalar.activation(gate_r[:, 2 * g:2 * g + 2, :].rearrange("p a b -> p (a b)"), bank[g][:, :],
                                 ACT.Gelu_apprx_tanh).then_inc(wide_act, 1)

        def r_gates_act(act):
            for h in range(KD):
                if h == KD - 1:
                    used(act, START["r_gate"])
                else:
                    act.wait_ge(rec_gates, h + 1)
                nc.scalar.activation(dec[:, h, :], bank[4 + h % 4][:, 0:T], ACT.Sigmoid, bias=gab[:, h:h + 1])
                nc.scalar.activation(inp[:, h, :], bank[4 + h % 4][:, T:2 * T], ACT.Sigmoid,
                                     bias=gxb[:, h:h + 1]).then_inc(rec_act, 1)
            act.wait_ge(rec_dve, 3)
            nc.scalar.activation(tnh, dec, ACT.Tanh).then_inc(rec_act, 1)
            act.wait_ge(rec_act, 11)
            nc.scalar.activation(dec, dec, ACT.Exp).then_inc(rec_act, 1)
            act.wait_ge(rec_dve, 4)
            nc.scalar.activation(tnh, tnh, ACT.Sqrt).then_inc(rec_act, 1)
            for g in range(2, 4):
                r_gelu_act(act, g)

        def r_mix_dve(v):
            n0 = START["r_in"]
            v.wait_ge(x_ready, 7)
            e, u, ln, d, z = stat[:, 176:184], stat[:, 184:192], stat[:, 192:200], stat[:, 200:208], stat[:, 208:216]
            step(v, nc.vector.tensor_scalar(d, lam, -1.0, None, ALU.mult))
            nc.vector.tensor_tensor(stat[:, 168:176], d, lam, ALU.min).then_inc(rec_dve, 1)
            v.wait_ge(rec_act, 1)
            nc.vector.tensor_scalar(u, e, 1.0, None, ALU.add).then_inc(rec_dve, 1)
            v.wait_ge(rec_dve, 2)
            step(v, nc.vector.tensor_scalar(d, u, 1.0, None, ALU.subtract))
            step(v, nc.vector.tensor_scalar(z, d, 0.0, None, ALU.is_equal))
            step(v, nc.vector.tensor_tensor(d, d, z, ALU.add))
            step(v, nc.vector.reciprocal(d, d))
            step(v, nc.vector.tensor_tensor(d, d, e, ALU.mult))
            v.wait_ge(rec_act, 2)
            step(v, nc.vector.tensor_tensor(d, d, ln, ALU.mult))
            step(v, nc.vector.tensor_tensor(z, z, e, ALU.mult))
            step(v, nc.vector.tensor_tensor(d, d, z, ALU.add))
            step(v, nc.vector.tensor_scalar(z, lam, 0.0, None, ALU.min))
            step(v, nc.vector.tensor_tensor(z, z, d, ALU.subtract))
            nc.vector.tensor_scalar(stat[:, C8:C8 + 8], z, 8.0, None, ALU.mult)
            step(v, nc.vector.memset(pad_rf, 0.0))
            base = 4 * KW - 1
            for g in range(4):
                if g % 2:
                    used(v, n0 + g // 2)
                else:
                    v.wait_ge(wide_done, 3 + g // 2)
                nc.vector.tensor_copy(pad_r[:, 2 * g:2 * g + 2, LW - 1:],
                                      bank[g][:, :].rearrange("p (a b) -> p a b", a=2)).then_inc(rec_in, 1)
                v.wait_ge(rec_in, g + 1)
                for i in range(2 * LW):
                    j, k = i // 2, 2 * g + i % 2
                    src = pad_r[:, k, j:j + T]
                    if j == 0:
                        tap = nc.vector.tensor_scalar(rec[:, k, :], src, rconvw[:, k, 0:1],
                                                      pc("rconvb")[:, k:k + 1], ALU.mult, ALU.add)
                    else:
                        v.wait_ge(tap_done, base + 2 * (LW - 1) * g + i - 1)
                        tap = nc.vector.scalar_tensor_tensor(rec[:, k, :], src, rconvw[:, k, j:j + 1], rec[:, k, :],
                                                             ALU.mult, ALU.add)
                    tap.then_inc(rec_done if j == LW - 1 else tap_done, 1)
            v.wait_ge(rec_act, 10)
            for k in range(KD):
                last = nc.vector.tensor_scalar(dec[:, k, :], dec[:, k, :], stat[:, C8 + k:C8 + k + 1], None, ALU.mult)
            last.then_inc(rec_dve, 1)
            v.wait_ge(rec_done, 8)
            step(v, nc.vector.tensor_tensor(inp, inp, rec, ALU.mult))
            v.wait_ge(rec_act, 12)
            step(v, nc.vector.tensor_scalar(spare, tnh, -1.0, 1.0, ALU.mult, ALU.add))
            step(v, nc.vector.reciprocal(spare, spare))
            step(v, nc.vector.scalar_tensor_tensor(tnh, tnh, -2.0, spare, ALU.mult, ALU.mult))
            nc.vector.tensor_scalar(tnh, tnh, 1.3e-35, None, ALU.max).then_inc(rec_dve, 1)
            v.wait_ge(rec_act, 13)
            step(v, nc.vector.tensor_tensor(tnh, tnh, inp, ALU.mult))
            for k in range(KD):
                last = nc.vector.tensor_tensor_scan(rec[:, k, :], dec[:, k, :], tnh[:, k, :], 0.0, ALU.mult, ALU.add)
            step(v, last)
            v.wait_ge(wide_act, 8)
            nc.vector.tensor_tensor(hT[:, :, :], rec, gate_r, ALU.mult).then_inc(rec_dve, 1)
            residual_add(v, "r_out")

        block = ctx.enter_context(nc.Block())

        @block.sync
        def _(sp):
            sp.dma_start(x[:, :, :], x_in.rearrange("(t p) d -> p t d", p=P)).then_inc(x_loaded, 16)
            for s in range(RING):
                sp.dma_start(ring[:, s, :], stream[s, :, :]).then_inc(slot_in[s], 16)
            turns = N_SLOTS // RING
            with sp.Fori(1, turns) as r:
                for s in range(RING):
                    sp.wait_ge(slot_used[s], r)
                    sp.dma_start(ring[:, s, :], stream[bass.ds(r * RING + s, 1), :, :]
                                 .rearrange("a p n -> (a p) n")).then_inc(slot_in[s], 16)
            for n in range(turns * RING, N_SLOTS):
                sp.wait_ge(slot_used[n % RING], n // RING)
                sp.dma_start(ring[:, n % RING, :], stream[n, :, :]).then_inc(slot_in[n % RING], 16)
            sp.wait_ge(x_ready, 10)
            sp.dma_start(out.rearrange("(t p) d -> p t d", p=P), x[:, :, :]).then_inc(stored, 16)
            sp.wait_ge(stored, 16)

        @block.scalar
        def _(act):
            act.dma_start(con[:, :], consts).then_inc(const_in, 16)
            act.dma_start(par[:, :], params).then_inc(const_in, 16)
            act.wait_ge(const_in, 32)

            def save(p):
                if debug is not None:
                    act.wait_ge(*X_SOURCE[p])
                    act.dma_start(debug[p].rearrange("(t p) d -> p t d", p=P), x[:, :, :]).then_inc(stored, 16)
                    act.wait_ge(stored, 16 * (p + 1))

            def norm(p, q):
                save(p)
                norm_act(act, p)
                if f"n{q}" in SPLIT_TURNS:
                    split_evac(act, 0, f"n{q}", q)
                else:
                    turn_evac(act, 0, f"n{q}")

            norm(0, 0)
            a_mix_act(act)
            norm(1, 1)
            moe_act(act, 0, START["moe0"])
            norm(2, 2)
            c_mix_act(act)
            norm(3, 3)
            act.dma_start(cat[:, 0, :], bass.AP(tensor=final_rows.tensor, offset=0, ap=[[0, P], [1, D]]))\
               .then_inc(final_in, 16)
            moe_act(act, 1, START["moe1"])
            save(4)
            norm_act(act, 4)
            act.wait_ge(*X_SOURCE[5])
            act.dma_start(onehot, buckets[0:32, :]).then_inc(bucket_in, 16)
            act.dma_start(off_mask, buckets[32:40, :]).then_inc(bucket_in, 16)
            norm(5, 4)
            ffn_act_engine(act, 0, START["ffn0"])
            norm(6, 5)
            s_mix_act(act)
            norm(7, 6)
            act.dma_start(cat[:, 0, :], bass.AP(tensor=final_rows.tensor, offset=D, ap=[[0, P], [1, D]]))\
               .then_inc(final_in, 16)
            ffn_act_engine(act, 1, START["ffn1"])
            norm(8, 7)
            ffn_act_engine(act, 2, START["ffn2"])
            norm(9, 8)
            r_mix_act(act)
            r_gates_act(act)
            norm(10, 9)
            ffn_act_engine(act, 3, START["ffn3"])
            save(11)
            norm_act(act, 11)

        @block.vector
        def _(v):
            nc.vector.memset(ones[:, :], 1.0).then_inc(scattered, 1)
            v.wait_ge(const_in, 32)
            norm_dve(v, 0, 0)
            a_mix_dve(v)
            norm_dve(v, 1, 1)
            moe_dve(v, 0, START["moe0"])
            norm_dve(v, 2, 2)
            c_mix_dve(v)
            norm_dve(v, 3, 3)
            moe_dve(v, 1, START["moe1"])
            final_norm(v, 4, 0)
            norm_dve(v, 5, 4)
            ffn_dve(v, 0, START["ffn0"])
            norm_dve(v, 6, 5)
            s_mix_dve(v)
            norm_dve(v, 7, 6)
            ffn_dve(v, 1, START["ffn1"])
            norm_dve(v, 8, 7)
            ffn_dve(v, 2, START["ffn2"])
            norm_dve(v, 9, 8)
            r_mix_dve(v)
            norm_dve(v, 10, 9)
            ffn_dve(v, 3, START["ffn3"])
            final_norm(v, 11, 1)

        @block.gpsimd
        def _(pool):
            pool.wait_ge(const_in, 32)
            for name in POWERS:
                src, dst, w = {"gmlp": (80, 104, 8), "heads": (80, 104, 24), "ln": (80, 104, 4)}.get(name, (MS, RS, 2))
                power_pool(pool, name, src, dst, w)
                if name == "n1":
                    moe_pool(pool, 0)
                if name == "n3":
                    moe_pool(pool, 1)

        @block.tensor
        def _(pe):
            pe.wait_ge(const_in, 32)
            norm_pe(pe, 0)
            a_mix_pe(pe)
            norm_pe(pe, 1)
            moe_pe(pe, 0, START["moe0"])
            norm_pe(pe, 2)
            c_mix_pe(pe)
            norm_pe(pe, 3)
            moe_pe(pe, 1, START["moe1"])
            norm_pe(pe, 4)
            ffn_pe(pe, 0, START["ffn0"])
            norm_pe(pe, 5)
            s_mix_pe(pe)
            norm_pe(pe, 6)
            ffn_pe(pe, 1, START["ffn1"])
            norm_pe(pe, 7)
            ffn_pe(pe, 2, START["ffn2"])
            norm_pe(pe, 8)
            r_mix_pe(pe)
            norm_pe(pe, 9)
            ffn_pe(pe, 3, START["ffn3"])


def rope_table(pos, width, theta):
    half = width // 2
    inv = np.power(np.float32(theta), -np.arange(half, dtype=np.float32) * np.float32(2.0 / width)).astype(np.float32)
    ang = pos.astype(np.float32)[:, None] * inv[None, :]
    cos, sin = np.cos(ang).astype(np.float32), np.sin(ang).astype(np.float32)
    return np.concatenate([cos, cos], 1), np.concatenate([-sin, sin], 1)


def constant_columns():
    pos = np.arange(T)

    def tiles(a):
        return a.reshape(NT, P, -1).transpose(1, 0, 2).reshape(P, -1)

    def table(pairs):
        cos, sin = (np.concatenate([pair[i] for pair in pairs], 1) for i in range(2))
        return np.concatenate([tiles(cos), tiles(sin)], 1)

    gap = pos[:, None] - pos[None, :]
    count = sum(((gap % d == 0) & (np.abs(gap) // d <= w // (2 * d))).astype(np.int64)
                for w, d in ((128, 1), (512, 4), (2048, 16)))
    band = np.where(count > 0, np.log(np.maximum(count, 1)), OFF).astype(np.float32)
    parts = {
        "ident": np.eye(P), "flip": np.eye(P)[::-1], "band": tiles(band),
        "ropeA": table([rope_table(pos, 16, 500000.0)]), "ropeC": table([rope_table(pos, 32, 500000.0)]),
        "ropeD": table([rope_table(pos // 64, 32, 10000.0), rope_table(pos % 64, 32, 10000.0)]),
        "iota": np.tile(np.arange(CAP), (P, 1)), "half": np.full((P, 32), -0.5),
    }
    return np.concatenate([parts[name].reshape(P, n) for name, n in CONSTS], 1).astype(np.float32)


def bucket_rows():
    dist = 255 - np.arange(SPAN)
    n = np.maximum(dist, 0)
    nf = np.maximum(n, 16).astype(np.float32)
    large = 16 + (np.log(nf / np.float32(16)) / np.float32(np.log(8.0)) * np.float32(16)).astype(np.int32)
    bucket = np.where(n < 16, n, np.minimum(large, 31))
    onehot = (bucket[None, :] == np.arange(32)[:, None]).astype(np.float32)
    window = np.where((dist >= 0) & (dist < 128), 0.0, OFF).astype(np.float32)
    return np.concatenate([onehot, np.tile(window, (8, 1))], 0)


def by_tile(v):
    return v.reshape(-1, P).T


def rows(v):
    return np.broadcast_to(v.reshape(1, -1), (P, v.size))


def param_columns(i):
    gains = [i["norm_mix"][0], i["norm_ffn"][0], i["norm_mix"][1], i["norm_ffn"][1], i["norm_ffn1_2"][0],
             i["norm_mix_2"][0], i["norm_ffn2_2"][0], i["norm_ffn1_2"][1], i["norm_mix_2"][1], i["norm_ffn2_2"][1]]
    relb = np.zeros((P, 8), np.float32)
    relb[0:32] = i["rel_bias_2"]
    parts = {
        "gains": np.concatenate([by_tile(g) for g in gains], 1),
        "router": i["moe_w_router"].reshape(2, KD, P, E).transpose(2, 0, 1, 3),
        "gmlp": rows(i["even_gmlp_norm"][0]),
        "wsT": i["even_w_spatial"][0].transpose(2, 0, 1), "bs": i["even_b_spatial"][0].T,
        "cgain": np.concatenate([by_tile(i["odd_cq_norm"][0]), by_tile(i["odd_ckv_norm"][0])], 1),
        "dgain": np.concatenate([rows(i["odd_dq_norm"][0])] * 8 + [rows(i["odd_dk_norm"][0])] * 2, 1),
        "sinks": rows(i["attn_sinks_2"][0]), "relb": relb,
        "convw": i["conv_b_w_2"][0].reshape(KW, 4, P).transpose(2, 1, 0), "convb": by_tile(i["conv_b_b_2"][0]),
        "lng": rows(i["conv_ln_g_2"][0]), "lnb": rows(i["conv_ln_b_2"][0]),
        "rconvw": i["lru_conv_w_2"][0].reshape(LW, KD, P).transpose(2, 1, 0), "rconvb": by_tile(i["lru_conv_b_2"][0]),
        "gab": by_tile(i["gate_a_b_2"][0]), "gxb": by_tile(i["gate_x_b_2"][0]), "lam": by_tile(i["lru_lambda_2"][0]),
    }
    return np.ascontiguousarray(np.concatenate([parts[name].reshape(P, n) for name, n in PARAMS], 1))


def weight_stream(i):
    s = np.zeros((N_SLOTS, P, SLOT), np.float32)

    def put(n, pieces):
        w, at = s[n].reshape(P, KD, 512), 0
        for m in pieces:
            w[:, :, at:at + m.shape[1]] = m.reshape(KD, P, -1).transpose(1, 0, 2)
            at += m.shape[1]

    def wide(name, m):
        for c in range(0, m.shape[1], 512):
            put(START[name] + c // 512, [m[:, c:c + 512]])

    def experts(name, l):
        for e in range(E):
            n = START[name] + 3 * e
            for m, w in enumerate((i["moe_w_gate"][l, e], i["moe_w_up"][l, e])):
                for half in range(2):
                    s[n + half].reshape(P, 4, 2, 512)[:, :, m] = w[512 * half:512 * half + 512].reshape(4, P, 512)\
                        .transpose(1, 0, 2)
            s[n + 2].reshape(P, 4, D)[:] = i["moe_w_down"][l, e].reshape(4, P, D).transpose(1, 0, 2)

    def ffn(name, g, u, d):
        cut = lambda m, f: m[:, f * P:(f + 1) * P].reshape(KD, P, P).transpose(1, 0, 2).reshape(P, UNIT)
        units = []
        for f in range(FT):
            units += [cut(g, f), cut(u, f)] + ([d[(f - 1) * P:f * P]] if f else [])
        units.append(d[(FT - 1) * P:])
        for n, m in enumerate(units):
            s[START[name] + n // 4][:, (n % 4) * UNIT:(n % 4 + 1) * UNIT] = m

    wide("a_in", i["even_w_in"][0])
    wide("a_out", i["even_w_out"][0])
    experts("moe0", 0)
    w, n = i["odd_w_in"][0], START["c_in"]
    put(n, [w[:, 0:416]])
    put(n + 1, [w[:, 416:928]])
    put(n + 2, [w[:, 928:1184]])
    n = START["c_up"]
    s[n][:, 0:1536].reshape(P, 2, 768)[:] = i["odd_w_cq_up"][0].reshape(2, P, 768).transpose(1, 0, 2)
    s[n][:, 1536:2560] = i["odd_w_ckv_up"][0]
    wide("c_out", i["odd_w_out"][0])
    experts("moe1", 1)
    ffn("ffn0", i["ffn1_wg_2"][0], i["ffn1_wu_2"][0], i["ffn1_wd_2"][0])
    w, n = i["even_w_in_2"][0], START["s_in"]
    a, g = (lambda c: w[:, 768 + c * P:896 + c * P]), (lambda c: w[:, 1280 + c * P:1408 + c * P])
    put(n, [a(0), g(0), a(1), g(1)])
    put(n + 1, [a(2), g(2), a(3), g(3)])
    put(n + 2, [w[:, 0:512]])
    put(n + 3, [w[:, 512:768]])
    wide("s_out", i["even_w_out_2"][0])
    ffn("ffn1", i["ffn2_wg_2"][0], i["ffn2_wu_2"][0], i["ffn2_wd_2"][0])
    ffn("ffn2", i["ffn1_wg_2"][1], i["ffn1_wu_2"][1], i["ffn1_wd_2"][1])
    wide("r_in", np.roll(i["odd_w_in_2"][0], D, 1))
    n = START["r_gate"]
    s[n][:, 0:1024].reshape(P, KD, P)[:] = i["gate_a_w_2"][0].transpose(1, 0, 2)
    s[n][:, 1024:2048].reshape(P, KD, P)[:] = i["gate_x_w_2"][0].transpose(1, 0, 2)
    wide("r_out", i["odd_w_out_2"][0])
    ffn("ffn3", i["ffn2_wg_2"][1], i["ffn2_wu_2"][1], i["ffn2_wd_2"][1])
    return s


DEBUG = False


def kernel(**inputs):
    import concourse.bacc as bacc
    from concourse.bass_utils import run_bass_kernel_spmd as run

    i = {name: np.asarray(a) for name, a in inputs.items()}
    arrays = {
        "stream": weight_stream(i), "params": param_columns(i), "consts": constant_columns(),
        "buckets": bucket_rows(), "final_rows": np.stack([i["final_norm"], i["norm_final_2"]]),
        "x_in": np.ascontiguousarray(i["x"][0]),
    }
    nc = bacc.Bacc("TRN2", target_bir_lowering=False, num_devices=1)
    args = {name: nc.dram_tensor(name, a.shape, mybir.dt.from_np(a.dtype), kind="ExternalInput").ap()
            for name, a in arrays.items()}
    out = nc.dram_tensor("out", (T, D), F32, kind="ExternalOutput").ap()
    debug = [nc.dram_tensor(f"debug{p}", (T, D), F32, kind="ExternalOutput").ap() for p in range(12)] if DEBUG else None
    build(nc, args["stream"], args["params"], args["consts"], args["buckets"], args["final_rows"], args["x_in"], out,
          debug)
    r = run(nc, [arrays], core_ids=[0]).results[0]
    y = r["out"].reshape(1, T, D)
    return (y, *[r[f"debug{p}"].reshape(1, T, D) for p in range(12)]) if DEBUG else y
```

```python
from contextlib import ExitStack

import concourse.bass as bass
import numpy as np
from concourse import mybir

F32 = mybir.dt.float32
F32R = mybir.dt.float32r
ACT = mybir.ActivationFunctionType
ALU = mybir.AluOpType
AX = mybir.AxisListType

P = 128
T = 256
NT = T // P
D = 1024
KD = D // P
SLOT = 4096
RING = 6
EPS, LN_EPS = 1e-6, 1e-5
OFF = -1e30

E, CAP = 16, 32
GRP = P // CAP
FF = 2816
FT = FF // P
UNITS = 3 * FT
UNIT = SLOT // 4
SPLIT = 4
HD = 64
A_HEADS, C_HEADS, G_HEADS, S_HEADS = 12, 8, 8, 8
C_DIM = 96
KW = 31
LW = 4

STAGES = [("a_in", 6), ("a_out", 2), ("moe0", 3 * E), ("c_in", 3), ("c_up", 1), ("c_out", 2), ("moe1", 3 * E),
          ("ffn0", 17), ("s_in", 4), ("s_out", 2), ("ffn1", 17), ("ffn2", 17), ("r_in", 4), ("r_gate", 1),
          ("r_out", 2), ("ffn3", 17)]
START, N_SLOTS = {}, 0
for _name, _n in STAGES:
    START[_name] = N_SLOTS
    N_SLOTS += _n

PARAMS = [("gains", 10 * KD), ("router", 2 * KD * E), ("gmlp", 256), ("wsT", 4 * P), ("bs", 4), ("cgain", 3),
          ("dgain", 640), ("sinks", 8), ("relb", 8), ("convw", 4 * KW), ("convb", 4), ("lng", 512), ("lnb", 512),
          ("rconvw", KD * LW), ("rconvb", KD), ("gab", KD), ("gxb", KD), ("lam", KD)]
CONSTS = [("ident", P), ("flip", P), ("band", 2 * T), ("ropeA", 4 * 16), ("ropeC", 4 * 32), ("ropeD", 4 * 64),
          ("iota", CAP), ("half", 32)]


def columns(parts):
    at, out = 0, {}
    for name, n in parts:
        out[name] = (at, at + n)
        at += n
    return out, at


PCOL, NPARAM = columns(PARAMS)
CCOL, NCONST = columns(CONSTS)
SPAN = 512


def build(nc, stream, params, consts, buckets, final_rows, x_in, out):
    ctx = ExitStack()
    with ctx:
        def sb(name, shape, dt=F32):
            return ctx.enter_context(nc.sbuf_tensor(name, shape, dt))

        def sem(name):
            return ctx.enter_context(nc.semaphore(name))

        ring = sb("ring", [P, RING, SLOT])
        x = sb("x", [P, NT, D])
        xn_base = nc.sbuf_base
        xn = sb("xn", [P, NT, D])
        hT_base = nc.sbuf_base
        hT = sb("hT", [P, KD, T])
        cat_base = nc.sbuf_base
        cat = sb("cat", [P, NT, D])
        par = sb("par", [P, NPARAM])
        con = sb("con", [P, NCONST])
        work_base = nc.sbuf_base
        work = sb("work", [P, 14848])
        stat = sb("stat", [P, 256])
        ones = sb("ones", [E, T])
        bank = [ctx.enter_context(nc.psum_tensor(f"bank{i}", [P, 512], F32)) for i in range(8)]
        spread = nc.dram_tensor("spread", [8, SPAN], F32)

        def pc(name):
            return par[:, PCOL[name][0]:PCOL[name][1]]

        def cc(name):
            return con[:, CCOL[name][0]:CCOL[name][1]]

        ident, flip = cc("ident"), cc("flip")
        gains = pc("gains").rearrange("p (n k) -> p n k", k=KD)
        W = work

        def region(at, shape):
            n = int(np.prod(shape))
            ap = W[:, at:at + n]
            if len(shape) == 2:
                return ap.rearrange("p (a b) -> p a b", a=shape[0])
            if len(shape) == 3:
                return ap.rearrange("p (a b c) -> p a b c", a=shape[0], b=shape[1])
            return ap

        def part(name, base, at, shape):
            return nc.alloc_sbuf_tensor_at(name, [P] + shape, F32R, offset=base + 4 * at)

        hT_hi = part("hT_hi", hT_base, 0, [KD, T])
        norm_lo, cat_lo = part("norm_lo", cat_base, 0, [KD, T]), part("cat_lo", xn_base, 0, [KD, T])
        act_hi, act_lo = part("act_hi", work_base, 3072, [2, T]), part("act_lo", work_base, 3584, [2, T])
        unit_hi, unit_lo = part("unit_hi", work_base, 5632, [SPLIT, UNIT]), part("unit_lo", work_base, 9728, [SPLIT, UNIT])
        few_hi, few_lo = part("few_hi", cat_base, 0, [2, UNIT]), part("few_lo", work_base, 12312, [2, UNIT])

        TMP = 14848 - 3072
        probs = region(TMP, (3, NT * T))
        probsT = region(TMP + 2048, (2, 512))

        const_in = sem("const_in")
        params_in = sem("params_in")
        x_loaded = sem("x_loaded")
        slot_in = [sem(f"slot_in{i}") for i in range(RING)]
        slot_used = [sem(f"slot_used{i}") for i in range(RING)]
        x_ready = sem("x_ready")
        x_half = sem("x_half")
        tail_done = sem("tail_done")
        sq_done = sem("sq_done")
        power_in = sem("power_in")
        power_out = sem("power_out")
        xn_done = [sem("xn0_done"), sem("xn1_done")]
        turned = sem("turned")
        turn_out = [sem("turn_out_act"), sem("turn_out_dve")]
        turn_src = sem("turn_src")
        proj_done = [sem("proj0_done"), sem("proj1_done")]
        proj_free = [sem("proj0_free"), sem("proj1_free")]
        dve_step = sem("dve_step")
        gelu_done = sem("gelu_done")
        gating_in = sem("gating_in")
        gating_done = sem("gating_done")
        scores_done = sem("scores_done")
        masked_done = sem("masked_done")
        probs_done = sem("probs_done")
        probs_turned = sem("probs_turned")
        probsT_done = sem("probsT_done")
        heads_done = sem("heads_done")
        cat_done = sem("cat_done")
        route_pe, route_act, route_dve = sem("route_pe"), sem("route_act"), sem("route_dve")
        staged = sem("staged")
        expert_gu = sem("expert_gu")
        expert_silu = sem("expert_silu")
        expert_act = sem("expert_act")
        expert_turned = sem("expert_turned")
        expert_actT = sem("expert_actT")
        y_out = [sem("y_out_act"), sem("y_out_dve")]
        scattered = sem("scattered")
        scatter_added = sem("scatter_added")
        turn_hi = sem("turn_hi")
        turn_lo = sem("turn_lo")
        hi_done = sem("hi_done")
        lo_done = sem("lo_done")
        unit_used = sem("unit_used")
        ffn_product = sem("ffn_product")
        ffn_silu = sem("ffn_silu")
        ffn_act = sem("ffn_act")
        wide_done = sem("wide_done")
        wide_act, wide_dve = sem("wide_act"), sem("wide_dve")
        bucket_in = sem("bucket_in")
        spread_done = sem("spread_done")
        spread_ready = sem("spread_ready")
        spread_out = sem("spread_out")
        rows_in = sem("rows_in")
        rec_in = sem("rec_in")
        bias_done = sem("bias_done")
        bias_out = sem("bias_out")
        tap_done = sem("tap_done")
        conv_done = sem("conv_done")
        conv_turned = sem("conv_turned")
        ln_done = sem("ln_done")
        conv_cat = sem("conv_cat")
        rec_done = sem("rec_done")
        rec_gates = sem("rec_gates")
        rec_act = sem("rec_act")
        rec_dve = sem("rec_dve")
        rec_out = sem("rec_out")
        rec_hi, rec_lo = sem("rec_hi"), sem("rec_lo")
        final_in = sem("final_in")
        stored = sem("stored")

        def ge(eng, s, v):
            if v > 0:
                eng.wait_ge(s, v)

        def slot(n):
            return ring[:, n % RING, :]

        def loaded(eng, n):
            eng.wait_ge(slot_in[n % RING], 16 * (n // RING + 1))

        def used(eng, n):
            eng.wait_ge(slot_used[n % RING], n // RING + 1)

        def release(ins, n):
            ins.then_inc(slot_used[n % RING], 1)

        dve_steps = [0]

        def step(eng, ins):
            ins.then_inc(dve_step, 1)
            dve_steps[0] += 1
            eng.wait_ge(dve_step, dve_steps[0])

        def norm_groups(q):
            groups = []
            for b in range(4):
                pieces = [(xn[:, t, (2 * b + kk) * P:(2 * b + kk + 1) * P], kk * T + t * P, P, P)
                          for kk in range(2) for t in range(NT)]
                outs = [(hT[:, 2 * b + kk, :], (P, kk * T, T), gains[:, q, 2 * b + kk:2 * b + kk + 1])
                        for kk in range(2)]
                groups.append((pieces, outs))
            return groups

        def cat_groups():
            groups = []
            for b in range(4):
                pieces = [(cat[:, t, (2 * b + kk) * P:(2 * b + kk + 1) * P], kk * T + t * P, P, P)
                          for kk in range(2) for t in range(NT)]
                groups.append((pieces, [(hT[:, 2 * b:2 * b + 2, :].rearrange("p a b -> p (a b)"), (P, 0, 512), None)]))
            return groups

        def pair_groups(blocks):
            groups = []
            for i in range(0, len(blocks), 2):
                pieces, outs = [], []
                for kk, (src, rows, dst) in enumerate(blocks[i:i + 2]):
                    pieces += [(src(t), kk * T + t * P, rows, P) for t in range(NT)]
                    outs.append((dst, (rows, kk * T, T), None))
                groups.append((pieces, outs))
            return groups

        uA = region(0, (NT, FF))
        qkA = region(5632, (12, T))
        A_GROUPS = pair_groups([(lambda t, b=b: uA[:, t, b * P:(b + 1) * P], P, qkA[:, b, :]) for b in range(12)])

        uC = region(0, (NT, 1280))
        upq = region(2560, (NT, 768))
        upkv = region(4096, (NT, D))
        qcT = region(6144, (C_HEADS, T))
        kcT = region(8192, (C_HEADS, T))
        dT = region(10240, (6, T))
        cT = region(TMP, (3, T))
        xnf = xn[:, :, :].rearrange("p a b -> p (a b)")
        kc = xnf[:, 0:1536].rearrange("p (t h c) -> p t h c", t=NT, h=C_HEADS)
        dkk = xnf[:, 1536:2048].rearrange("p (t h c) -> p t h c", t=NT, h=4)
        cg = pc("cgain")
        C1_GROUPS = [
            ([(uC[:, t, k * P:(k + 1) * P], k * T + t * P, P, P) for k in range(2) for t in range(NT)],
             [(cT[:, k, :], (P, k * T, T), cg[:, k:k + 1]) for k in range(2)]),
            ([(uC[:, t, 256:384], t * P, P, P) for t in range(NT)], [(cT[:, 2, :], (P, 0, T), cg[:, 2:3])]),
        ]
        C2_GROUPS = pair_groups(
            [(lambda t, h=h: upq[:, t, h * C_DIM:(h + 1) * C_DIM], C_DIM, qcT[0:C_DIM, h, :]) for h in range(C_HEADS)]
            + [(lambda t, h=h: kc[:, t, h, :], C_DIM, kcT[0:C_DIM, h, :]) for h in range(C_HEADS)])
        C3_GROUPS = pair_groups(
            [(lambda t, b=b: uC[:, t, 512 + b * P:640 + b * P], P, dT[:, b, :]) for b in range(4)]
            + [(lambda t, b=b: dkk[:, t, 2 * b:2 * b + 2, :].rearrange("p a b -> p (a b)"), P, dT[:, 4 + b, :])
               for b in range(2)])

        uS = region(0, (NT, 768))
        glu = region(1536, (4, T + KW - 1))
        gluf = W[:, 1536:1536 + 4 * (T + KW - 1)]
        gate_s = region(2680, (2, T))
        qkS = region(3192, (6, T))
        bias_s = region(4728, (S_HEADS, 2 * T))
        rows_s = region(TMP - 1024, (S_HEADS, 2 * T))
        conv_s = [cat[:, c // 2, 512 + (c % 2) * T:512 + (c % 2 + 1) * T] for c in range(4)]
        onehot = W[0:32, 8824:8824 + SPAN]
        off_mask = W[0:8, 9336:9336 + SPAN]
        spread_sb = W[0:8, 9848:9848 + SPAN]
        S1_GROUPS = pair_groups([(lambda t, b=b: uS[:, t, b * P:(b + 1) * P], P, qkS[:, b, :]) for b in range(4)]
                                + [(lambda t, b=b: dkk[:, t, 2 * b:2 * b + 2, :].rearrange("p a b -> p (a b)"), P,
                                    qkS[:, 4 + b, :]) for b in range(2)])

        gate_r = region(0, (KD, T))
        pad_r = region(2048, (KD, T + LW - 1))
        pad_rf = W[:, 2048:2048 + KD * (T + LW - 1)]
        rec = region(4120, (KD, T))
        dec = region(6168, (KD, T))
        inp = region(8216, (KD, T))
        tnh = region(10264, (KD, T))
        spare = pad_rf[:, 0:2048].rearrange("p (a b) -> p a b", a=KD)

        hsel = region(0, (GRP, KD, P))
        pick = region(4096, (NT, 512))
        pickg = region(5120, (NT, 512))
        putT = region(6144, (GRP, T))
        hcur = region(7168, (KD, P))
        pcur = region(8192, (T,))
        ybuf = region(8448, (D,))
        silu_e = region(9472, (2, P))
        act_e = region(9728, (2, P))
        actT_e = region(9984, (2, P))
        aff = region(10240, (NT, E))
        scan_a = W[0:E, 10272:10272 + T]
        scan_b = W[0:E, 10528:10528 + T]
        chosen = W[0:E, 10784:10784 + T]
        placed = W[0:E, 11040:11040 + T]
        top8 = W[0:E, 11296:11304]
        posT = region(11304, (NT, E))

        silu_f = region(2048, (2, T))
        act_f = region(2560, (2, T))

        TURNS, TURN_AT = [], {}
        for name, groups in (("n0", norm_groups(0)), ("a", A_GROUPS), ("cat_a", cat_groups()), ("n1", norm_groups(1)),
                             ("n2", norm_groups(2)), ("c1", C1_GROUPS), ("c3", C3_GROUPS), ("c2", C2_GROUPS), ("cat_c", cat_groups()),
                             ("n3", norm_groups(3)), ("n4", norm_groups(4)), ("n5", norm_groups(5)),
                             ("s1", S1_GROUPS), ("cat_s", cat_groups()), ("n6", norm_groups(6)),
                             ("n7", norm_groups(7)), ("n8", norm_groups(8)), ("n9", norm_groups(9))):
            TURN_AT[name] = (len(TURNS), len(TURNS) + len(groups))
            TURNS += groups

        SPLIT_TURNS = ("n0", "cat_a", "n2", "cat_c", "n4", "cat_s", "n6", "n7", "n9")
        TURN_DONE, totals = [], {}
        for name, (first, end) in TURN_AT.items():
            for g in range(first, end):
                signal = turn_lo if name in SPLIT_TURNS else turn_out[g % 2]
                totals[signal.name] = totals.get(signal.name, 0) + 1
                TURN_DONE.append((signal, totals[signal.name]))

        def turn_pe(pe, name, lo=0, hi=None):
            first, end = TURN_AT[name]
            for g in range(first + lo, end if hi is None else first + hi):
                if g >= 4:
                    pe.wait_ge(*TURN_DONE[g - 4])
                for src, at, rows, cols in TURNS[g][0]:
                    last = nc.tensor.transpose(bank[g % 4][0:rows, at:at + cols], src, ident)
                last.then_inc(turned, 1)

        def turn_evac(eng, which, name):
            for g in range(*TURN_AT[name]):
                if g % 2 != which:
                    continue
                eng.wait_ge(turned, g + 1)
                for dst, (rows, at, n), gain in TURNS[g][1]:
                    src = bank[g % 4][0:rows, at:at + n]
                    if which == 0:
                        last = nc.scalar.activation(dst, src, ACT.Copy, scale=1.0 if gain is None else gain)
                    elif gain is None:
                        last = nc.vector.tensor_copy(dst, src)
                    else:
                        last = nc.vector.tensor_scalar(dst, src, gain, None, ALU.mult)
                last.then_inc(turn_out[which], 1)

        def split_evac(eng, which, name, j):
            g = TURN_AT[name][0] + j
            if which == 0:
                eng.wait_ge(turned, g + 1)
            else:
                eng.wait_ge(turn_hi, TURN_DONE[g][1])
            low = cat_lo if name.startswith("cat") else norm_lo
            for kk in range(2):
                k = 2 * j + kk
                src, high = bank[g % 4][:, kk * T:(kk + 1) * T], hT_hi[:, k, :]
                gain = None if name.startswith("cat") else gains[:, int(name[1:]), k:k + 1]
                if which == 0:
                    last = nc.scalar.activation(high, src, ACT.Copy, scale=1.0 if gain is None else gain)
                elif gain is None:
                    last = nc.vector.tensor_tensor(low[:, k, :], src, high.bitcast(F32), ALU.subtract)
                else:
                    last = nc.vector.scalar_tensor_tensor(low[:, k, :], src, gain, high.bitcast(F32), ALU.mult,
                                                          ALU.subtract)
            last.then_inc(turn_lo if which else turn_hi, 1)

        def turns_out(eng, name):
            first, end = TURN_AT[name]
            for g in range(max(first, end - 2), end):
                eng.wait_ge(*TURN_DONE[g])

        def gate_unit(f):
            return max(3 * f - 1, 0)

        def up_unit(f):
            return max(3 * f, 1)

        def down_unit(f):
            return min(3 * f + 4, UNITS - 1)

        PASS = 8
        PASS_UNITS = 3 * PASS
        STAGE_UNITS = {"a_in": 24, "a_out": 8, "c_in": 12, "c_out": 8, "ffn0": UNITS, "s_out": 8, "ffn1": UNITS,
                       "ffn2": UNITS, "r_out": 8, "ffn3": UNITS}

        def slot_end(name, u):
            return u % 4 == 3 or u == STAGE_UNITS[name] - 1

        def low_count(name, u):
            return sum(1 for i in range(u + 1) if not slot_end(name, i))

        UNIT_BASE, LOW_BASE = {}, {}
        for name in STAGE_UNITS:
            UNIT_BASE[name] = sum(STAGE_UNITS[i] for i in UNIT_BASE)
            LOW_BASE[name] = sum(low_count(i, STAGE_UNITS[i] - 1) for i in LOW_BASE)

        def raw_unit(name, u):
            return slot(START[name] + u // 4)[:, (u % 4) * UNIT:(u % 4 + 1) * UNIT]

        def depth(name):
            return 2 if name == "r_out" else SPLIT

        def high_buf(name, u):
            return (few_hi if name == "r_out" else unit_hi)[:, u % depth(name), :]

        def low_buf(name, u):
            return (few_lo if name == "r_out" else unit_lo)[:, u % depth(name), :]

        def split_high(act, name, u, it=0):
            n = START[name] + u // 4
            if u % 4 == 0:
                act.wait_ge(slot_in[n % RING], 16 * (n // RING + 1) + 16 * it)
            if u >= depth(name):
                act.wait_ge(unit_used, UNIT_BASE[name] + u - depth(name) + 1 + PASS_UNITS * it)
            nc.scalar.activation(high_buf(name, u), raw_unit(name, u), ACT.Copy).then_inc(hi_done, 1)

        def split_low(v, name, u, it=0):
            n = START[name] + u // 4
            v.wait_ge(hi_done, UNIT_BASE[name] + u + 1 + PASS_UNITS * it)
            low = nc.vector.tensor_tensor(low_buf(name, u), raw_unit(name, u), high_buf(name, u).bitcast(F32),
                                          ALU.subtract)
            low.then_inc(slot_used[n % RING] if slot_end(name, u) else lo_done, 1)

        def high_ready(pe, name, u, it=0):
            pe.wait_ge(hi_done, UNIT_BASE[name] + u + 1 + PASS_UNITS * it)

        def low_ready(pe, name, u, it=0):
            n = START[name] + u // 4
            if slot_end(name, u):
                pe.wait_ge(slot_used[n % RING], n // RING + 1 + it)
            else:
                pe.wait_ge(lo_done, LOW_BASE[name] + low_count(name, u) + (PASS_UNITS - RING) * it)

        PROJ, PROJ_AT = [], {}
        SPLIT_PROJ = {"a_in": "n0", "a_out": "cat_a", "c_in": "n2", "c_out": "cat_c", "s_out": "cat_s", "r_out": None}

        def plain(n, width, last=True):
            w = slot(n).rearrange("p (k n) -> p k n", k=KD)
            return (n, KD, lambda k: w[:, k, 0:width], lambda k, t: hT[:, k, t * P:(t + 1) * P], width, last)

        def up(n, tiles, first, base, stride, width, last):
            return (n, tiles, lambda k: slot(n)[:, base + k * stride:base + k * stride + width],
                    lambda k, t: cT[:, first + k, t * P:(t + 1) * P], width, last)

        def stage(name, items):
            PROJ_AT[name] = (len(PROJ), len(PROJ) + len(items))
            PROJ.extend(items)

        n = START["a_in"]
        stage("a_in", [plain(n + c, 512 if c < 5 else 256) for c in range(6)])
        stage("a_out", [plain(START["a_out"] + c, 512) for c in range(2)])
        n = START["c_in"]
        stage("c_in", [plain(n, 512), plain(n + 1, 512), plain(n + 2, 256)])
        n = START["c_up"]
        stage("c_up", [up(n, 2, 0, 0, 768, 512, False), up(n, 2, 0, 512, 768, 256, False),
                       up(n, 1, 2, 1536, 0, 512, False), up(n, 1, 2, 2048, 0, 512, True)])
        stage("c_out", [plain(START["c_out"] + c, 512) for c in range(2)])
        n = START["s_in"]
        stage("s_in", [plain(n + 2, 512), plain(n + 3, 256)])
        stage("s_out", [plain(START["s_out"] + c, 512) for c in range(2)])
        stage("r_out", [plain(START["r_out"] + c, 512) for c in range(2)])
        LAST_ADDS = {PROJ_AT[s][1] - 1 for s in ("a_out", "c_out", "s_out", "r_out")}

        def split_stage(m):
            for name in SPLIT_PROJ:
                first, end = PROJ_AT[name]
                if first <= m < end:
                    return name, m - first
            return None

        def late_up(m):
            return PROJ_AT["c_up"][0] + 2 <= m < PROJ_AT["c_up"][1]

        def proj_bank(m, t):
            return bank[(4 if split_stage(m) or late_up(m) else 0) + 2 * t + m % 2]

        def freed(m, t):
            return sum(1 for i in range(m + 1) if not (i in LAST_ADDS and (t == 1 or split_stage(i)[0] in TAILS)))

        def proj_pe(pe, name):
            for m in range(*PROJ_AT[name]):
                n, tiles, rhs, lhs, width, last_use = PROJ[m]
                loaded(pe, n)
                for t in range(NT):
                    if m >= 2 and not late_up(m):
                        ge(pe, proj_free[t], freed(m - 2, t))
                    for k in range(tiles):
                        mm = nc.tensor.matmul(proj_bank(m, t)[:, 0:width], lhs(k, t), rhs(k),
                                              start=(k == 0), stop=(k == tiles - 1))
                    if t == 1 and last_use:
                        release(mm, n)
                    else:
                        mm.then_inc(proj_done[t], 1)

        def split_proj_pe(pe, name):
            first, end = PROJ_AT[name]
            turns = TURN_AT[SPLIT_PROJ[name]][0] if SPLIT_PROJ[name] else None
            left_lo = norm_lo if name in ("a_in", "c_in") else cat_lo
            for m in range(first, end):
                width = PROJ[m][4]
                for t in range(NT):
                    if m >= 2:
                        ge(pe, proj_free[t], freed(m - 2, t))
                if m in LAST_ADDS and name in TAILS:
                    for t in range(NT):
                        for j in range(4):
                            u = 4 * (m - first) + j
                            high = high_buf(name, u).rearrange("p (k c) -> p k c", k=2)
                            low = low_buf(name, u).rearrange("p (k c) -> p k c", k=2)
                            high_ready(pe, name, u)
                            low_ready(pe, name, u)
                            for kk in range(2):
                                for left, right in ((hT_hi, high), (left_lo, high), (hT_hi, low)):
                                    mm = nc.tensor.matmul(proj_bank(m, t)[:, 0:width],
                                                          left[:, 2 * j + kk, t * P:(t + 1) * P], right[:, kk, 0:width],
                                                          start=(j == 0 and kk == 0 and right is high and left is hT_hi),
                                                          stop=(j == 3 and kk == 1 and right is low),
                                                          skip_group_check=True)
                            if t == 1:
                                mm.then_inc(unit_used, 1)
                        if t == 0:
                            mm.then_inc(tail_done, 1)
                    continue
                for j in range(4):
                    u = 4 * (m - first) + j
                    high = high_buf(name, u).rearrange("p (k c) -> p k c", k=2)
                    low = low_buf(name, u).rearrange("p (k c) -> p k c", k=2)
                    if m == first:
                        pe.wait_ge(*(TURN_DONE[turns + j] if SPLIT_PROJ[name] else (rec_lo, j + 1)))
                    high_ready(pe, name, u)
                    for kk in range(2):
                        for t in range(NT):
                            for left in (hT_hi, left_lo):
                                nc.tensor.matmul(proj_bank(m, t)[:, 0:width], left[:, 2 * j + kk, t * P:(t + 1) * P],
                                                 high[:, kk, 0:width], start=(j == 0 and kk == 0 and left is hT_hi),
                                                 stop=False, skip_group_check=True)
                    low_ready(pe, name, u)
                    for kk in range(2):
                        for t in range(NT):
                            mm = nc.tensor.matmul(proj_bank(m, t)[:, 0:width], hT_hi[:, 2 * j + kk, t * P:(t + 1) * P],
                                                  low[:, kk, 0:width], start=False, stop=(j == 3 and kk == 1),
                                                  skip_group_check=True)
                    mm.then_inc(unit_used, 1)

        def split_proj(eng, which, name, dst=None, midway=None):
            first, end = PROJ_AT[name]
            part_of = split_low if which else split_high
            for j in range(4):
                if j == 2 and midway is not None:
                    midway()
                split_evac(eng, which, SPLIT_PROJ[name], j)
                if j >= EARLY or name not in STAGE_AFTER.values():
                    part_of(eng, name, j)
            for m in range(first, end):
                if m + 1 < end:
                    for j in range(4):
                        part_of(eng, name, 4 * (m + 1 - first) + j)
                if dst is not None:
                    proj_copy_one(eng, m, which, dst(m - first))

        def proj_out(eng, m, t):
            if split_stage(m):
                name, c = split_stage(m)
                eng.wait_ge(unit_used, UNIT_BASE[name] + 4 * c + 4)
            elif t == 1 and PROJ[m][5]:
                used(eng, PROJ[m][0])
            else:
                eng.wait_ge(proj_done[t], sum(1 for i in range(m + 1)
                                              if not (t == 1 and PROJ[i][5]) and split_stage(i) is None))

        def proj_copy_one(eng, m, t, dst):
            proj_out(eng, m, t)
            src = proj_bank(m, t)[:, 0:PROJ[m][4]]
            if t == 0:
                nc.scalar.activation(dst, src, ACT.Copy).then_inc(proj_free[t], 1)
            else:
                nc.vector.tensor_copy(dst, src).then_inc(proj_free[t], 1)

        def proj_copy(eng, name, t, dst):
            first, end = PROJ_AT[name]
            for m in range(first, end):
                proj_copy_one(eng, m, t, dst(m - first))

        def projected(eng, name):
            m = PROJ_AT[name][1] - 1
            eng.wait_ge(proj_free[0], freed(m, 0))
            eng.wait_ge(proj_free[1], freed(m, 1))

        def residual_add(v, name):
            first, end = PROJ_AT[name]
            for m in range(first, end):
                for t in range(NT):
                    early = m == end - 1 and t == 0 and name in TAILS
                    if early:
                        v.wait_ge(tail_done, TAILS.index(name) + 1)
                    else:
                        proj_out(v, m, t)
                    xs = x[:, t, (m - first) * 512:(m - first + 1) * 512]
                    add = nc.vector.tensor_tensor(xs, proj_bank(m, t)[:, :], xs, ALU.add)
                    if early:
                        add.then_inc(x_half, 1)
                    else:
                        add.then_inc(x_ready if m == end - 1 and t == 1 else proj_free[t], 1)

        X_SOURCE = [(x_loaded, 16), (x_ready, 1), (scatter_added, 4), (x_ready, 2), (scatter_added, 8), (x_ready, 3),
                    (x_ready, 4), (x_ready, 5), (x_ready, 6), (x_ready, 7), (x_ready, 8), (x_ready, 9)]
        TAILS = ["a_out", "c_out", "ffn0", "s_out", "ffn1", "ffn2", "ffn3"]
        X_HALF = {1: 1, 3: 2, 6: 3, 7: 4, 8: 5, 9: 6, 11: 7}
        POWERS = {name: i for i, name in enumerate(
            ["n0", "gmlp", "n1", "n2", "latents", "heads", "n3", "f0", "n4", "n5", "ln", "n6", "n7", "n8", "n9", "f1"])}
        SS, MS, RS = 64, 66, 68

        STAGE_AFTER = {"n2": "c_in", "n4": "ffn0", "n6": "ffn1", "n7": "ffn2", "n9": "ffn3"}
        EARLY = 2

        def norm_act(act, p, name=None):
            act.wait_ge(*((x_half, X_HALF[p]) if p in X_HALF else X_SOURCE[p]))
            squares = W[:, D:2 * D]
            nc.scalar.activation(squares, x[:, 0, :], ACT.Square, accum_out=stat[:, SS:SS + 1]).then_inc(sq_done, 1)
            if name in STAGE_AFTER:
                act.wait_ge(*X_SOURCE[p])
                for u in range(EARLY):
                    split_high(act, STAGE_AFTER[name], u)
            if name is not None:
                act.wait_ge(power_out, POWERS[name] + 1)
                nc.scalar.activation(xn[:, 0, :], x[:, 0, :], ACT.Copy, scale=stat[:, RS:RS + 1]).then_inc(xn_done[0], 1)

        def power_pool(pool, name, src, dst, w):
            pool.wait_ge(power_in, POWERS[name] + 1)
            nc.gpsimd.tensor_tensor(stat[:, dst:dst + w], stat[:, src:src + w], cc("half")[:, 0:w],
                                    ALU.pow).then_inc(power_out, 1)

        def norm_root(v, p, name):
            v.wait_ge(*X_SOURCE[p])
            nc.vector.tensor_tensor_reduce(xn[:, 1, :], x[:, 1, :], x[:, 1, :], 1.0, 0.0, ALU.mult, ALU.add,
                                           stat[:, SS + 1:SS + 2]).then_inc(sq_done, 1)
            v.wait_ge(sq_done, 2 * (p + 1))
            nc.vector.tensor_scalar(stat[:, MS:MS + 2], stat[:, SS:SS + 2], 1.0 / D, EPS, ALU.mult,
                                    ALU.add).then_inc(power_in, 1)
            v.wait_ge(power_out, POWERS[name] + 1)

        def norm_dve(v, p, q):
            norm_root(v, p, f"n{q}")
            nc.vector.tensor_scalar(xn[:, 1, :], x[:, 1, :], stat[:, RS + 1:RS + 2], None, ALU.mult).then_inc(xn_done[1], 1)
            if f"n{q}" in STAGE_AFTER:
                for u in range(EARLY):
                    split_low(v, STAGE_AFTER[f"n{q}"], u)
            if f"n{q}" not in SPLIT_TURNS:
                turn_evac(v, 1, f"n{q}")

        def norm_pe(pe, q):
            pe.wait_ge(xn_done[0], q + 1)
            pe.wait_ge(xn_done[1], q + 1)
            turn_pe(pe, f"n{q}")
            if f"n{q}" not in SPLIT_TURNS:
                turns_out(pe, f"n{q}")

        def final_norm(v, p, i):
            norm_root(v, p, f"f{i}")
            v.wait_ge(final_in, 16 * (i + 1))
            for t in range(NT):
                last = nc.vector.scalar_tensor_tensor(x[:, t, :], x[:, t, :], stat[:, RS + t:RS + t + 1],
                                                      W[:, 0:D] if i else cat[:, 0, :], ALU.mult, ALU.mult)
                if i == 1 and t == 0:
                    last.then_inc(x_half, 1)
            last.then_inc(x_ready, 1)

        def half_rows(h):
            return slice(64 * (h % 2), 64 * (h % 2) + 64)

        band = cc("band")
        HEADS = {
            "a": [(qkA[half_rows(h), h // 2, :], qkA[half_rows(h), 6 + h // 2, :],
                   lambda s, h=h: uA[:, s, 1536 + h * HD:1536 + (h + 1) * HD], HD ** -0.5, band, None, h * HD)
                  for h in range(A_HEADS)],
            "c": [(qcT[0:C_DIM, h, :], kcT[0:C_DIM, h, :], lambda s, h=h: upkv[:, s, h * P + HD:(h + 1) * P],
                   C_DIM ** -0.5, None, None, h * HD) for h in range(C_HEADS)]
                 + [(dT[half_rows(h), h // 2, :], dT[half_rows(h), 4 + h // 4, :],
                     lambda s, h=h: uC[:, s, 1152 + (h // 4) * HD:1152 + (h // 4 + 1) * HD],
                     HD ** -0.5, None, None, 512 + h * HD) for h in range(G_HEADS)],
            "s": [(qkS[half_rows(h), h // 2, :], qkS[half_rows(h), 4 + h // 4, :],
                   lambda s, h=h: uS[:, s, 640 + (h // 4) * HD:640 + (h // 4 + 1) * HD],
                   HD ** -0.5, bias_s[:, h, :], h, h * HD) for h in range(S_HEADS)],
        }
        HEAD_AT = {"a": 0, "c": A_HEADS, "s": A_HEADS + C_HEADS + G_HEADS}
        SINK_NEG = 128

        def attend_pe(pe, name):
            g0, heads = HEAD_AT[name], HEADS[name]
            for i in range(len(heads) + 3):
                if i < len(heads):
                    g, (q, k, *_) = g0 + i, heads[i]
                    ge(pe, masked_done, g - 1)
                    for t in range(NT):
                        mm = nc.tensor.matmul(bank[4 + g % 2][:, t * T:(t + 1) * T], q[:, t * P:(t + 1) * P], k,
                                              start=True, stop=True)
                    mm.then_inc(scores_done, 1)
                if 2 <= i < len(heads) + 2:
                    g = g0 + i - 2
                    pe.wait_ge(probs_done, g + 1)
                    ge(pe, probsT_done, g - 1)
                    for s in range(NT):
                        for t in range(NT):
                            mm = nc.tensor.matmul(bank[6 + g % 2][:, s * T + t * P:s * T + (t + 1) * P],
                                                  probs[:, g % 3, t * T + s * P:t * T + (s + 1) * P], ident,
                                                  start=True, stop=True)
                    mm.then_inc(probs_turned, 1)
                if i >= 3:
                    g, v = g0 + i - 3, heads[i - 3][2]
                    pe.wait_ge(probsT_done, g + 1)
                    ge(pe, cat_done, g - 1)
                    for t in range(NT):
                        for s in range(NT):
                            mm = nc.tensor.matmul(bank[2 + g % 2][:, t * HD:(t + 1) * HD],
                                                  probsT[:, g % 2, s * T + t * P:s * T + (t + 1) * P], v(s),
                                                  start=(s == 0), stop=(s == NT - 1))
                    mm.then_inc(heads_done, 1)

        def attend_act(act, name):
            g0, heads = HEAD_AT[name], HEADS[name]
            for i in range(len(heads) + 2):
                if i < len(heads):
                    g, at = g0 + i, 16 * ((g0 + i) % 4)
                    act.wait_ge(masked_done, g + 1)
                    for t in range(NT):
                        row = probs[:, g % 3, t * T:(t + 1) * T]
                        last = nc.scalar.activation(row, row, ACT.Exp, bias=stat[:, at + t:at + t + 1],
                                                    accum_out=stat[:, at + 2 + t:at + 3 + t])
                    if heads[i][5] is not None:
                        last = nc.scalar.activation(stat[:, at + 6:at + 8], stat[:, at + 4:at + 6], ACT.Exp)
                    last.then_inc(probs_done, 1)
                if i >= 2:
                    g = g0 + i - 2
                    act.wait_ge(probs_turned, g + 1)
                    ge(act, heads_done, g - 1)
                    nc.scalar.activation(probsT[:, g % 2, :], bank[6 + g % 2][:, :], ACT.Copy).then_inc(probsT_done, 1)

        def attend_dve(v, name, between=None):
            g0, heads = HEAD_AT[name], HEADS[name]
            for i in range(len(heads) + 3):
                if i < len(heads):
                    scale, bias, sink = heads[i][3:6]
                    g, at = g0 + i, 16 * ((g0 + i) % 4)
                    v.wait_ge(scores_done, g + 1)
                    ge(v, probs_turned, g - 2)
                    if bias is None:
                        step(v, nc.vector.tensor_scalar(probs[:, g % 3, :], bank[4 + g % 2][:, :], scale, None,
                                                        ALU.mult))
                    else:
                        step(v, nc.vector.scalar_tensor_tensor(probs[:, g % 3, :], bank[4 + g % 2][:, :], scale,
                                                               bias, ALU.mult, ALU.add))
                    top = nc.vector.tensor_reduce(stat[:, at:at + 2],
                                                  probs[:, g % 3, :].rearrange("p (t s) -> p t s", t=NT), AX.X,
                                                  ALU.max, negate=True)
                    if sink is not None:
                        step(v, top)
                        step(v, nc.vector.tensor_scalar(stat[:, at:at + 2], stat[:, at:at + 2],
                                                        stat[:, SINK_NEG + sink:SINK_NEG + sink + 1], None, ALU.min))
                        top = nc.vector.tensor_scalar(stat[:, at + 4:at + 6], stat[:, at:at + 2],
                                                      pc("sinks")[:, sink:sink + 1], None, ALU.add)
                    top.then_inc(masked_done, 1)
                if i >= 3:
                    g, at = g0 + i - 3, 16 * ((g0 + i - 3) % 4)
                    v.wait_ge(probs_done, g + 1)
                    sums = stat[:, at + 2:at + 4]
                    if heads[i - 3][5] is not None:
                        step(v, nc.vector.tensor_tensor(sums, sums, stat[:, at + 6:at + 8], ALU.add))
                    step(v, nc.vector.reciprocal(stat[:, at + 8:at + 10], sums))
                    v.wait_ge(heads_done, g + 1)
                    col = heads[i - 3][6]
                    nc.vector.tensor_tensor(cat[:, :, col:col + HD],
                                            bank[2 + g % 2][:, 0:NT * HD].rearrange("p (t c) -> p t c", t=NT),
                                            stat[:, at + 8:at + 10].unsqueeze(2).to_broadcast([P, NT, HD]),
                                            ALU.mult).then_inc(cat_done, 1)
                if between is not None:
                    between(i)

        def rope(v, items, half, signal=None, at=TMP):
            temps = []
            for view, cos, sin in items:
                h, r = view.shape[1], view.shape[2]
                a, b = region(at, (h, r)), region(at + h * r, (h, r))
                at += 2 * h * r
                temps.append((a, b))
                nc.vector.tensor_tensor(a, view, cos.unsqueeze(1).to_broadcast([P, h, r]), ALU.mult)
                for lo in range(0, r, 2 * half):
                    mid, hi = lo + half, lo + 2 * half
                    nc.vector.tensor_tensor(b[:, :, lo:mid], view[:, :, mid:hi],
                                            sin[:, lo:mid].unsqueeze(1).to_broadcast([P, h, half]), ALU.mult)
                    last = nc.vector.tensor_tensor(b[:, :, mid:hi], view[:, :, lo:mid],
                                                   sin[:, mid:hi].unsqueeze(1).to_broadcast([P, h, half]), ALU.mult)
            step(v, last)
            for (view, _, _), (a, b) in zip(items, temps):
                last = nc.vector.tensor_tensor(view, a, b, ALU.add)
            if signal is None:
                step(v, last)
            else:
                last.then_inc(signal, 1)

        ropeA = cc("ropeA").rearrange("p (n t c) -> p n t c", n=2, t=NT)
        gate_u = uA[:, :, 2304:2560]
        gate_v = uA[:, :, 2560:2816]

        def a_mix_dve(v):
            split_proj(v, 1, "a_in", lambda c: uA[:, 1, c * 512:c * 512 + PROJ[PROJ_AT["a_in"][0] + c][4]])
            projected(v, "a_in")
            v.wait_ge(params_in, 16)
            for t in range(NT):
                rope(v, [(uA[:, t, 0:1536].rearrange("p (h c) -> p h c", c=HD)[:, :, 0:16], ropeA[:, 0, t, :],
                          ropeA[:, 1, t, :])], 8, turn_src if t else None)
            v.wait_ge(gelu_done, 1)
            v.wait_ge(turn_src, 1)
            sq = region(TMP, (NT, 256))
            step(v, nc.vector.tensor_tensor(sq, gate_v, gate_v, ALU.mult))
            step(v, nc.vector.tensor_reduce(stat[:, 80:88].rearrange("p (t g) -> p t g", t=NT),
                                            sq.rearrange("p t (g c) -> p t g c", g=4), AX.X, ALU.add))
            nc.vector.tensor_scalar(stat[:, 80:88], stat[:, 80:88], 1.0 / HD, EPS, ALU.mult,
                                    ALU.add).then_inc(power_in, 1)
            v.wait_ge(power_out, POWERS["gmlp"] + 1)
            for t in range(NT):
                gv = gate_v[:, t, :].rearrange("p (g c) -> p g c", g=4)
                last = nc.vector.tensor_tensor(gv, gv, stat[:, 104 + 4 * t:108 + 4 * t].unsqueeze(2)
                                               .to_broadcast([P, 4, HD]), ALU.mult)
            step(v, last)
            nc.vector.tensor_tensor(gate_v, gate_v, pc("gmlp").unsqueeze(1).to_broadcast([P, NT, 256]),
                                    ALU.mult).then_inc(gating_in, 1)
            turn_evac(v, 1, "a")
            v.wait_ge(gating_done, 1)
            for g in range(4):
                mixed = bank[0][:, :].rearrange("p (t c) -> p t c", t=NT)[:, :, g * HD:(g + 1) * HD]
                last = nc.vector.scalar_tensor_tensor(cat[:, :, 768 + g * HD:768 + (g + 1) * HD], mixed,
                                                      pc("bs")[:, g:g + 1], gate_u[:, :, g * HD:(g + 1) * HD],
                                                      ALU.add, ALU.mult)
            last.then_inc(turn_src, 1)
            attend_dve(v, "a")
            split_proj(v, 1, "a_out")
            residual_add(v, "a_out")

        def a_mix_act(act):
            split_proj(act, 0, "a_in", lambda c: uA[:, 0, c * 512:c * 512 + PROJ[PROJ_AT["a_in"][0] + c][4]])
            projected(act, "a_in")
            act.wait_ge(params_in, 16)
            nc.scalar.activation(uA[:, :, 2304:2816], uA[:, :, 2304:2816], ACT.Gelu_apprx_tanh).then_inc(gelu_done, 1)
            turn_evac(act, 0, "a")
            attend_act(act, "a")
            split_proj(act, 0, "a_out")

        def a_mix_pe(pe):
            split_proj_pe(pe, "a_in")
            pe.wait_ge(params_in, 16)
            pe.wait_ge(turn_src, 1)
            turn_pe(pe, "a")
            turns_out(pe, "a")
            pe.wait_ge(gating_in, 1)
            wsT = pc("wsT").rearrange("p (g q) -> p g q", g=4)
            for t in range(NT):
                for g in range(4):
                    mm = nc.tensor.matmul(bank[0][:, t * 256 + g * HD:t * 256 + (g + 1) * HD], wsT[:, g, :],
                                          gate_v[:, t, g * HD:(g + 1) * HD], start=True, stop=True)
            mm.then_inc(gating_done, 1)
            attend_pe(pe, "a")
            pe.wait_ge(turn_src, 2)
            pe.wait_ge(cat_done, HEAD_AT["a"] + A_HEADS)
            turn_pe(pe, "cat_a")
            split_proj_pe(pe, "a_out")

        ropeC = cc("ropeC").rearrange("p (n t c) -> p n t c", n=2, t=NT)
        ropeD = cc("ropeD").rearrange("p (n t c) -> p n t c", n=2, t=NT)

        def c_mix_dve(v):
            split_proj(v, 1, "c_in", lambda c: uC[:, 1, c * 512:c * 512 + PROJ[PROJ_AT["c_in"][0] + c][4]])
            projected(v, "c_in")
            sq = W[:, 6144:6144 + 2304].rearrange("p (t c) -> p t c", t=NT)
            step(v, nc.vector.tensor_tensor(sq[:, :, 0:384], uC[:, :, 0:384], uC[:, :, 0:384], ALU.mult))
            nc.vector.tensor_reduce(stat[:, 80:82], sq[:, :, 0:256], AX.X, ALU.add)
            step(v, nc.vector.tensor_reduce(stat[:, 82:84], sq[:, :, 256:384], AX.X, ALU.add))
            nc.vector.tensor_scalar(stat[:, 80:82], stat[:, 80:82], 1.0 / 256, EPS, ALU.mult, ALU.add)
            nc.vector.tensor_scalar(stat[:, 82:84], stat[:, 82:84], 1.0 / 128, EPS, ALU.mult,
                                    ALU.add).then_inc(power_in, 1)
            last = nc.vector.tensor_tensor(sq[:, :, 512:1152], uC[:, :, 512:1152], uC[:, :, 512:1152], ALU.mult)
            v.wait_ge(power_out, POWERS["latents"] + 1)
            for t in range(NT):
                nc.vector.tensor_scalar(uC[:, t, 0:256], uC[:, t, 0:256], stat[:, 104 + t:105 + t], None, ALU.mult)
                last = nc.vector.tensor_scalar(uC[:, t, 256:384], uC[:, t, 256:384], stat[:, 106 + t:107 + t], None,
                                               ALU.mult)
            last.then_inc(turn_src, 1)
            v.wait_ge(turn_src, 3)
            for t in range(NT):
                last = nc.vector.tensor_reduce(stat[:, 84 + 10 * t:94 + 10 * t],
                                               sq[:, t, 512:1152].rearrange("p (h c) -> p h c", c=HD), AX.X, ALU.add)
            step(v, last)
            nc.vector.tensor_scalar(stat[:, 84:104], stat[:, 84:104], 1.0 / HD, EPS, ALU.mult,
                                    ALU.add).then_inc(power_in, 1)
            turn_evac(v, 1, "c1")
            v.wait_ge(power_out, POWERS["heads"] + 1)
            for t in range(NT):
                dv = uC[:, t, 512:1152].rearrange("p (h c) -> p h c", c=HD)
                last = nc.vector.tensor_tensor(dv, dv, stat[:, 108 + 10 * t:118 + 10 * t].unsqueeze(2)
                                               .to_broadcast([P, 10, HD]), ALU.mult)
            step(v, last)
            step(v, nc.vector.tensor_tensor(uC[:, :, 512:1152], uC[:, :, 512:1152],
                                            pc("dgain").unsqueeze(1).to_broadcast([P, NT, 640]), ALU.mult))
            for t in range(NT):
                rope(v, [(uC[:, t, 512:1152].rearrange("p (h c) -> p h c", c=HD), ropeD[:, 0, t, :],
                          ropeD[:, 1, t, :])], 16, at=6144)
                for b in range(4):
                    last = nc.vector.tensor_copy(dkk[:, t, b, :], uC[:, t, 1024 + (b // 2) * HD:1088 + (b // 2) * HD])
            last.then_inc(turn_src, 1)
            turns_out(v, "c1")
            proj_copy(v, "c_up", 1, lambda c: (upq[:, 1, 0:512], upq[:, 1, 512:768], upkv[:, 1, 0:512],
                                               upkv[:, 1, 512:1024])[c])
            projected(v, "c_up")
            for t in range(NT):
                rope(v, [(upq[:, t, :].rearrange("p (h c) -> p h c", c=C_DIM)[:, :, HD:C_DIM], ropeC[:, 0, t, :],
                          ropeC[:, 1, t, :]),
                         (uC[:, t, 384:416].unsqueeze(1), ropeC[:, 0, t, :], ropeC[:, 1, t, :])], 16)
            for t in range(NT):
                nc.vector.tensor_copy(kc[:, t, :, 0:HD], upkv[:, t, :].rearrange("p (h c) -> p h c", h=8)[:, :, 0:HD])
                last = nc.vector.tensor_copy(kc[:, t, :, HD:C_DIM],
                                             uC[:, t, 384:416].unsqueeze(1).to_broadcast([P, C_HEADS, C_DIM - HD]))
            last.then_inc(turn_src, 1)
            turn_evac(v, 1, "c3")
            turn_evac(v, 1, "c2")
            attend_dve(v, "c")
            split_proj(v, 1, "c_out")
            residual_add(v, "c_out")

        def c_mix_act(act):
            split_proj(act, 0, "c_in", lambda c: uC[:, 0, c * 512:c * 512 + PROJ[PROJ_AT["c_in"][0] + c][4]])
            turn_evac(act, 0, "c1")
            proj_copy(act, "c_up", 0, lambda c: (upq[:, 0, 0:512], upq[:, 0, 512:768], upkv[:, 0, 0:512],
                                                 upkv[:, 0, 512:1024])[c])
            turn_evac(act, 0, "c3")
            turn_evac(act, 0, "c2")
            attend_act(act, "c")
            split_proj(act, 0, "c_out")

        def c_mix_pe(pe):
            split_proj_pe(pe, "c_in")
            pe.wait_ge(turn_src, 3)
            turn_pe(pe, "c1")
            turns_out(pe, "c1")
            proj_pe(pe, "c_up")
            projected(pe, "c_up")
            pe.wait_ge(turn_src, 4)
            turn_pe(pe, "c3")
            pe.wait_ge(turn_src, 5)
            turn_pe(pe, "c2")
            turns_out(pe, "c2")
            attend_pe(pe, "c")
            pe.wait_ge(cat_done, HEAD_AT["c"] + C_HEADS + G_HEADS)
            turn_pe(pe, "cat_c")
            split_proj_pe(pe, "c_out")

        router = pc("router").rearrange("p (l k e) -> p l k e", l=2, k=KD)
        iota = cc("iota")

        def moe_pe(pe, l, n0):
            q = 1 if l == 0 else 3
            s, a, d = 15 * l, 7 * l, 11 * l
            for t in range(NT):
                for k in range(KD):
                    mm = nc.tensor.matmul(bank[4][:, t * E:(t + 1) * E], hT[:, k, t * P:(t + 1) * P],
                                          router[:, l, k, :], start=(k == 0), stop=(k == KD - 1))
            mm.then_inc(route_pe, 1)
            pe.wait_ge(route_dve, d + 2)
            for t in range(NT):
                mm = nc.tensor.transpose(bank[5][0:E, t * P:(t + 1) * P], aff[:, t, :], ident)
            mm.then_inc(route_pe, 1)
            pe.wait_ge(route_dve, d + 3)
            for t in range(NT):
                mm = nc.tensor.transpose(bank[4][:, t * E:(t + 1) * E], placed[:, t * P:(t + 1) * P], ident[0:E, 0:E])
            mm.then_inc(route_pe, 1)
            pe.wait_ge(route_dve, d + 4)
            for k in range(KD):
                for t in range(NT):
                    mm = nc.tensor.matmul(bank[k // 4][:, (k % 4) * P:(k % 4 + 1) * P], xn[:, t, k * P:(k + 1) * P],
                                          pick[:, t, 0:P], start=(t == 0), stop=(t == NT - 1))
                if k % 4 == 3:
                    mm.then_inc(route_pe, 1)
            pe.wait_ge(route_act, a + 2)
            pe.wait_ge(route_dve, d + 5)

            def others():
                for k in range(KD):
                    if k >= 4:
                        pe.wait_ge(*((route_act, a + 3 + (k - 4) // 2) if k % 2 == 0
                                     else (route_dve, d + 7 + (k - 4) // 2)))
                    for t in range(NT):
                        mm = nc.tensor.matmul(bank[k % 4][:, P:4 * P], xn[:, t, k * P:(k + 1) * P], pick[:, t, P:4 * P],
                                              start=(t == 0), stop=(t == NT - 1))
                    mm.then_inc(route_pe, 1)
                pe.wait_ge(route_dve, d + 6)
                for b in range(2):
                    pe.wait_ge(*((route_dve, d + 9) if b else (route_act, a + 5)))
                    for gg in range(2):
                        for t in range(NT):
                            mm = nc.tensor.transpose(bank[b][:, gg * T + t * P:gg * T + (t + 1) * P],
                                                     pickg[:, t, (2 * b + gg) * P:(2 * b + gg + 1) * P], ident)
                    mm.then_inc(route_pe, 1)

            def group(g, first):
                seen = 4 * l + g
                for e in range(GRP):
                    na, nb, nd = n0 + 3 * e, n0 + 3 * e + 1, n0 + 3 * e + 2
                    for half, n in enumerate((na, nb)):
                        pe.wait_ge(slot_in[n % RING], 16 * (n // RING + 1) + 32 * g)
                        w = slot(n).rearrange("p (k m c) -> p k m c", k=4, m=2)
                        for kk in range(4):
                            for j in range(4):
                                mm = nc.tensor.matmul(bank[4 + e % 2][32 * j:32 * j + 32, 0:256],
                                                      hcur[:, 4 * half + kk, e * CAP:(e + 1) * CAP],
                                                      w[:, kk, :, j * P:(j + 1) * P],
                                                      start=(half == 0 and kk == 0), stop=(half == 1 and kk == 3),
                                                      skip_group_check=True)
                        if half == 0:
                            release(mm, na)
                        else:
                            mm.then_inc(expert_gu, 1)
                    pe.wait_ge(expert_act, 4 * seen + e + 1)
                    nc.tensor.transpose(bank[6][:, 0:P], act_e[:, e % 2, :], ident).then_inc(expert_turned, 1)
                    pe.wait_ge(expert_actT, 4 * seen + e + 1)
                    pe.wait_ge(slot_in[nd % RING], 16 * (nd // RING + 1) + 32 * g)
                    if e >= 1:
                        pe.wait_ge(y_out[0], 4 * seen + e)
                        pe.wait_ge(y_out[1], 4 * seen + e)
                    w = slot(nd).rearrange("p (j c) -> p j c", j=4)
                    for j in range(4):
                        for i in range(4):
                            mm = nc.tensor.matmul(bank[7][32 * i:32 * i + 32, 0:256],
                                                  actT_e[:, e % 2, j * CAP:(j + 1) * CAP],
                                                  w[:, j, i * 256:(i + 1) * 256], start=(j == 0), stop=(j == 3),
                                                  skip_group_check=True)
                            if j == 0 and i == 0:
                                release(mm, nb)
                    release(mm, nd)
                    if first and e == 1:
                        others()
                if first:
                    pe.wait_ge(route_act, a + 7)
                    pe.wait_ge(route_dve, d + 11)
                pe.wait_ge(y_out[0], 4 * seen + 4)
                pe.wait_ge(y_out[1], 4 * seen + 4)
                for t in range(NT):
                    for half in range(2):
                        mm = nc.tensor.matmul(bank[2 * t + half][:, :], pcur[:, t * P:(t + 1) * P],
                                              ybuf[:, half * 512:(half + 1) * 512], start=True, stop=True)
                mm.then_inc(scattered, 1)

            group(0, True)
            with pe.Fori(1, E // GRP) as g:
                pe.wait_ge(staged, 3 * l + g)
                group(g, False)

        def moe_act(act, l, n0):
            q = 1 if l == 0 else 3
            s, d = 15 * l, 11 * l
            act.wait_ge(route_dve, d + 1)
            for t in range(NT):
                last = nc.scalar.activation(aff[:, t, :], bank[4][:, t * E:(t + 1) * E], ACT.Exp,
                                            bias=stat[:, 72 + t:73 + t], accum_out=stat[:, 74 + t:75 + t])
            last.then_inc(route_act, 1)
            act.wait_ge(route_pe, s + 4)
            for k in range(4):
                last = nc.scalar.activation(hcur[:, k, :], bank[0][:, k * P:(k + 1) * P], ACT.Copy,
                                            scale=gains[:, q, k:k + 1])
            last.then_inc(route_act, 1)

            def others():
                for k in range(0, KD, 2):
                    act.wait_ge(route_pe, s + 6 + k)
                    nc.scalar.activation(hsel[:, 1:GRP, k, :], bank[k % 4][:, P:].rearrange("p (g c) -> p g c", g=GRP - 1),
                                         ACT.Copy, scale=gains[:, q, k:k + 1]).then_inc(route_act, 1)
                act.wait_ge(route_pe, s + 14)
                nc.scalar.activation(pcur, bank[0][:, 0:T], ACT.Copy)
                nc.scalar.activation(putT[:, 1, :], bank[0][:, T:2 * T], ACT.Copy).then_inc(route_act, 1)

            def group(g, first):
                seen = 4 * l + g
                for e in range(GRP):
                    nd = n0 + 3 * e + 2
                    act.wait_ge(expert_gu, 4 * seen + e + 1)
                    nc.scalar.activation(silu_e[:, e % 2, :], bank[4 + e % 2][:, 0:P], ACT.Silu).then_inc(expert_silu, 1)
                    if e == 0:
                        act.wait_ge(scattered, seen + 1)
                    act.wait_ge(slot_used[nd % RING], nd // RING + 1 + 2 * g)
                    for i in range(2):
                        last = nc.scalar.activation(ybuf[32 * e:32 * e + 32, i * 256:(i + 1) * 256],
                                                    bank[7][32 * i:32 * i + 32, 0:256], ACT.Copy)
                    last.then_inc(y_out[0], 1)
                    if first and e == 1:
                        others()

            group(0, True)
            with act.Fori(1, E // GRP) as g:
                group(g, False)

        def moe_dve(v, l, n0):
            q = 1 if l == 0 else 3
            s, a = 15 * l, 7 * l
            v.wait_ge(route_pe, s + 1)
            nc.vector.tensor_reduce(stat[:, 72:74], bank[4][:, 0:NT * E].rearrange("p (t e) -> p t e", t=NT), AX.X,
                                    ALU.max, negate=True).then_inc(route_dve, 1)
            v.wait_ge(route_act, a + 1)
            step(v, nc.vector.reciprocal(stat[:, 76:78], stat[:, 74:76]))
            nc.vector.tensor_tensor(aff, aff, stat[:, 76:78].unsqueeze(2).to_broadcast([P, NT, E]),
                                    ALU.mult).then_inc(route_dve, 1)
            v.wait_ge(route_pe, s + 2)
            step(v, nc.vector.tensor_copy(scan_a, bank[5][0:E, 0:T]))
            src, dst = scan_a, scan_b
            for _ in range(CAP // 8):
                step(v, nc.vector.max(top8, src))
                step(v, nc.vector.match_replace(dst, top8, src, -1.0))
                src, dst = dst, src
            step(v, nc.vector.tensor_scalar(chosen, src, -1.0, None, ALU.is_equal))
            step(v, nc.vector.tensor_tensor_scan(dst, ones[:, :], chosen, 0.0, ALU.mult, ALU.add))
            step(v, nc.vector.tensor_tensor(placed, dst, chosen, ALU.mult))
            nc.vector.tensor_scalar(placed, placed, -1.0, None, ALU.add).then_inc(route_dve, 1)
            v.wait_ge(route_pe, s + 3)
            step(v, nc.vector.tensor_copy(posT.rearrange("p t e -> p (t e)"), bank[4][:, 0:NT * E]))
            for t in range(NT):
                last = nc.vector.tensor_tensor(pick[:, t, :].rearrange("p (e c) -> p e c", e=E),
                                               iota.unsqueeze(1).to_broadcast([P, E, CAP]),
                                               posT[:, t, :].unsqueeze(2).to_broadcast([P, E, CAP]), ALU.is_equal)
            last.then_inc(route_dve, 1)
            v.wait_ge(route_pe, s + 5)
            for k in range(4, KD):
                last = nc.vector.tensor_scalar(hcur[:, k, :], bank[1][:, (k - 4) * P:(k - 3) * P], gains[:, q, k:k + 1],
                                               None, ALU.mult)
            last.then_inc(route_dve, 1)
            v.wait_ge(route_dve, 11 * l + 4)
            for t in range(NT):
                last = nc.vector.tensor_tensor(pickg[:, t, :].rearrange("p (e c) -> p e c", e=E),
                                               pick[:, t, :].rearrange("p (e c) -> p e c", e=E),
                                               aff[:, t, :].unsqueeze(2).to_broadcast([P, E, CAP]), ALU.mult)
            last.then_inc(route_dve, 1)

            def others():
                for k in range(1, KD, 2):
                    v.wait_ge(route_pe, s + 6 + k)
                    nc.vector.tensor_scalar(hsel[:, 1:GRP, k, :],
                                            bank[k % 4][:, P:].rearrange("p (g c) -> p g c", g=GRP - 1),
                                            gains[:, q, k:k + 1], None, ALU.mult).then_inc(route_dve, 1)
                v.wait_ge(route_pe, s + 15)
                nc.vector.tensor_copy(putT[:, 2:4, :].rearrange("p a b -> p (a b)"),
                                      bank[1][:, :]).then_inc(route_dve, 1)

            def group(g, first):
                seen = 4 * l + g
                for e in range(GRP):
                    nd = n0 + 3 * e + 2
                    v.wait_ge(expert_silu, 4 * seen + e + 1)
                    nc.vector.tensor_tensor(act_e[:, e % 2, :], silu_e[:, e % 2, :], bank[4 + e % 2][:, P:2 * P],
                                            ALU.mult).then_inc(expert_act, 1)
                    v.wait_ge(expert_turned, 4 * seen + e + 1)
                    nc.vector.tensor_copy(actT_e[:, e % 2, :], bank[6][:, 0:P]).then_inc(expert_actT, 1)
                    if e == 0:
                        v.wait_ge(scattered, seen + 1)
                    v.wait_ge(slot_used[nd % RING], nd // RING + 1 + 2 * g)
                    for i in range(2, 4):
                        last = nc.vector.tensor_copy(ybuf[32 * e:32 * e + 32, i * 256:(i + 1) * 256],
                                                     bank[7][32 * i:32 * i + 32, 0:256])
                    last.then_inc(y_out[1], 1)
                    if first and e == 1:
                        others()
                v.wait_ge(scattered, seen + 2)
                for t in range(NT):
                    for half in range(2):
                        xs = x[:, t, half * 512:(half + 1) * 512]
                        last = nc.vector.tensor_tensor(xs, bank[2 * t + half][:, :], xs, ALU.add)
                last.then_inc(scatter_added, 1)

            group(0, True)
            with v.Fori(1, E // GRP) as g:
                group(g, False)

        def moe_pool(pool, l):
            pool.wait_ge(route_act, 7 * l + 7)
            pool.wait_ge(route_dve, 11 * l + 11)
            with pool.Fori(1, E // GRP) as g:
                pool.wait_ge(scattered, 4 * l + g + 1)
                nc.gpsimd.tensor_copy(hcur.rearrange("p k c -> p (k c)"), W[:, bass.ds(g * (KD * P), KD * P)])
                nc.gpsimd.tensor_copy(pcur, W[:, bass.ds(g * T + 6144, T)]).then_inc(staged, 1)

        FFN_TURNS = {"ffn0": "n4", "ffn1": "n6", "ffn2": "n7", "ffn3": "n9"}

        def ffn_pe(pe, i):
            base, name = FT * i, f"ffn{i}"
            turns = TURN_AT[FFN_TURNS[name]][0]

            def hidden(f, u, at, it):
                out = bank[4 + f % 4][:, at:at + T]
                high = unit_hi[:, u % SPLIT, :].rearrange("p (k c) -> p k c", k=KD)
                low = unit_lo[:, u % SPLIT, :].rearrange("p (k c) -> p k c", k=KD)
                high_ready(pe, name, u, it)
                for k in range(KD):
                    if u == 0 and k % 2 == 0:
                        pe.wait_ge(*TURN_DONE[turns + k // 2])
                    nc.tensor.matmul(out, high[:, k, :], hT_hi[:, k, :], start=(k == 0), stop=False)
                    nc.tensor.matmul(out, high[:, k, :], norm_lo[:, k, :], start=False, stop=False)
                low_ready(pe, name, u, it)
                for k in range(KD):
                    mm = nc.tensor.matmul(out, low[:, k, :], hT_hi[:, k, :], start=False, stop=(k == KD - 1))
                mm.then_inc(unit_used, 1)

            def gate_up(f, it=0):
                if f >= 4:
                    pe.wait_ge(ffn_act, base + f - 3 + PASS * it)
                hidden(f, gate_unit(f), 0, it)
                hidden(f, up_unit(f), T, it)

            def down(f, it=0):
                u = down_unit(f)
                high_ready(pe, name, u, it)
                pe.wait_ge(ffn_act, base + f + 1 + PASS * it)
                if f == FT - 1:
                    low_ready(pe, name, u, it)
                    for j in range(4):
                        t, half = j // 2, j % 2
                        for left, right in ((act_hi, unit_hi), (act_lo, unit_hi), (act_hi, unit_lo)):
                            mm = nc.tensor.matmul(bank[j][:, :], left[:, f % 2, t * P:(t + 1) * P],
                                                  right[:, u % SPLIT, half * 512:(half + 1) * 512], start=False,
                                                  stop=(right is unit_lo), skip_group_check=True)
                        if j == 1:
                            mm.then_inc(tail_done, 1)
                    mm.then_inc(unit_used, 1)
                    return
                for j in range(4):
                    t, half = j // 2, j % 2
                    for left in (act_hi, act_lo):
                        nc.tensor.matmul(bank[j][:, :], left[:, f % 2, t * P:(t + 1) * P],
                                         unit_hi[:, u % SPLIT, half * 512:(half + 1) * 512],
                                         start=(f == 0 and left is act_hi), stop=False, skip_group_check=True)
                low_ready(pe, name, u, it)
                for j in range(4):
                    t, half = j // 2, j % 2
                    mm = nc.tensor.matmul(bank[j][:, :], act_hi[:, f % 2, t * P:(t + 1) * P],
                                          unit_lo[:, u % SPLIT, half * 512:(half + 1) * 512], start=False,
                                          stop=False, skip_group_check=True)
                mm.then_inc(unit_used, 1)

            gate_up(0)
            gate_up(1)
            down(0)
            with pe.Fori(0, 2) as it:
                for f in range(2, 2 + PASS):
                    gate_up(f, it)
                    down(f - 1, it)
            for f in range(2 + 2 * PASS, FT):
                gate_up(f)
                down(f - 1)
            down(FT - 1)

        def ffn_act_engine(act, i):
            base, name = FT * i, f"ffn{i}"

            def tile(f, it=0):
                if f + 1 < FT:
                    split_high(act, name, gate_unit(f + 1), it)
                    split_high(act, name, up_unit(f + 1), it)
                split_high(act, name, down_unit(f), it)
                act.wait_ge(unit_used, UNIT_BASE[name] + up_unit(f) + 1 + PASS_UNITS * it)
                if f >= 2:
                    act.wait_ge(ffn_act, base + f - 1 + PASS * it)
                nc.scalar.activation(silu_f[:, f % 2, :], bank[4 + f % 4][:, 0:T], ACT.Silu).then_inc(ffn_silu, 1)

            for j in range(4):
                split_evac(act, 0, FFN_TURNS[name], j)
            tile(0)
            tile(1)
            with act.Fori(0, 2) as it:
                for f in range(2, 2 + PASS):
                    tile(f, it)
            for f in range(2 + 2 * PASS, FT):
                tile(f)

        def ffn_dve(v, i):
            base, name = FT * i, f"ffn{i}"

            def tile(f, it=0):
                if f + 1 < FT:
                    split_low(v, name, gate_unit(f + 1), it)
                    split_low(v, name, up_unit(f + 1), it)
                split_low(v, name, down_unit(f), it)
                v.wait_ge(ffn_silu, base + f + 1 + PASS * it)
                if f >= 2:
                    v.wait_ge(unit_used, UNIT_BASE[name] + down_unit(f - 2) + 1 + PASS_UNITS * it)
                up = bank[4 + f % 4][:, T:2 * T]
                nc.vector.tensor_tensor(act_f[:, f % 2, :], silu_f[:, f % 2, :], up, ALU.mult).then_inc(ffn_product, 1)
                nc.vector.tensor_tensor(act_hi[:, f % 2, :], silu_f[:, f % 2, :], up, ALU.mult).then_inc(ffn_product, 1)
                v.wait_ge(ffn_product, 2 * (base + f + 1) + 2 * PASS * it)
                nc.vector.tensor_tensor(act_lo[:, f % 2, :], act_f[:, f % 2, :], act_hi[:, f % 2, :].bitcast(F32),
                                        ALU.subtract).then_inc(ffn_act, 1)

            for j in range(4):
                split_evac(v, 1, FFN_TURNS[name], j)
            tile(0)
            tile(1)
            with v.Fori(0, 2) as it:
                for f in range(2, 2 + PASS):
                    tile(f, it)
            for f in range(2 + 2 * PASS, FT):
                tile(f)
            for t in range(NT):
                if t == 0:
                    v.wait_ge(tail_done, TAILS.index(name) + 1)
                else:
                    v.wait_ge(unit_used, UNIT_BASE[name] + UNITS)
                for half in range(2):
                    xs = x[:, t, half * 512:(half + 1) * 512]
                    last = nc.vector.scalar_tensor_tensor(xs, bank[2 * t + half][:, :], 0.5, xs, ALU.mult, ALU.add)
                last.then_inc(x_ready if t else x_half, 1)

        conv_bank = [bank[(TURN_AT["cat_s"][0] + 2 + t) % 4] for t in range(NT)]
        TAPS = [(j, 2 * pair + c) for pair in range(2) for j in range(KW) for c in range(2)]

        def s_mix_pe(pe):
            n0 = START["s_in"]
            pe.wait_ge(bucket_in, 32)
            nc.tensor.matmul(bank[0][0:8, :], pc("relb")[0:32, :], onehot, start=True, stop=True).then_inc(spread_done, 1)
            places = [(n0, 0, P), (n0, 2 * P, 3 * P), (n0 + 1, 0, P), (n0 + 1, 2 * P, 3 * P)]
            for c, (n, av, ag) in enumerate(places):
                if c % 2 == 0:
                    loaded(pe, n)
                w = slot(n).rearrange("p (k c) -> p k c", k=KD)
                for at, col in ((0, av), (T, ag)):
                    for k in range(KD):
                        mm = nc.tensor.matmul(bank[4 + c][:, at:at + T], w[:, k, col:col + P], hT[:, k, :],
                                              start=(k == 0), stop=(k == KD - 1))
                if c % 2 == 0:
                    mm.then_inc(wide_done, 1)
                else:
                    release(mm, n)
            pe.wait_ge(spread_ready, 1)
            proj_pe(pe, "s_in")
            pe.wait_ge(rows_in, 32)
            pe.wait_ge(wide_act, 4)
            pe.wait_ge(wide_dve, 4)
            for h in range(S_HEADS):
                ge(pe, bias_out, h - 3)
                nc.tensor.matmul(bank[4 + h % 4][:, :], flip, rows_s[:, h, :], start=True,
                                 stop=True).then_inc(bias_done, 1)
            pe.wait_ge(turn_src, 6)
            turn_pe(pe, "s1")
            turns_out(pe, "s1")
            pe.wait_ge(bias_out, S_HEADS)
            attend_pe(pe, "s")
            pe.wait_ge(conv_done, 1)
            for t in range(NT):
                for c in range(4):
                    mm = nc.tensor.transpose(conv_bank[t][:, c * P:(c + 1) * P], conv_s[c][:, t * P:(t + 1) * P], ident)
            mm.then_inc(conv_turned, 1)
            pe.wait_ge(cat_done, HEAD_AT["s"] + S_HEADS)
            turn_pe(pe, "cat_s", 0, 2)
            pe.wait_ge(conv_cat, 1)
            turn_pe(pe, "cat_s", 2, 4)
            split_proj_pe(pe, "s_out")

        def s_mix_act(act):
            n0 = START["s_in"]
            act.wait_ge(spread_ready, 1)
            act.dma_start(spread.ap(), spread_sb).then_inc(spread_out, 16)
            act.wait_ge(spread_out, 16)
            for t in range(NT):
                src = bass.AP(tensor=spread, offset=P - P * t, ap=[[1, P], [SPAN, S_HEADS], [1, T]])
                act.dma_start(rows_s[:, :, t * T:(t + 1) * T], src).then_inc(rows_in, 16)
            for c in range(4):
                if c % 2 == 0:
                    act.wait_ge(wide_done, 1 + c // 2)
                else:
                    used(act, n0 + c // 2)
                ge(act, wide_dve, c - 1)
                nc.scalar.activation(gate_s[:, c % 2, :], bank[4 + c][:, T:2 * T], ACT.Sigmoid).then_inc(wide_act, 1)
            proj_copy(act, "s_in", 0, lambda c: (uS[:, 0, 0:512], uS[:, 0, 512:768])[c])
            for h in range(S_HEADS):
                act.wait_ge(bias_done, h + 1)
                nc.scalar.activation(bias_s[:, h, :], bank[4 + h % 4][:, :], ACT.Copy).then_inc(bias_out, 1)
            turn_evac(act, 0, "s1")
            attend_act(act, "s")

            def conv_silu():
                act.wait_ge(ln_done, 1)
                nc.scalar.activation(cat[:, :, 512:1024], cat[:, :, 512:1024], ACT.Silu).then_inc(conv_cat, 1)

            split_proj(act, 0, "s_out", midway=conv_silu)

        def s_mix_dve(v):
            v.wait_ge(x_ready, 4)
            step(v, nc.vector.tensor_scalar(stat[:, SINK_NEG:SINK_NEG + 8], pc("sinks"), -1.0, None, ALU.mult))
            nc.vector.memset(gluf, 0.0)
            v.wait_ge(spread_done, 1)
            v.wait_ge(bucket_in, 32)
            nc.vector.tensor_tensor(spread_sb, bank[0][0:8, :], off_mask, ALU.add).then_inc(spread_ready, 1)

            def gated(c):
                v.wait_ge(wide_act, c + 1)
                nc.vector.tensor_tensor(glu[:, c, KW - 1:], gate_s[:, c % 2, :], bank[4 + c][:, 0:T],
                                        ALU.mult).then_inc(wide_dve, 1)

            convw = pc("convw").rearrange("p (c j) -> p c j", c=4)

            def taps(first, end):
                for i in range(first, end):
                    j, c = TAPS[i]
                    g = glu[:, c, j:j + T]
                    if j == 0:
                        v.wait_ge(wide_dve, c + 1)
                        tap = nc.vector.tensor_scalar(conv_s[c], g, convw[:, c, 0:1], pc("convb")[:, c:c + 1],
                                                      ALU.mult, ALU.add)
                    else:
                        v.wait_ge(tap_done, i - 1)
                        tap = nc.vector.scalar_tensor_tensor(conv_s[c], g, convw[:, c, j:j + 1], conv_s[c],
                                                             ALU.mult, ALU.add)
                    tap.then_inc(conv_done if i == 4 * KW - 1 else tap_done, 1)

            gated(0)
            gated(1)
            taps(0, 28)
            gated(2)
            gated(3)
            taps(28, 84)
            proj_copy(v, "s_in", 1, lambda c: (uS[:, 1, 0:512], uS[:, 1, 512:768])[c])
            projected(v, "s_in")
            for t in range(NT):
                for b in range(4):
                    last = nc.vector.tensor_copy(dkk[:, t, b, :], uS[:, t, 512 + (b // 2) * HD:576 + (b // 2) * HD])
            last.then_inc(turn_src, 1)
            taps(84, 104)
            turn_evac(v, 1, "s1")
            attend_dve(v, "s", lambda i: taps(104 + 2 * i, min(106 + 2 * i, 4 * KW)))
            v.wait_ge(conv_turned, 1)
            for t in range(NT):
                last = nc.vector.bn_stats(stat[:, 136 + 6 * t:142 + 6 * t], conv_bank[t][:, :])
            step(v, last)
            for t in range(NT):
                last = nc.vector.bn_aggr(stat[:, 148 + 2 * t:150 + 2 * t], stat[:, 136 + 6 * t:142 + 6 * t])
            step(v, last)
            nc.vector.tensor_scalar(stat[:, 80:84], stat[:, 148:152], LN_EPS, None, ALU.add).then_inc(power_in, 1)
            v.wait_ge(power_out, POWERS["ln"] + 1)
            ct = cat[:, :, 512:1024]
            for t in range(NT):
                last = nc.vector.tensor_scalar(ct[:, t, :], conv_bank[t][:, :], stat[:, 148 + 2 * t:149 + 2 * t],
                                               stat[:, 105 + 2 * t:106 + 2 * t], ALU.subtract, ALU.mult)
            step(v, last)
            step(v, nc.vector.tensor_tensor(ct, ct, pc("lng").unsqueeze(1).to_broadcast([P, NT, 512]), ALU.mult))
            nc.vector.tensor_tensor(ct, ct, pc("lnb").unsqueeze(1).to_broadcast([P, NT, 512]), ALU.add)\
                .then_inc(ln_done, 1)
            split_proj(v, 1, "s_out")
            residual_add(v, "s_out")

        gab, gxb, lam = pc("gab"), pc("gxb"), pc("lam")
        rconvw = pc("rconvw").rearrange("p (k j) -> p k j", k=KD)
        C8 = 160

        def r_mix_pe(pe):
            n0 = START["r_in"]
            def halves(g):
                n = n0 + g // 2
                if g % 2 == 0:
                    loaded(pe, n)
                if g >= 4:
                    pe.wait_ge(rec_in, g - 3)
                w = slot(n).rearrange("p (k c) -> p k c", k=KD)
                for i in range(2):
                    col = (g % 2) * 256 + i * P
                    for k in range(KD):
                        mm = nc.tensor.matmul(bank[g % 4][:, i * T:(i + 1) * T], w[:, k, col:col + P], hT[:, k, :],
                                              start=(k == 0), stop=(k == KD - 1))
                if g % 2:
                    release(mm, n)
                else:
                    mm.then_inc(wide_done, 1)

            for g in range(6):
                halves(g)
            n = START["r_gate"]
            loaded(pe, n)
            for h in range(KD):
                pe.wait_ge(rec_done, h + 1)
                if h >= 4:
                    pe.wait_ge(rec_act, h - 1)
                for m in range(2):
                    mm = nc.tensor.matmul(bank[4 + h % 4][:, m * T:(m + 1) * T],
                                          slot(n)[:, (m * KD + h) * P:(m * KD + h + 1) * P], rec[:, h, :],
                                          start=True, stop=True)
                if h == KD - 1:
                    release(mm, n)
                else:
                    mm.then_inc(rec_gates, 1)
            for g in range(6, 8):
                halves(g)
            split_proj_pe(pe, "r_out")

        def r_mix_act(act):
            n0 = START["r_in"]
            act.wait_ge(rec_dve, 1)
            nc.scalar.activation(stat[:, 176:184], stat[:, 168:176], ACT.Exp).then_inc(rec_act, 1)
            act.wait_ge(rec_dve, 2)
            nc.scalar.activation(stat[:, 192:200], stat[:, 184:192], ACT.Ln).then_inc(rec_act, 1)

            for g in range(2):
                r_gelu_act(act, g)

        def r_gelu_act(act, g):
            if g % 2:
                used(act, START["r_in"] + 2 + g // 2)
            else:
                act.wait_ge(wide_done, 5 + g // 2)
            nc.scalar.activation(gate_r[:, 2 * g:2 * g + 2, :].rearrange("p a b -> p (a b)"), bank[g][:, :],
                                 ACT.Gelu_apprx_tanh).then_inc(wide_act, 1)

        def r_gates_act(act):
            for h in range(KD):
                if h == KD - 1:
                    used(act, START["r_gate"])
                else:
                    act.wait_ge(rec_gates, h + 1)
                nc.scalar.activation(dec[:, h, :], bank[4 + h % 4][:, 0:T], ACT.Sigmoid, bias=gab[:, h:h + 1])
                nc.scalar.activation(inp[:, h, :], bank[4 + h % 4][:, T:2 * T], ACT.Sigmoid,
                                     bias=gxb[:, h:h + 1]).then_inc(rec_act, 1)
            act.wait_ge(rec_dve, 3)
            nc.scalar.activation(tnh, dec, ACT.Tanh).then_inc(rec_act, 1)
            act.wait_ge(rec_act, 11)
            nc.scalar.activation(dec, dec, ACT.Exp).then_inc(rec_act, 1)
            act.wait_ge(rec_act, 12)
            nc.scalar.activation(spare, dec, ACT.Square).then_inc(rec_act, 1)
            act.wait_ge(rec_dve, 4)
            nc.scalar.activation(tnh, tnh, ACT.Sqrt, scale=-1.0).then_inc(rec_act, 1)
            for g in range(2, 4):
                r_gelu_act(act, g)
            for j in range(4):
                if j < 2:
                    split_high(act, "r_out", j)
                act.wait_ge(rec_out, j + 1)
                nc.scalar.activation(hT_hi[:, 2 * j:2 * j + 2, :], tnh[:, 2 * j:2 * j + 2, :], ACT.Copy).then_inc(rec_hi, 1)
            for u in range(2, 8):
                split_high(act, "r_out", u)

        def r_mix_dve(v):
            n0 = START["r_in"]
            v.wait_ge(x_ready, 7)
            e, u, ln, d, z = stat[:, 176:184], stat[:, 184:192], stat[:, 192:200], stat[:, 200:208], stat[:, 208:216]
            step(v, nc.vector.tensor_scalar(d, lam, -1.0, None, ALU.mult))
            nc.vector.tensor_tensor(stat[:, 168:176], d, lam, ALU.min).then_inc(rec_dve, 1)
            v.wait_ge(rec_act, 1)
            nc.vector.tensor_scalar(u, e, 1.0, None, ALU.add).then_inc(rec_dve, 1)
            v.wait_ge(rec_dve, 2)
            step(v, nc.vector.tensor_scalar(d, u, 1.0, None, ALU.subtract))
            step(v, nc.vector.tensor_scalar(z, d, 0.0, None, ALU.is_equal))
            step(v, nc.vector.tensor_tensor(d, d, z, ALU.add))
            step(v, nc.vector.reciprocal(d, d))
            step(v, nc.vector.tensor_tensor(d, d, e, ALU.mult))
            v.wait_ge(rec_act, 2)
            step(v, nc.vector.tensor_tensor(d, d, ln, ALU.mult))
            step(v, nc.vector.tensor_tensor(z, z, e, ALU.mult))
            step(v, nc.vector.tensor_tensor(d, d, z, ALU.add))
            step(v, nc.vector.tensor_scalar(z, lam, 0.0, None, ALU.min))
            step(v, nc.vector.tensor_tensor(z, z, d, ALU.subtract))
            nc.vector.tensor_scalar(stat[:, C8:C8 + 8], z, 8.0, None, ALU.mult)
            step(v, nc.vector.memset(pad_rf, 0.0))
            base = 4 * KW - 1
            for g in range(4):
                if g % 2:
                    used(v, n0 + g // 2)
                else:
                    v.wait_ge(wide_done, 3 + g // 2)
                nc.vector.tensor_copy(pad_r[:, 2 * g:2 * g + 2, LW - 1:],
                                      bank[g][:, :].rearrange("p (a b) -> p a b", a=2)).then_inc(rec_in, 1)
                v.wait_ge(rec_in, g + 1)
                for i in range(2 * LW):
                    j, k = i // 2, 2 * g + i % 2
                    src = pad_r[:, k, j:j + T]
                    if j == 0:
                        tap = nc.vector.tensor_scalar(rec[:, k, :], src, rconvw[:, k, 0:1],
                                                      pc("rconvb")[:, k:k + 1], ALU.mult, ALU.add)
                    else:
                        v.wait_ge(tap_done, base + 2 * (LW - 1) * g + i - 1)
                        tap = nc.vector.scalar_tensor_tensor(rec[:, k, :], src, rconvw[:, k, j:j + 1], rec[:, k, :],
                                                             ALU.mult, ALU.add)
                    tap.then_inc(rec_done if j == LW - 1 else tap_done, 1)
            v.wait_ge(rec_act, 10)
            for k in range(KD):
                last = nc.vector.tensor_scalar(dec[:, k, :], dec[:, k, :], stat[:, C8 + k:C8 + k + 1], None, ALU.mult)
            last.then_inc(rec_dve, 1)
            v.wait_ge(rec_done, 8)
            step(v, nc.vector.tensor_tensor(inp, inp, rec, ALU.mult))
            v.wait_ge(rec_act, 11)
            step(v, nc.vector.tensor_scalar(tnh, tnh, -1.3e-35, None, ALU.min))
            v.wait_ge(rec_act, 13)
            nc.vector.scalar_tensor_tensor(tnh, spare, 1.0, tnh, ALU.add, ALU.mult).then_inc(rec_dve, 1)
            v.wait_ge(rec_act, 14)

            def output(j):
                two = slice(2 * j, 2 * j + 2)
                step(v, nc.vector.tensor_tensor(tnh[:, two, :], tnh[:, two, :], inp[:, two, :], ALU.mult))
                for k in range(2 * j, 2 * j + 2):
                    last = nc.vector.tensor_tensor_scan(rec[:, k, :], dec[:, k, :], tnh[:, k, :], 0.0, ALU.mult, ALU.add)
                step(v, last)
                v.wait_ge(wide_act, 5 + j)
                nc.vector.tensor_tensor(tnh[:, two, :], rec[:, two, :], gate_r[:, two, :], ALU.mult).then_inc(rec_out, 1)

            def output_low(j):
                two = slice(2 * j, 2 * j + 2)
                v.wait_ge(rec_hi, j + 1)
                nc.vector.tensor_tensor(cat_lo[:, two, :], tnh[:, two, :], hT_hi[:, two, :].bitcast(F32),
                                        ALU.subtract).then_inc(rec_lo, 1)

            output(0)
            split_low(v, "r_out", 0)
            output_low(0)
            output(1)
            split_low(v, "r_out", 1)
            output_low(1)
            output(2)
            output(3)
            output_low(2)
            output_low(3)
            for u in range(2, 8):
                split_low(v, "r_out", u)
            residual_add(v, "r_out")

        block = ctx.enter_context(nc.Block())

        @block.sync
        def _(sp):
            sp.dma_start(x[:, :, :], x_in.rearrange("(t p) d -> p t d", p=P)).then_inc(x_loaded, 16)
            sp.dma_start(con[:, :], consts).then_inc(const_in, 16)
            first = PCOL["gains"][1]
            sp.dma_start(par[:, 0:first], params[:, 0:first]).then_inc(const_in, 16)
            for s in range(RING):
                if s == 2:
                    sp.dma_start(par[:, first:], params[:, first:]).then_inc(params_in, 16)
                sp.dma_start(ring[:, s, :], stream[s, :, :]).then_inc(slot_in[s], 16)
            turns = N_SLOTS // RING
            with sp.Fori(1, turns) as r:
                for s in range(RING):
                    sp.wait_ge(slot_used[s], r)
                    sp.dma_start(ring[:, s, :], stream[bass.ds(r * RING + s, 1), :, :]
                                 .rearrange("a p n -> (a p) n")).then_inc(slot_in[s], 16)
            for n in range(turns * RING, N_SLOTS):
                sp.wait_ge(slot_used[n % RING], n // RING)
                sp.dma_start(ring[:, n % RING, :], stream[n, :, :]).then_inc(slot_in[n % RING], 16)
            for t, (signal, value) in enumerate(((x_half, 8), (x_ready, 10))):
                sp.wait_ge(signal, value)
                sp.dma_start(out[t * P:(t + 1) * P, :], x[:, t, :]).then_inc(stored, 16)
            sp.wait_ge(stored, 16 * NT)

        @block.scalar
        def _(act):
            def norm(p, q):
                norm_act(act, p, f"n{q}")
                if f"n{q}" not in SPLIT_TURNS:
                    turn_evac(act, 0, f"n{q}")

            norm(0, 0)
            act.wait_ge(const_in, 32)
            a_mix_act(act)
            norm(1, 1)
            moe_act(act, 0, START["moe0"])
            norm(2, 2)
            c_mix_act(act)
            norm(3, 3)
            act.dma_start(cat[:, 0, :], bass.AP(tensor=final_rows.tensor, offset=0, ap=[[0, P], [1, D]]))\
               .then_inc(final_in, 16)
            moe_act(act, 1, START["moe1"])
            norm_act(act, 4)
            norm(5, 4)
            ffn_act_engine(act, 0)
            act.wait_ge(*X_SOURCE[6])
            act.dma_start(onehot, buckets[0:32, :]).then_inc(bucket_in, 16)
            act.dma_start(off_mask, buckets[32:40, :]).then_inc(bucket_in, 16)
            norm(6, 5)
            s_mix_act(act)
            norm(7, 6)
            ffn_act_engine(act, 1)
            norm(8, 7)
            ffn_act_engine(act, 2)
            norm(9, 8)
            r_mix_act(act)
            r_gates_act(act)
            act.wait_ge(*X_SOURCE[10])
            act.dma_start(W[:, 0:D], bass.AP(tensor=final_rows.tensor, offset=D, ap=[[0, P], [1, D]]))\
               .then_inc(final_in, 16)
            norm(10, 9)
            ffn_act_engine(act, 3)
            norm_act(act, 11)

        @block.vector
        def _(v):
            nc.vector.memset(ones[:, :], 1.0).then_inc(scattered, 1)
            norm_dve(v, 0, 0)
            v.wait_ge(const_in, 32)
            a_mix_dve(v)
            norm_dve(v, 1, 1)
            moe_dve(v, 0, START["moe0"])
            norm_dve(v, 2, 2)
            c_mix_dve(v)
            norm_dve(v, 3, 3)
            moe_dve(v, 1, START["moe1"])
            final_norm(v, 4, 0)
            norm_dve(v, 5, 4)
            ffn_dve(v, 0)
            norm_dve(v, 6, 5)
            s_mix_dve(v)
            norm_dve(v, 7, 6)
            ffn_dve(v, 1)
            norm_dve(v, 8, 7)
            ffn_dve(v, 2)
            norm_dve(v, 9, 8)
            r_mix_dve(v)
            norm_dve(v, 10, 9)
            ffn_dve(v, 3)
            final_norm(v, 11, 1)

        @block.gpsimd
        def _(pool):
            pool.wait_ge(const_in, 32)
            for name in POWERS:
                src, dst, w = {"gmlp": (80, 104, 8), "latents": (80, 104, 4), "heads": (84, 108, 20), "ln": (80, 104, 4)}.get(name, (MS, RS, 2))
                power_pool(pool, name, src, dst, w)
                if name == "n1":
                    moe_pool(pool, 0)
                if name == "n3":
                    moe_pool(pool, 1)

        @block.tensor
        def _(pe):
            pe.wait_ge(const_in, 32)
            norm_pe(pe, 0)
            a_mix_pe(pe)
            norm_pe(pe, 1)
            moe_pe(pe, 0, START["moe0"])
            norm_pe(pe, 2)
            c_mix_pe(pe)
            norm_pe(pe, 3)
            moe_pe(pe, 1, START["moe1"])
            norm_pe(pe, 4)
            ffn_pe(pe, 0)
            norm_pe(pe, 5)
            s_mix_pe(pe)
            norm_pe(pe, 6)
            ffn_pe(pe, 1)
            norm_pe(pe, 7)
            ffn_pe(pe, 2)
            norm_pe(pe, 8)
            r_mix_pe(pe)
            norm_pe(pe, 9)
            ffn_pe(pe, 3)


def rope_table(pos, width, theta):
    half = width // 2
    inv = np.power(np.float32(theta), -np.arange(half, dtype=np.float32) * np.float32(2.0 / width)).astype(np.float32)
    ang = pos.astype(np.float32)[:, None] * inv[None, :]
    cos, sin = np.cos(ang).astype(np.float32), np.sin(ang).astype(np.float32)
    return np.concatenate([cos, cos], 1), np.concatenate([-sin, sin], 1)


def constant_columns():
    pos = np.arange(T)

    def tiles(a):
        return a.reshape(NT, P, -1).transpose(1, 0, 2).reshape(P, -1)

    def table(pairs):
        cos, sin = (np.concatenate([pair[i] for pair in pairs], 1) for i in range(2))
        return np.concatenate([tiles(cos), tiles(sin)], 1)

    gap = pos[:, None] - pos[None, :]
    count = sum(((gap % d == 0) & (np.abs(gap) // d <= w // (2 * d))).astype(np.int64)
                for w, d in ((128, 1), (512, 4), (2048, 16)))
    band = np.where(count > 0, np.log(np.maximum(count, 1)), OFF).astype(np.float32)
    parts = {
        "ident": np.eye(P), "flip": np.eye(P)[::-1], "band": tiles(band),
        "ropeA": table([rope_table(pos, 16, 500000.0)]), "ropeC": table([rope_table(pos, 32, 500000.0)]),
        "ropeD": table([rope_table(pos // 64, 32, 10000.0), rope_table(pos % 64, 32, 10000.0)]),
        "iota": np.tile(np.arange(CAP), (P, 1)), "half": np.full((P, 32), -0.5),
    }
    return np.concatenate([parts[name].reshape(P, n) for name, n in CONSTS], 1).astype(np.float32)


def bucket_rows():
    dist = 255 - np.arange(SPAN)
    n = np.maximum(dist, 0)
    nf = np.maximum(n, 16).astype(np.float32)
    large = 16 + (np.log(nf / np.float32(16)) / np.float32(np.log(8.0)) * np.float32(16)).astype(np.int32)
    bucket = np.where(n < 16, n, np.minimum(large, 31))
    onehot = (bucket[None, :] == np.arange(32)[:, None]).astype(np.float32)
    window = np.where((dist >= 0) & (dist < 128), 0.0, OFF).astype(np.float32)
    return np.concatenate([onehot, np.tile(window, (8, 1))], 0)


def by_tile(v):
    return v.reshape(-1, P).T


def rows(v):
    return np.broadcast_to(v.reshape(1, -1), (P, v.size))


def param_columns(i):
    gains = [i["norm_mix"][0], i["norm_ffn"][0], i["norm_mix"][1], i["norm_ffn"][1], i["norm_ffn1_2"][0],
             i["norm_mix_2"][0], i["norm_ffn2_2"][0], i["norm_ffn1_2"][1], i["norm_mix_2"][1], i["norm_ffn2_2"][1]]
    relb = np.zeros((P, 8), np.float32)
    relb[0:32] = i["rel_bias_2"]
    parts = {
        "gains": np.concatenate([by_tile(g) for g in gains], 1),
        "router": i["moe_w_router"].reshape(2, KD, P, E).transpose(2, 0, 1, 3),
        "gmlp": rows(i["even_gmlp_norm"][0]),
        "wsT": i["even_w_spatial"][0].transpose(2, 0, 1), "bs": i["even_b_spatial"][0].T,
        "cgain": np.concatenate([by_tile(i["odd_cq_norm"][0]), by_tile(i["odd_ckv_norm"][0])], 1),
        "dgain": np.concatenate([rows(i["odd_dq_norm"][0])] * 8 + [rows(i["odd_dk_norm"][0])] * 2, 1),
        "sinks": rows(i["attn_sinks_2"][0]), "relb": relb,
        "convw": i["conv_b_w_2"][0].reshape(KW, 4, P).transpose(2, 1, 0), "convb": by_tile(i["conv_b_b_2"][0]),
        "lng": rows(i["conv_ln_g_2"][0]), "lnb": rows(i["conv_ln_b_2"][0]),
        "rconvw": i["lru_conv_w_2"][0].reshape(LW, KD, P).transpose(2, 1, 0), "rconvb": by_tile(i["lru_conv_b_2"][0]),
        "gab": by_tile(i["gate_a_b_2"][0]), "gxb": by_tile(i["gate_x_b_2"][0]), "lam": by_tile(i["lru_lambda_2"][0]),
    }
    return np.ascontiguousarray(np.concatenate([parts[name].reshape(P, n) for name, n in PARAMS], 1))


def weight_stream(i):
    s = np.zeros((N_SLOTS, P, SLOT), np.float32)

    def put(n, pieces):
        w, at = s[n].reshape(P, KD, 512), 0
        for m in pieces:
            w[:, :, at:at + m.shape[1]] = m.reshape(KD, P, -1).transpose(1, 0, 2)
            at += m.shape[1]

    def wide(name, m):
        for c in range(0, m.shape[1], 512):
            put(START[name] + c // 512, [m[:, c:c + 512]])

    def experts(name, l):
        for e in range(E):
            n = START[name] + 3 * e
            for m, w in enumerate((i["moe_w_gate"][l, e], i["moe_w_up"][l, e])):
                for half in range(2):
                    s[n + half].reshape(P, 4, 2, 512)[:, :, m] = w[512 * half:512 * half + 512].reshape(4, P, 512)\
                        .transpose(1, 0, 2)
            s[n + 2].reshape(P, 4, D)[:] = i["moe_w_down"][l, e].reshape(4, P, D).transpose(1, 0, 2)

    def ffn(name, g, u, d):
        cut = lambda m, f: m[:, f * P:(f + 1) * P].reshape(KD, P, P).transpose(1, 0, 2).reshape(P, UNIT)
        units = []
        for f in range(FT):
            units += [cut(g, f), cut(u, f)] + ([d[(f - 1) * P:f * P]] if f else [])
        units.append(d[(FT - 1) * P:])
        for n, m in enumerate(units):
            s[START[name] + n // 4][:, (n % 4) * UNIT:(n % 4 + 1) * UNIT] = m

    wide("a_in", i["even_w_in"][0])
    wide("a_out", i["even_w_out"][0])
    experts("moe0", 0)
    w, n = i["odd_w_in"][0], START["c_in"]
    put(n, [w[:, 0:416]])
    put(n + 1, [w[:, 416:928]])
    put(n + 2, [w[:, 928:1184]])
    n = START["c_up"]
    s[n][:, 0:1536].reshape(P, 2, 768)[:] = i["odd_w_cq_up"][0].reshape(2, P, 768).transpose(1, 0, 2)
    s[n][:, 1536:2560] = i["odd_w_ckv_up"][0]
    wide("c_out", i["odd_w_out"][0])
    experts("moe1", 1)
    ffn("ffn0", i["ffn1_wg_2"][0], i["ffn1_wu_2"][0], i["ffn1_wd_2"][0])
    w, n = i["even_w_in_2"][0], START["s_in"]
    a, g = (lambda c: w[:, 768 + c * P:896 + c * P]), (lambda c: w[:, 1280 + c * P:1408 + c * P])
    put(n, [a(0), g(0), a(1), g(1)])
    put(n + 1, [a(2), g(2), a(3), g(3)])
    put(n + 2, [w[:, 0:512]])
    put(n + 3, [w[:, 512:768]])
    wide("s_out", i["even_w_out_2"][0])
    ffn("ffn1", i["ffn2_wg_2"][0], i["ffn2_wu_2"][0], i["ffn2_wd_2"][0])
    ffn("ffn2", i["ffn1_wg_2"][1], i["ffn1_wu_2"][1], i["ffn1_wd_2"][1])
    wide("r_in", np.roll(i["odd_w_in_2"][0], D, 1))
    n = START["r_gate"]
    s[n][:, 0:1024].reshape(P, KD, P)[:] = i["gate_a_w_2"][0].transpose(1, 0, 2)
    s[n][:, 1024:2048].reshape(P, KD, P)[:] = i["gate_x_w_2"][0].transpose(1, 0, 2)
    wide("r_out", i["odd_w_out_2"][0])
    ffn("ffn3", i["ffn2_wg_2"][1], i["ffn2_wu_2"][1], i["ffn2_wd_2"][1])
    return s


def kernel(**inputs):
    import concourse.bacc as bacc
    from concourse.bass_utils import run_bass_kernel_spmd as run

    i = {name: np.asarray(a) for name, a in inputs.items()}
    arrays = {
        "stream": weight_stream(i), "params": param_columns(i), "consts": constant_columns(),
        "buckets": bucket_rows(), "final_rows": np.stack([i["final_norm"], i["norm_final_2"]]),
        "x_in": np.ascontiguousarray(i["x"][0]),
    }
    nc = bacc.Bacc("TRN2", target_bir_lowering=False, num_devices=1)
    args = {name: nc.dram_tensor(name, a.shape, mybir.dt.from_np(a.dtype), kind="ExternalInput").ap()
            for name, a in arrays.items()}
    out = nc.dram_tensor("out", (T, D), F32, kind="ExternalOutput").ap()
    build(nc, args["stream"], args["params"], args["consts"], args["buckets"], args["final_rows"], args["x_in"], out)
    r = run(nc, [arrays], core_ids=[0]).results[0]
    return r["out"].reshape(1, T, D)
```
